# Optimizing a Trainium2 kernel written in Bass

```python
import math
import jax, jax.numpy as jnp
from jax import lax
import numpy as np

D_MODEL = 1024
BATCH = 1
SEQ = 512
DEPTH = 1

CHUNK = 64
Q_BLOCK = 128
MEM_LEN = 256
MIX_WIDTH = D_MODEL
FOX_WIDTH = MIX_WIDTH // 2
FOX_HEAD_DIM = 64
FOX_HEADS = FOX_WIDTH // FOX_HEAD_DIM
GLA_WIDTH = MIX_WIDTH - FOX_WIDTH
GLA_HEADS = 4
GLA_VALUE_DIM = GLA_WIDTH // GLA_HEADS
GLA_KEY_DIM = GLA_VALUE_DIM // 2
GLA_KEY_WIDTH = GLA_HEADS * GLA_KEY_DIM
GLA_GATE_RANK = 16
GLA_TAU = 16.0
XATTN_HEADS = 4
XATTN_HEAD_DIM = D_MODEL // XATTN_HEADS
D_FF = 4 * D_MODEL
EPS = 1e-6
IN_SIZES = (FOX_WIDTH, FOX_WIDTH, FOX_WIDTH, FOX_HEADS,
            GLA_KEY_WIDTH, GLA_KEY_WIDTH, GLA_WIDTH, GLA_GATE_RANK, GLA_WIDTH)
IN_WIDTH = sum(IN_SIZES)


def _split_points():
    return [int(v) for v in np.cumsum(np.array(IN_SIZES))[:-1]]

def rms_norm(x, g):
    xf = x.astype(jnp.float32)
    y = xf * lax.rsqrt(jnp.mean(xf * xf, axis=-1, keepdims=True) + EPS)
    return (y * g.astype(jnp.float32)).astype(x.dtype)

def fox_attention(q, k, v, log_f):
    B, S, H, D = q.shape
    scale = 1.0 / math.sqrt(D)
    c = jnp.transpose(jnp.cumsum(log_f, axis=1), (0, 2, 1))
    outs = []
    for i in range(S // Q_BLOCK):
        start, end = i * Q_BLOCK, (i + 1) * Q_BLOCK
        qb = q[:, start:end]
        kb = k[:, :end]
        vb = v[:, :end]
        s = jnp.einsum('bqhd,bkhd->bhqk', qb, kb).astype(jnp.float32) * scale
        bias = c[:, :, start:end, None] - c[:, :, None, :end]
        q_pos = start + jnp.arange(Q_BLOCK)
        k_pos = jnp.arange(end)
        mask = k_pos[None, :] <= q_pos[:, None]
        s = jnp.where(mask, s + bias, -jnp.inf)
        p = jax.nn.softmax(s, axis=-1)
        outs.append(jnp.einsum('bhqk,bkhd->bqhd', p.astype(vb.dtype), vb))
    return jnp.concatenate(outs, axis=1)

def gla_chunked(q, k, v, g_log):
    B, S, H, Dk = q.shape
    Dv = v.shape[-1]
    N = S // CHUNK

    def to_chunks(a):
        return jnp.transpose(a.astype(jnp.float32).reshape(B, N, CHUNK, H, a.shape[-1]), (0, 3, 1, 2, 4))

    qc = to_chunks(q) * (Dk ** -0.5)
    kc = to_chunks(k)
    vc = to_chunks(v)
    bc = jnp.cumsum(to_chunks(g_log), axis=3)
    q_dec = qc * jnp.exp(bc)
    k_dec = kc * jnp.exp(-bc)
    A = jnp.einsum('bhnck,bhnsk->bhncs', q_dec, k_dec)
    tril = jnp.tril(jnp.ones((CHUNK, CHUNK), dtype=bool))
    A = jnp.where(tril, A, 0.0)
    o_intra = jnp.einsum('bhncs,bhnsv->bhncv', A, vc)
    b_last = bc[:, :, :, -1:, :]
    dS = jnp.einsum('bhnck,bhncv->bhnkv', kc * jnp.exp(b_last - bc), vc)
    decay = jnp.exp(b_last[:, :, :, 0, :])

    def step(state, inp):
        d, ds = inp
        return d[..., None] * state + ds, state

    init = jnp.zeros((B, H, Dk, Dv), jnp.float32)
    _, s_prev = lax.scan(step, init, (jnp.moveaxis(decay, 2, 0), jnp.moveaxis(dS, 2, 0)))
    s_prev = jnp.moveaxis(s_prev, 0, 2)
    o_inter = jnp.einsum('bhnck,bhnkv->bhncv', q_dec, s_prev)
    o = o_intra + o_inter
    o = jnp.transpose(o, (0, 2, 3, 1, 4)).reshape(B, S, H, Dv)
    return o.astype(v.dtype)

def parallel_mixer(xn, w_in, fox_b_f, fox_q_norm_g, fox_k_norm_g,
                   gla_w_gate2, gla_b_gate, gla_out_norm_g, w_out):
    B, S, _ = xn.shape
    proj = xn @ w_in
    fq, fk, fv, ff, gq, gk, gv, glr, gr = jnp.split(proj, _split_points(), axis=-1)
    fq = rms_norm(fq.reshape(B, S, FOX_HEADS, FOX_HEAD_DIM), fox_q_norm_g)
    fk = rms_norm(fk.reshape(B, S, FOX_HEADS, FOX_HEAD_DIM), fox_k_norm_g)
    fv = fv.reshape(B, S, FOX_HEADS, FOX_HEAD_DIM)
    log_f = jax.nn.log_sigmoid((ff + fox_b_f).astype(jnp.float32))
    fox_out = fox_attention(fq, fk, fv, log_f).reshape(B, S, FOX_WIDTH)
    g_log = jax.nn.log_sigmoid((glr @ gla_w_gate2 + gla_b_gate).astype(jnp.float32)) / GLA_TAU
    g_log = g_log.reshape(B, S, GLA_HEADS, GLA_KEY_DIM)
    gla_o = gla_chunked(gq.reshape(B, S, GLA_HEADS, GLA_KEY_DIM),
                        gk.reshape(B, S, GLA_HEADS, GLA_KEY_DIM),
                        gv.reshape(B, S, GLA_HEADS, GLA_VALUE_DIM), g_log)
    gla_o = rms_norm(gla_o, gla_out_norm_g.reshape(GLA_HEADS, GLA_VALUE_DIM)).reshape(B, S, GLA_WIDTH)
    gla_out = gla_o * jax.nn.silu(gr)
    return jnp.concatenate([fox_out, gla_out], axis=-1) @ w_out

def memory_cross_attention(hn, memn, wq, wkv, q_norm_g, k_norm_g, wo):
    B, S, _ = hn.shape
    M = memn.shape[1]
    q = rms_norm((hn @ wq).reshape(B, S, XATTN_HEADS, XATTN_HEAD_DIM), q_norm_g)
    k, v = jnp.split(memn @ wkv, 2, axis=-1)
    k = rms_norm(k.reshape(B, M, XATTN_HEADS, XATTN_HEAD_DIM), k_norm_g)
    v = v.reshape(B, M, XATTN_HEADS, XATTN_HEAD_DIM)
    s = jnp.einsum('bshd,bmhd->bhsm', q, k).astype(jnp.float32) / math.sqrt(XATTN_HEAD_DIM)
    p = jax.nn.softmax(s, axis=-1)
    o = jnp.einsum('bhsm,bmhd->bshd', p.astype(v.dtype), v).reshape(B, S, D_MODEL)
    return o @ wo

def first_inputs(seed: int = 0) -> dict:
    key = jax.random.key(seed)
    ks = jax.random.split(key, 24)
    f32 = jnp.float32

    def nrm(k, shape, scale):
        return jax.random.normal(k, shape, f32) * scale

    def gain(k, shape):
        return jnp.ones(shape, f32) + 0.02 * jax.random.normal(k, shape, f32)

    return {
        "x": nrm(ks[0], (BATCH, SEQ, D_MODEL), 1.0),
        "mem": nrm(ks[1], (BATCH, MEM_LEN, D_MODEL), 1.0),
        "norm_mix_g": gain(ks[2], (D_MODEL,)),
        "w_in": nrm(ks[3], (D_MODEL, IN_WIDTH), D_MODEL ** -0.5),
        "fox_b_f": 2.0 + 0.1 * jax.random.normal(ks[4], (FOX_HEADS,), f32),
        "fox_q_norm_g": gain(ks[5], (FOX_HEAD_DIM,)),
        "fox_k_norm_g": gain(ks[6], (FOX_HEAD_DIM,)),
        "gla_w_gate2": nrm(ks[7], (GLA_GATE_RANK, GLA_KEY_WIDTH), GLA_GATE_RANK ** -0.5),
        "gla_b_gate": nrm(ks[8], (GLA_KEY_WIDTH,), 0.02),
        "gla_out_norm_g": gain(ks[9], (GLA_WIDTH,)),
        "w_out": nrm(ks[10], (MIX_WIDTH, D_MODEL), MIX_WIDTH ** -0.5),
        "norm_xattn_g": gain(ks[11], (D_MODEL,)),
        "norm_mem_g": gain(ks[12], (D_MODEL,)),
        "xattn_wq": nrm(ks[13], (D_MODEL, D_MODEL), D_MODEL ** -0.5),
        "xattn_wkv": nrm(ks[14], (D_MODEL, 2 * D_MODEL), D_MODEL ** -0.5),
        "xattn_q_norm_g": gain(ks[15], (XATTN_HEAD_DIM,)),
        "xattn_k_norm_g": gain(ks[16], (XATTN_HEAD_DIM,)),
        "xattn_wo": nrm(ks[17], (D_MODEL, D_MODEL), D_MODEL ** -0.5),
        "norm_mlp_g": gain(ks[18], (D_MODEL,)),
        "mlp_w1": nrm(ks[19], (D_MODEL, D_FF), D_MODEL ** -0.5),
        "mlp_w2": nrm(ks[20], (D_FF, D_MODEL), D_FF ** -0.5),
    }

def first_block(x, mem, norm_mix_g, w_in, fox_b_f, fox_q_norm_g, fox_k_norm_g,
              gla_w_gate2, gla_b_gate, gla_out_norm_g, w_out,
              norm_xattn_g, norm_mem_g, xattn_wq, xattn_wkv, xattn_q_norm_g,
              xattn_k_norm_g, xattn_wo, norm_mlp_g, mlp_w1, mlp_w2):
    h = x
    for _ in range(DEPTH):
        h = h + parallel_mixer(rms_norm(h, norm_mix_g), w_in, fox_b_f, fox_q_norm_g,
                               fox_k_norm_g, gla_w_gate2, gla_b_gate, gla_out_norm_g, w_out)
        h = h + memory_cross_attention(rms_norm(h, norm_xattn_g), rms_norm(mem, norm_mem_g),
                                       xattn_wq, xattn_wkv, xattn_q_norm_g, xattn_k_norm_g, xattn_wo)
        u = jax.nn.relu(rms_norm(h, norm_mlp_g) @ mlp_w1)
        h = h + (u * u) @ mlp_w2
    return h


HEAD_DIM = 64
DA_HEADS = 8
DA_V_DIM = 2 * HEAD_DIM
NSA_HEADS = 16
NSA_GROUPS = 2
NSA_HPG = NSA_HEADS // NSA_GROUPS
CMP_BLOCK = 32
CMP_STRIDE = 16
CMP_HIDDEN = 256
SLC_BLOCK = 64
SLC_TOPN = 16
WIN = 512
SLC_Q_BLOCK = 64
D_FF_2 = 2816
ROPE_THETA = 10000.0
NEG_INF = -1e30
FORCE_SCORE = 1e9

DA_QK_W = DA_HEADS * 2 * HEAD_DIM
DA_V_W = DA_HEADS * DA_V_DIM
NSA_Q_W = NSA_HEADS * HEAD_DIM
NSA_KV_W = NSA_GROUPS * HEAD_DIM
NSA_GATE_W = 3 * NSA_HEADS
IN_WIDTHS = (DA_QK_W, DA_QK_W, DA_V_W, NSA_Q_W) + (NSA_KV_W,) * 6 + (NSA_GATE_W, D_MODEL, D_MODEL)
D_IN = sum(IN_WIDTHS)


def rmsnorm(x, g):
    xf = x.astype(jnp.float32)
    y = xf * lax.rsqrt(jnp.mean(xf * xf, axis=-1, keepdims=True) + EPS)
    return (y * g.astype(jnp.float32)).astype(x.dtype)

def swiglu(h, w1, w3, w2):
    return (jax.nn.silu(h @ w1) * (h @ w3)) @ w2

def rope_tables(T, dim):
    pos = jnp.arange(T, dtype=jnp.float32)
    inv = 1.0 / (ROPE_THETA ** (jnp.arange(0, dim, 2, dtype=jnp.float32) / dim))
    ang = pos[:, None] * inv[None, :]
    return jnp.cos(ang), jnp.sin(ang)

def apply_rope(x, cos, sin):
    half = x.shape[-1] // 2
    shape = (1, x.shape[1]) + (1,) * (x.ndim - 3) + (half,)
    c = cos.reshape(shape).astype(x.dtype)
    s = sin.reshape(shape).astype(x.dtype)
    x1, x2 = x[..., :half], x[..., half:]
    return jnp.concatenate([x1 * c - x2 * s, x2 * c + x1 * s], axis=-1)

def _sweep(block_fn, n_blocks):
    out = lax.map(block_fn, jnp.arange(n_blocks))
    out = jnp.moveaxis(out, 0, 1)
    return out.reshape((out.shape[0], n_blocks * out.shape[2]) + out.shape[3:])

def diff_attention(q, k, v, cos, sin, lam_params, head_gain, lam_init):
    B, T = q.shape[0], q.shape[1]
    q = apply_rope(q, cos, sin)
    k = apply_rope(k, cos, sin)
    lp = lam_params.astype(jnp.float32)
    lam = jnp.exp(jnp.sum(lp[0] * lp[1])) - jnp.exp(jnp.sum(lp[2] * lp[3])) + lam_init
    kpos = jnp.arange(T)
    scale = HEAD_DIM ** -0.5

    def block(i):
        qb = lax.dynamic_slice_in_dim(q, i * Q_BLOCK, Q_BLOCK, axis=1)
        qpos = i * Q_BLOCK + jnp.arange(Q_BLOCK)
        s = jnp.einsum('bqhcd,bkhcd->bhcqk', qb, k).astype(jnp.float32) * scale
        s = jnp.where(kpos[None, :] <= qpos[:, None], s, NEG_INF)
        p = jax.nn.softmax(s, axis=-1)
        a = p[:, :, 0] - lam * p[:, :, 1]
        return jnp.einsum('bhqk,bkhe->bqhe', a.astype(v.dtype), v)

    o = _sweep(block, T // Q_BLOCK)
    o = rmsnorm(o, head_gain) * (1.0 - lam_init)
    return o.reshape(B, T, DA_V_W)

def compress(x_raw, pos, w1, w2):
    B, T = x_raw.shape[0], x_raw.shape[1]
    n_cmp = (T - CMP_BLOCK) // CMP_STRIDE + 1
    idx = np.arange(n_cmp)[:, None] * CMP_STRIDE + np.arange(CMP_BLOCK)[None, :]
    blocks = x_raw[:, idx] + pos[:, None, :]
    blocks = jnp.swapaxes(blocks, 2, 3).reshape(B, n_cmp, NSA_GROUPS, CMP_BLOCK * HEAD_DIM)
    return jax.nn.gelu(blocks @ w1) @ w2

def _overlap_matrix(n_cmp, n_slc):
    start = np.arange(n_cmp) * CMP_STRIDE
    sb = np.arange(n_slc) * SLC_BLOCK
    ov = (start[:, None] < sb[None, :] + SLC_BLOCK) & (start[:, None] + CMP_BLOCK > sb[None, :])
    return ov.astype(np.float32)

def nsa(q, k_cmp, v_cmp, k_slc, v_slc, k_win, v_win, gate_logits, cos, sin, cmp_pos, cmp_w1, cmp_w2):
    B, T = q.shape[0], q.shape[1]
    dt = q.dtype
    scale = HEAD_DIM ** -0.5
    t = jnp.arange(T)

    kc = compress(k_cmp, cmp_pos[0], cmp_w1[0], cmp_w2[0])
    vc = compress(v_cmp, cmp_pos[1], cmp_w1[1], cmp_w2[1])
    n_cmp = kc.shape[1]
    s = jnp.einsum('btgjd,bngd->btgjn', q, kc).astype(jnp.float32) * scale
    c_valid = ((jnp.arange(n_cmp) * CMP_STRIDE + CMP_BLOCK - 1)[None, :] <= t[:, None])[None, :, None, None, :]
    p_cmp = jnp.where(c_valid, jax.nn.softmax(jnp.where(c_valid, s, NEG_INF), axis=-1), 0.0)
    o_cmp = jnp.einsum('btgjn,bngd->btgjd', p_cmp.astype(dt), vc)

    n_slc = T // SLC_BLOCK
    overlap = jnp.asarray(_overlap_matrix(n_cmp, n_slc))
    imp = jnp.einsum('btgjn,ns->btgs', p_cmp, overlap)
    blk_t = t // SLC_BLOCK
    sblk = jnp.arange(n_slc)
    causal = sblk[None, :] <= blk_t[:, None]
    forced = (sblk[None, :] == 0) | (sblk[None, :] == blk_t[:, None]) | (sblk[None, :] == blk_t[:, None] - 1)
    score = jnp.where(forced[None, :, None, :], FORCE_SCORE,
                      jnp.where(causal[None, :, None, :], imp, -1.0))
    _, sel = lax.top_k(score, min(SLC_TOPN, n_slc))
    sel_valid = sel <= blk_t[None, :, None, None]

    qr = apply_rope(q, cos, sin)
    ks = apply_rope(k_slc, cos, sin)
    kw = apply_rope(k_win, cos, sin)

    ks_blk = ks.reshape(B, n_slc, SLC_BLOCK, NSA_GROUPS, HEAD_DIM).transpose(0, 3, 1, 2, 4)
    vs_blk = v_slc.reshape(B, n_slc, SLC_BLOCK, NSA_GROUPS, HEAD_DIM).transpose(0, 3, 1, 2, 4)
    bidx = jnp.arange(B)[:, None, None, None]
    gidx = jnp.arange(NSA_GROUPS)[None, None, :, None]

    def slc_block(i):
        qb = lax.dynamic_slice_in_dim(qr, i * SLC_Q_BLOCK, SLC_Q_BLOCK, axis=1)
        selb = lax.dynamic_slice_in_dim(sel, i * SLC_Q_BLOCK, SLC_Q_BLOCK, axis=1)
        validb = lax.dynamic_slice_in_dim(sel_valid, i * SLC_Q_BLOCK, SLC_Q_BLOCK, axis=1)
        qpos = i * SLC_Q_BLOCK + jnp.arange(SLC_Q_BLOCK)
        kg = ks_blk[bidx, gidx, selb]
        vg = vs_blk[bidx, gidx, selb]
        kpos = selb[..., None] * SLC_BLOCK + jnp.arange(SLC_BLOCK)
        mask = validb[..., None] & (kpos <= qpos[None, :, None, None, None])
        s = jnp.einsum('bqgjd,bqgnld->bqgjnl', qb, kg).astype(jnp.float32) * scale
        s = jnp.where(mask[:, :, :, None], s, NEG_INF)
        sh = s.shape
        p = jax.nn.softmax(s.reshape(sh[:4] + (-1,)), axis=-1).reshape(sh)
        return jnp.einsum('bqgjnl,bqgnld->bqgjd', p.astype(dt), vg)

    o_slc = _sweep(slc_block, T // SLC_Q_BLOCK)

    kw_pad = jnp.pad(kw, ((0, 0), (WIN, 0), (0, 0), (0, 0)))
    vw_pad = jnp.pad(v_win, ((0, 0), (WIN, 0), (0, 0), (0, 0)))

    def win_block(i):
        qb = lax.dynamic_slice_in_dim(qr, i * Q_BLOCK, Q_BLOCK, axis=1)
        qpos = i * Q_BLOCK + jnp.arange(Q_BLOCK)
        kb = lax.dynamic_slice_in_dim(kw_pad, i * Q_BLOCK, WIN + Q_BLOCK, axis=1)
        vb = lax.dynamic_slice_in_dim(vw_pad, i * Q_BLOCK, WIN + Q_BLOCK, axis=1)
        kpos = i * Q_BLOCK - WIN + jnp.arange(WIN + Q_BLOCK)
        mask = (kpos[None, :] >= 0) & (kpos[None, :] <= qpos[:, None]) & (kpos[None, :] > qpos[:, None] - WIN)
        s = jnp.einsum('bqgjd,bkgd->bqgjk', qb, kb).astype(jnp.float32) * scale
        s = jnp.where(mask[None, :, None, None, :], s, NEG_INF)
        p = jax.nn.softmax(s, axis=-1)
        return jnp.einsum('bqgjk,bkgd->bqgjd', p.astype(dt), vb)

    o_win = _sweep(win_block, T // Q_BLOCK)

    g = jax.nn.sigmoid(gate_logits.astype(jnp.float32)).astype(dt).reshape(B, T, NSA_GROUPS, NSA_HPG, 3)
    o = g[..., 0:1] * o_cmp + g[..., 1:2] * o_slc + g[..., 2:3] * o_win
    return o.reshape(B, T, NSA_Q_W)

def token_mix(h, w_in, da_lambda, da_head_norm, cmp_pos, cmp_w1, cmp_w2, w_proj_da, w_proj_nsa, w_out, lam_init):
    B, T = h.shape[0], h.shape[1]
    proj = h @ w_in
    offs = []
    acc = 0
    for w in IN_WIDTHS[:-1]:
        acc += w
        offs.append(acc)
    (q_da, k_da, v_da, q_ns, kc_raw, vc_raw, ks_raw, vs_raw, kw_raw, vw_raw,
     g_ns, g_a, g_b) = jnp.split(proj, offs, axis=-1)
    cos, sin = rope_tables(T, HEAD_DIM)
    y_da = diff_attention(q_da.reshape(B, T, DA_HEADS, 2, HEAD_DIM),
                          k_da.reshape(B, T, DA_HEADS, 2, HEAD_DIM),
                          v_da.reshape(B, T, DA_HEADS, DA_V_DIM),
                          cos, sin, da_lambda, da_head_norm, lam_init)
    kv = lambda a: a.reshape(B, T, NSA_GROUPS, HEAD_DIM)
    y_ns = nsa(q_ns.reshape(B, T, NSA_GROUPS, NSA_HPG, HEAD_DIM),
               kv(kc_raw), kv(vc_raw), kv(ks_raw), kv(vs_raw), kv(kw_raw), kv(vw_raw),
               g_ns, cos, sin, cmp_pos, cmp_w1, cmp_w2)
    merged = jax.nn.sigmoid(g_a) * (y_da @ w_proj_da) + jax.nn.sigmoid(g_b) * (y_ns @ w_proj_nsa)
    return merged @ w_out

def second_inputs(seed: int = 0) -> dict:
    key = jax.random.key(seed)
    ks = jax.random.split(key, 24)
    f32 = jnp.float32

    def w(k, shape, fan_in):
        return jax.random.normal(k, shape, f32) * fan_in ** -0.5

    def gain(k, shape):
        return 1.0 + 0.05 * jax.random.normal(k, shape, f32)

    return {
        'x': jax.random.normal(ks[0], (BATCH, SEQ, D_MODEL), f32),
        'ffn1_norm': gain(ks[1], (DEPTH, D_MODEL)),
        'ffn1_w1': w(ks[2], (DEPTH, D_MODEL, D_FF_2), D_MODEL),
        'ffn1_w3': w(ks[3], (DEPTH, D_MODEL, D_FF_2), D_MODEL),
        'ffn1_w2': w(ks[4], (DEPTH, D_FF_2, D_MODEL), D_FF_2),
        'mix_norm': gain(ks[5], (DEPTH, D_MODEL)),
        'w_in': w(ks[6], (DEPTH, D_MODEL, D_IN), D_MODEL),
        'da_lambda': 0.1 * jax.random.normal(ks[7], (DEPTH, 4, HEAD_DIM), f32),
        'da_head_norm': gain(ks[8], (DEPTH, DA_HEADS, DA_V_DIM)),
        'cmp_pos': 0.1 * jax.random.normal(ks[9], (DEPTH, 2, CMP_BLOCK, HEAD_DIM), f32),
        'cmp_w1': w(ks[10], (DEPTH, 2, CMP_BLOCK * HEAD_DIM, CMP_HIDDEN), CMP_BLOCK * HEAD_DIM),
        'cmp_w2': w(ks[11], (DEPTH, 2, CMP_HIDDEN, HEAD_DIM), CMP_HIDDEN),
        'w_proj_da': w(ks[12], (DEPTH, DA_V_W, D_MODEL), DA_V_W),
        'w_proj_nsa': w(ks[13], (DEPTH, NSA_Q_W, D_MODEL), NSA_Q_W),
        'w_out': w(ks[14], (DEPTH, D_MODEL, D_MODEL), D_MODEL),
        'ffn2_norm': gain(ks[15], (DEPTH, D_MODEL)),
        'ffn2_w1': w(ks[16], (DEPTH, D_MODEL, D_FF_2), D_MODEL),
        'ffn2_w3': w(ks[17], (DEPTH, D_MODEL, D_FF_2), D_MODEL),
        'ffn2_w2': w(ks[18], (DEPTH, D_FF_2, D_MODEL), D_FF_2),
        'final_norm': gain(ks[19], (D_MODEL,)),
    }

def second_block(x, ffn1_norm, ffn1_w1, ffn1_w3, ffn1_w2, mix_norm, w_in, da_lambda, da_head_norm,
              cmp_pos, cmp_w1, cmp_w2, w_proj_da, w_proj_nsa, w_out,
              ffn2_norm, ffn2_w1, ffn2_w3, ffn2_w2, final_norm):
    for l in range(DEPTH):
        lam_init = 0.8 - 0.6 * math.exp(-0.3 * l)
        h = rmsnorm(x, ffn1_norm[l])
        x = x + 0.5 * swiglu(h, ffn1_w1[l], ffn1_w3[l], ffn1_w2[l])
        h = rmsnorm(x, mix_norm[l])
        x = x + token_mix(h, w_in[l], da_lambda[l], da_head_norm[l], cmp_pos[l], cmp_w1[l], cmp_w2[l],
                          w_proj_da[l], w_proj_nsa[l], w_out[l], lam_init)
        h = rmsnorm(x, ffn2_norm[l])
        x = x + 0.5 * swiglu(h, ffn2_w1[l], ffn2_w3[l], ffn2_w2[l])
    return rmsnorm(x, final_norm)


def setup_inputs(seed=0):
    out = dict(first_inputs(seed))
    for name, value in second_inputs(seed + 1).items():
        if name != "x":
            out[name + "_2"] = value
    return out


def reference(
    x, mem, norm_mix_g, w_in, fox_b_f, fox_q_norm_g, fox_k_norm_g, gla_w_gate2, gla_b_gate,
    gla_out_norm_g, w_out, norm_xattn_g, norm_mem_g, xattn_wq, xattn_wkv, xattn_q_norm_g,
    xattn_k_norm_g, xattn_wo, norm_mlp_g, mlp_w1, mlp_w2, ffn1_norm_2, ffn1_w1_2, ffn1_w3_2,
    ffn1_w2_2, mix_norm_2, w_in_2, da_lambda_2, da_head_norm_2, cmp_pos_2, cmp_w1_2, cmp_w2_2,
    w_proj_da_2, w_proj_nsa_2, w_out_2, ffn2_norm_2, ffn2_w1_2, ffn2_w3_2, ffn2_w2_2,
    final_norm_2,
):
    x = first_block(
        x, mem, norm_mix_g, w_in, fox_b_f, fox_q_norm_g, fox_k_norm_g, gla_w_gate2, gla_b_gate,
        gla_out_norm_g, w_out, norm_xattn_g, norm_mem_g, xattn_wq, xattn_wkv, xattn_q_norm_g,
        xattn_k_norm_g, xattn_wo, norm_mlp_g, mlp_w1, mlp_w2,
    )
    return second_block(
        x, ffn1_norm_2, ffn1_w1_2, ffn1_w3_2, ffn1_w2_2, mix_norm_2, w_in_2, da_lambda_2,
        da_head_norm_2, cmp_pos_2, cmp_w1_2, cmp_w2_2, w_proj_da_2, w_proj_nsa_2, w_out_2,
        ffn2_norm_2, ffn2_w1_2, ffn2_w3_2, ffn2_w2_2, final_norm_2,
    )


_drawn_inputs = setup_inputs


def setup_inputs(seed=0):
    import zlib

    import numpy as np

    out = dict(_drawn_inputs(seed))
    spreads = {}
    factors = {'norm_mix_g': 2.891,
     'fox_b_f': 3.05,
     'fox_q_norm_g': 8.0,
     'fox_k_norm_g': 8.0,
     'gla_b_gate': 8.0,
     'gla_out_norm_g': 6.88,
     'norm_xattn_g': 8.0,
     'norm_mem_g': 8.0,
     'xattn_q_norm_g': 8.0,
     'xattn_k_norm_g': 8.0,
     'norm_mlp_g': 3.374,
     'ffn1_norm_2': 4.391,
     'mix_norm_2': 3.837,
     'da_head_norm_2': 35.056,
     'cmp_pos_2': 24.956,
     'ffn2_norm_2': 13.514}
    for name, (base, spread) in spreads.items():
        noise = np.random.default_rng([zlib.crc32(name.encode()), seed]).standard_normal(out[name].shape)
        drawn = base * np.exp(spread * noise) if base else spread * noise
        out[name] = __import__('jax').numpy.asarray(drawn.astype(out[name].dtype))
    for name, factor in factors.items():
        out[name] = (out[name] * factor).astype(out[name].dtype)
    return out
```

```python
from contextlib import ExitStack
import numpy as np
import concourse.bass as bass
from concourse import mybir

ALU = mybir.AluOpType
ACT = mybir.ActivationFunctionType
F32 = mybir.dt.float32
F32R = mybir.dt.float32r

PART = 128
T, M, D = 512, 256, 1024
KT = D // PART
PC = 256
QT = T // PART
HALF = 64
D_FF, D_FF2 = 4096, 2816
CMP_L, CMP_S = 32, 16
NCMP = (T - CMP_L) // CMP_S + 1
EPS = 1e-6
NEG = -1e30
BIG = 3e38
LAM_INIT = 0.8 - 0.6
FOX, GLA_KW, GLA_VW = 512, 256, 512

W1_COL, at = {}, 0
for name_, width_ in (("fq", 512), ("fk", 512), ("fv", 512), ("ff", 8), ("gqk", 512), ("gv", 512), ("glr", 16), ("gr", 512)):
    W1_COL[name_] = at
    at += width_
W2_COL, at = {}, 0
for name_, width_ in (("q", 1024), ("k", 1024), ("v", 1024), ("nq", 1024), ("kv", 768), ("gate", 48), ("ga", 1024), ("gb", 1024)):
    W2_COL[name_] = at
    at += width_

P0, at = {}, 0
for name_, count_ in (("fqk", 4), ("fv", 2), ("small", 1), ("gqk", 2), ("gv", 2), ("gr", 2), ("wout", 4),
                      ("xk", 4), ("xv", 4), ("xq", 4), ("xo", 4), ("mlp", 32), ("ffn1", 34),
                      ("da0", 6), ("da1", 6), ("mda", 8), ("kv", 4), ("cmp", 4), ("nq0", 2), ("nq1", 2),
                      ("mnsa", 8), ("wout2", 4), ("ffn2", 34)):
    P0[name_] = at
    at += count_
PANELS = at

ROWS, at = {}, 0
for name_, count_ in (("norm_mix_g", 8), ("norm_xattn_g", 8), ("norm_mem_g", 8), ("norm_mlp_g", 8),
                      ("ffn1_norm_2", 8), ("mix_norm_2", 8), ("ffn2_norm_2", 8), ("final_norm_2", 8),
                      ("gla_out_norm_g", 4), ("da_head_norm_2", 8), ("gla_b_gate", 2), ("xattn_q_norm_g", 2),
                      ("xattn_k_norm_g", 2), ("fox_q_norm_g", 1), ("fox_k_norm_g", 1), ("cmp_pos_2", 32)):
    ROWS[name_] = at
    at += count_
NROWS = at

UINIT = 8
U0 = {"fox": UINIT}
U0["xa"] = U0["fox"] + 4 * 8
U0["da0"] = U0["xa"] + 4 * 4
U0["da1"] = U0["da0"] + 4 * 8
U0["ns0"] = U0["da1"] + 4 * 8
U0["ns1"] = U0["ns0"] + 4 * 24
U0["end"] = U0["ns1"] + 4 * 24
FINIT = 4
F0 = {"fox": FINIT, "gla": FINIT + 4, "xa": FINIT + 8, "da0": FINIT + 16, "da1": FINIT + 20, "ns0": FINIT + 24, "ns1": FINIT + 28, "end": FINIT + 32}
A0 = {"fox": 0, "xa": 4, "da0": 8, "da1": 12, "ns0": 16, "ns1": 20}
R0 = {"da0": 0, "da1": 8, "kv": 16, "ns0": 18, "ns1": 22}
RA0 = {"da0": 0, "da1": 4, "kv": 8, "ns0": 9, "ns1": 13}
CF0 = {"da0": 0, "da1": 16, "ns0": 32, "ns1": 32 + 96}
MLP0 = {"mlp": 2, "ffn1": 2 + 32, "ffn2": 2 + 32 + 22}
NORM = {"mix": 0, "mem": 1, "xattn": 2, "mlp": 3, "ffn1": 4, "mix2": 5, "ffn2": 6, "final": 7}


def constants():
    p = np.arange(PART)
    parts, where, at = [], {}, 0

    def put(name, a):
        nonlocal at
        a = np.asarray(a, np.float32).reshape(PART, -1)
        where[name] = at
        at += a.shape[1]
        parts.append(a)

    put("ident", np.eye(PART))
    wide = np.zeros((PART, T))
    wide[:, T - PART:] = np.where(p[None, :] <= p[:, None], 0.0, NEG)
    put("causal", wide)
    t = np.arange(T).reshape(QT, PART)
    valid = (np.arange(NCMP) * CMP_S + CMP_L - 1)[None, None, :] <= t[:, :, None]
    put("cmpmask", np.where(valid, 0.0, NEG).transpose(1, 0, 2))
    put("cmpany", (valid.any(-1)).astype(np.float32).T)
    put("tril", (p[:, None] % HALF) <= np.arange(HALF)[None, :])
    put("chunk", np.tile(np.arange(T)[None, :] % HALF != 0, (PART, 1)))
    put("ones", np.ones((PART, T)))
    put("block", (p[:, None] // HALF) == (p[None, :] // HALF))
    rot = np.zeros((PART, PART))
    for o in range(PART):
        if o % HALF < HALF // 2:
            rot[o + HALF // 2, o] = -1.0
        else:
            rot[o - HALF // 2, o] = 1.0
    put("rot", rot)
    inv = (np.float32(1.0) / (np.float32(10000.0) ** (np.arange(0, HALF, 2, dtype=np.float32) / np.float32(HALF)))).astype(np.float32)
    ang = (np.arange(T, dtype=np.float32)[:, None] * inv[None, :]).astype(np.float32)
    put("cos", np.cos(ang).T[p % (HALF // 2)])
    put("sin", np.sin(ang).T[p % (HALF // 2)])
    sel = np.zeros((PART, 8))
    sel[HALF + np.arange(8), np.arange(8)] = -float(HALF) ** 0.5
    put("sel", sel)
    put("eps", np.full((PART, 1), EPS))
    put("one", np.ones((PART, 1)))
    return np.ascontiguousarray(np.concatenate(parts, axis=1)), where


CONSTS, CAT = constants()
N_ROW_LOADS = len(ROWS) + 2


def build(nc, d, out):
    ctx = ExitStack()
    with ctx:
        def sb(name, shape, dt=F32):
            return ctx.enter_context(nc.sbuf_tensor(name, shape, dt))

        def sem(name):
            return ctx.enter_context(nc.semaphore(name))

        h = sb("h", [PART, KT, T])
        xh = sb("xh", [PART, KT, T], F32R)
        xl = sb("xl", [PART, KT, T], F32R)
        ah = sb("ah", [PART, KT, T], F32R)
        al = sb("al", [PART, KT, T], F32R)
        raw = sb("raw", [PART, 2, KT, PC])
        wh = sb("wh", [PART, 2, KT, PC], F32R)
        wl = sb("wl", [PART, 2, KT, PC], F32R)
        cst = sb("cst", [PART, CONSTS.shape[1]])
        gT = sb("gT", [PART, NROWS])
        foxb = sb("foxb", [8, 1])
        lam = sb("lam", [PART, 4])
        gate2 = sb("gate2", [16, GLA_KW])
        negm = sb("negm", [PART, 24])
        rsum = sb("rsum", [PART, 24])
        rinv = sb("rinv", [PART, 24])
        coef = sb("coef", [PART, 24])
        hss = sb("hss", [PART, 4])
        hstd = sb("hstd", [PART, 4])
        hinv = sb("hinv", [PART, 4])
        AW = 16720
        arena = sb("arena", [PART, AW])

        class Arena:
            def __init__(self, at=0):
                self.at = at

            def __call__(self, *shape):
                n = int(np.prod(shape))
                assert self.at + n <= AW, (self.at, n)
                v = arena[:, self.at:self.at + n]
                self.at += n
                if len(shape) == 2:
                    v = v.rearrange("p (a b) -> p a b", a=shape[0])
                elif len(shape) == 3:
                    v = v.rearrange("p (a b c) -> p a b c", a=shape[0], b=shape[1])
                return v

        memT = arena[:, AW - KT * M:].rearrange("p (k t) -> p k t", k=KT)

        def bank(name):
            return ctx.enter_context(nc.psum_tensor(name, [PART, 512], F32))

        pl = [bank("lin0"), bank("lin1")]
        ps = [bank("score0"), bank("score1")]
        pt = [bank("turned0"), bank("turned1")]
        po = [bank("mix0"), bank("mix1")]

        def c_(name, n, rows=PART):
            return cst[0:rows, CAT[name]:CAT[name] + n]

        ident = c_("ident", PART)
        ones = c_("ones", PART)
        eps = c_("eps", 1)

        def gcol(name, k):
            return gT[:, ROWS[name] + k:ROWS[name] + k + 1]

        ld_const, ld_rows, ld_x, ld_mem, ld_late = sem("ld_const"), sem("ld_rows"), sem("ld_x"), sem("ld_mem"), sem("ld_late")
        raw_in = [sem("raw_in0"), sem("raw_in1")]
        hi_done, conv_done = sem("hi_done"), sem("conv_done")
        lin_done = sem("lin_done")
        lin_freed = [sem("lin_freed0"), sem("lin_freed1")]
        st_t, st_c = sem("st_t"), sem("st_c")
        nm_sq, nm_mm, nm_std, nm_rs, nm_xn, nm_hi, nm_lo = (sem("nm_" + n) for n in ("sq", "mm", "std", "rs", "xn", "hi", "lo"))
        hn_mm, hn_std, hn_rs, hn_out = (sem("hn_" + n) for n in ("mm", "std", "rs", "out"))
        ls_a, ls_v = sem("ls_a"), sem("ls_v")
        at_st, at_ks = sem("at_st"), sem("at_ks")
        at_s, at_m, at_p, at_t, at_o, at_r, at_cf, at_of = (sem("at_" + n) for n in ("s", "m", "p", "t", "o", "r", "cf", "of"))
        at_pt = [sem("at_pt0"), sem("at_pt1")]
        fin_n, fin_ss, fin_std, fin_rs = sem("fin_n"), sem("fin_ss"), sem("fin_std"), sem("fin_rs")
        fin_t, fin_g, fin_hi, fin_read = sem("fin_t"), sem("fin_g"), sem("fin_hi"), sem("fin_read")
        rp_t, rp_a, rp_b = sem("rp_t"), sem("rp_a"), sem("rp_b")
        gl_g, gl_st, gl_v, gl_kt, gl_kn, gl_a, gl_at, gl_i, gl_s, gl_oi, gl_on, gl_sv = (
            sem("gl_" + n) for n in ("g", "st", "v", "kt", "kn", "a", "at", "i", "s", "oi", "on", "sv"))
        ml_u, ml_hi, ml_lo = sem("ml_u"), sem("ml_hi"), sem("ml_lo")
        lam_s, lam_p, lam_d = sem("lam_s"), sem("lam_p"), sem("lam_d")
        mg_sg, mg_t, mg_hi, mg_lo = sem("mg_sg"), sem("mg_t"), sem("mg_hi"), sem("mg_lo")
        cb_f, cb_hi, cb_lo, cb_o, cb_k = (sem("cb_" + n) for n in ("f", "hi", "lo", "o", "k"))
        kd = sem("kd")
        go_sp, go_pool, go_pe, go_act, go_dve = sem("go_sp"), sem("go_pool"), sem("go_pe"), sem("go_act"), sem("go_dve")
        zero_s = sem("zero_s")
        out_t, out_c, out_d = sem("out_t"), sem("out_c"), sem("out_d")

        A = Arena()
        x_in, mem_in, rows_in, lp_in = A(QT, D), A(M // PART, D), A(PART), A(4, HALF)

        A = Arena()
        N_sq, N_xn, N_std, N_rs = A(2, T), A(2, T), A(T), A(T)
        N_end = A.at
        F_out, O_nat = A(KT, T), A(QT, D)

        A = Arena()
        SM, PB, PTs = A(2, T), A(2, T), A(2, T)
        att_end = A.at

        A = Arena(att_end)
        X_on = A(QT, PART)
        X_q, X_k = A(2, T), A(2, T)
        X_qk, X_v = A(8, T), A(QT, FOX)
        X_z, X_e, X_c = A(T), A(T), A(T)
        H_sq, H_std, H_rs = SM, PB, PTs
        assert A.at <= AW - KT * M

        A = Arena()
        G_z, G_e = A(2, T), A(2, T)
        G_b = A(2, T)
        G_dec = A(2, T // HALF)
        G_qk, G_ke, G_v, G_r = A(4, T), A(2, T), A(QT, GLA_VW), A(4, T)
        G_qs, G_ks, G_es, G_vs = A(2, PART), A(2, PART), A(2, PART), A(GLA_VW)
        G_kn, G_at, G_S = A(2, PART), A(2, 2, HALF), A(2, PART)
        G_on, G_t = A(4, PART), A(4, PART)
        GLRX = AW - KT * M - T
        assert A.at <= GLRX
        G_glr = arena[:, GLRX:GLRX + T]

        A = Arena(att_end)
        C_on, C_q = A(QT, M), A(2, T)
        C_Q, C_K, C_V = A(KT, T), A(KT, M), A(2, D)
        C_rs = A(2, T)
        C_sq, C_std = C_on.rearrange("p a b -> p (a b)").rearrange("p (a b) -> p a b", a=2), C_q
        assert A.at <= AW - KT * M

        A = Arena(N_end)
        E_t, E_u = A(2, T), A(2, T)

        A = Arena(att_end)
        D_on, D_q, D_k, D_t = A(QT, PART), A(T), A(T), A(2, T)
        D_Q, D_K, D_V = A(4, T), A(4, T), A(QT, 512)
        D_g = A(T)

        A = Arena(att_end)
        S_on, S_qr, S_q, S_t = A(QT, PART), A(T), A(T), A(T)
        S_mg = A(KT, T)
        S_Q = A(4, T)
        S_kd = A(2, 2, T)
        S_v = A(2, QT, PART)
        S_gate = A(QT, 48)
        S_gs = A(QT, 6)
        S_kc, S_vc = A(2 * NCMP), A(2, HALF)
        S_w2k, S_w2v = A(2, PART), A(2, HALF)
        S_h1 = A(2, 2, 2 * NCMP)
        S_sg = A(2, T)
        assert A.at <= AW, A.at
        S_x2 = S_Q
        S_bf = SM
        S_kr = PTs
        S_kraw = PB
        B_h = ah[:, 0:2, :].rearrange("p a b -> p (a b)")[:, 0:16 * 2 * NCMP].rearrange("p (j g n) -> p j g n", j=16, g=2)
        B_l = al[:, 0:2, :].rearrange("p a b -> p (a b)")[:, 0:16 * 2 * NCMP].rearrange("p (j g n) -> p j g n", j=16, g=2)

        def tiles(w):
            return w.rearrange("(q p) n -> p q n", p=PART)

        w_in, w_in2 = tiles(d["w_in"]), tiles(d["w_in_2"][0])
        w_out, w_out2 = tiles(d["w_out"]), tiles(d["w_out_2"][0])
        xwq, xwkv, xwo = tiles(d["xattn_wq"]), tiles(d["xattn_wkv"]), tiles(d["xattn_wo"])
        mw1, mw2 = tiles(d["mlp_w1"]), tiles(d["mlp_w2"])
        ffw = {n: tuple(tiles(d[f"{n}_{w}_2"][0]) for w in ("w1", "w3", "w2")) for n in ("ffn1", "ffn2")}
        wda, wns = tiles(d["w_proj_da_2"][0]), tiles(d["w_proj_nsa_2"][0])
        cw1 = [tiles(d["cmp_w1_2"][0, a]) for a in range(2)]

        block = ctx.enter_context(nc.Block())

        @block.sync
        def _(sp):
            sp.dma_start(cst[:], d["consts"]).then_inc(ld_const, 16)
            n_rows = 0
            for name, r in ROWS.items():
                v = d[name]
                if name in ("fox_q_norm_g", "fox_k_norm_g"):
                    for a in range(2):
                        sp.dma_start(rows_in[r:r + 1, a * HALF:(a + 1) * HALF], v.rearrange("(a n) -> a n", a=1)).then_inc(ld_rows, 16)
                        n_rows += 1
                    continue
                if name == "cmp_pos_2":
                    v = v[0].rearrange("v (j b) e -> (v j) (b e)", b=2)
                elif name == "da_head_norm_2":
                    v = v[0]
                elif len(v.shape) == 2:
                    v = v[0].rearrange("(k p) -> k p", p=PART)
                else:
                    v = v.rearrange("(k p) -> k p", p=PART)
                sp.dma_start(rows_in[r:r + v.shape[0], :], v).then_inc(ld_rows, 16)
                n_rows += 1
            assert n_rows == N_ROW_LOADS
            sp.dma_start(x_in, d["x"][0].rearrange("(t p) n -> p t n", p=PART)).then_inc(ld_x, 16)
            sp.dma_start(mem_in, d["mem"][0].rearrange("(t p) n -> p t n", p=PART)).then_inc(ld_mem, 16)
            sp.dma_start(foxb[:], d["fox_b_f"].rearrange("(n a) -> n a", a=1)).then_inc(ld_late, 16)
            sp.dma_start(gate2[:], d["gla_w_gate2"]).then_inc(ld_late, 16)
            sp.dma_start(lp_in[0:1], d["da_lambda_2"]).then_inc(ld_late, 16)

            def load(p, s, src):
                if not (isinstance(p, int) and p < 2):
                    sp.wait_ge(conv_done, p - 1)
                    sp.sem_inc(go_sp, 1)
                sp.dma_start(raw[:, s, 0:src.shape[1], 0:src.shape[2]], src).then_inc(raw_in[s], 16)

            def run(p0, n, w, col, rows=KT):
                if n <= 2:
                    for j in range(n):
                        load(p0 + j, (p0 + j) % 2, w[:, 0:rows, col + j * PC:col + (j + 1) * PC])
                    return
                with sp.Fori(0, n // 2) as i:
                    for j in range(2):
                        load(i * 2 + (p0 + j), (p0 + j) % 2, w[:, 0:rows, bass.ds(i * (2 * PC) + (col + j * PC), PC)])

            run(P0["fqk"], 2, w_in, W1_COL["fq"])
            run(P0["fqk"] + 2, 2, w_in, W1_COL["fk"])
            run(P0["fv"], 2, w_in, W1_COL["fv"])
            p = P0["small"]
            sp.wait_ge(conv_done, p - 1)
            sp.dma_start(raw[:, p % 2, :, 0:8], w_in[:, :, W1_COL["ff"]:W1_COL["ff"] + 8]).then_inc(raw_in[p % 2], 16)
            sp.wait_ge(raw_in[p % 2], 16 * (p // 2 + 1))
            sp.dma_start(raw[:, p % 2, :, PART:PART + 16], w_in[:, :, W1_COL["glr"]:W1_COL["glr"] + 16]).then_inc(raw_in[p % 2], 16)
            run(P0["gqk"], 2, w_in, W1_COL["gqk"])
            run(P0["gv"], 2, w_in, W1_COL["gv"])
            run(P0["gr"], 2, w_in, W1_COL["gr"])
            run(P0["wout"], 4, w_out, 0)
            run(P0["xk"], 8, xwkv, 0)
            run(P0["xq"], 4, xwq, 0)
            run(P0["xo"], 4, xwo, 0)
            with sp.Fori(0, D_FF // D) as r:
                for j in range(4):
                    load(r * 8 + (P0["mlp"] + j), (P0["mlp"] + j) % 2, mw1[:, :, bass.ds(r * D + j * PC, PC)])
                for j in range(4):
                    load(r * 8 + (P0["mlp"] + 4 + j), (P0["mlp"] + j) % 2, mw2[:, bass.ds(r * KT, KT), j * PC:(j + 1) * PC])

            def ffn(name):
                w1, w3, w2 = ffw[name]
                p0 = P0[name]
                with sp.Fori(0, 2) as r:
                    for j in range(4):
                        for e, w in enumerate((w1, w3)):
                            load(r * 12 + (p0 + 2 * j + e), (p0 + e) % 2, w[:, :, bass.ds(r * D + j * PC, PC)])
                    for j in range(4):
                        load(r * 12 + (p0 + 8 + j), (p0 + j) % 2, w2[:, bass.ds(r * KT, KT), j * PC:(j + 1) * PC])
                for j in range(3):
                    for e, w in enumerate((w1, w3)):
                        load(p0 + 24 + 2 * j + e, (p0 + e) % 2, w[:, :, 2 * D + j * PC:2 * D + (j + 1) * PC])
                for j in range(4):
                    load(p0 + 30 + j, (p0 + j) % 2, w2[:, 2 * KT:, j * PC:(j + 1) * PC])

            ffn("ffn1")
            for a in range(2):
                for n, name in enumerate("qkv"):
                    run(P0[f"da{a}"] + 2 * n, 2, w_in2, W2_COL[name] + a * 512)

            def alternate(p0, wa, ca, wb):
                with sp.Fori(0, 4) as i:
                    load(i * 2 + p0, p0 % 2, wa[:, :, bass.ds(i * PC + ca, PC)])
                    load(i * 2 + (p0 + 1), (p0 + 1) % 2, wb[:, :, bass.ds(i * PC, PC)])

            alternate(P0["mda"], w_in2, W2_COL["ga"], wda)
            for j in range(3):
                load(P0["kv"] + j, (P0["kv"] + j) % 2, w_in2[:, :, W2_COL["kv"] + j * PC:W2_COL["kv"] + (j + 1) * PC])
            load(P0["kv"] + 3, (P0["kv"] + 3) % 2, w_in2[:, :, W2_COL["gate"]:W2_COL["gate"] + 48])
            for a in range(2):
                for j in range(2):
                    load(P0["cmp"] + 2 * a + j, (P0["cmp"] + j) % 2, cw1[a][:, j * KT:(j + 1) * KT, :])
            sp.wait_ge(lin_freed[1], P0["kv"])
            w2 = d["cmp_w2_2"][0].rearrange("a (c p) e -> a p c e", p=PART)
            for a in range(2):
                sp.dma_start(S_w2k[:, :, a * HALF:(a + 1) * HALF], w2[0]).then_inc(ld_late, 16)
            sp.dma_start(S_w2v, w2[1]).then_inc(ld_late, 16)
            for g in range(2):
                run(P0[f"nq{g}"], 2, w_in2, W2_COL["nq"] + g * 512)
            alternate(P0["mnsa"], w_in2, W2_COL["gb"], wns)
            run(P0["wout2"], 4, w_out2, 0)
            ffn("ffn2")
            for t in range(QT):
                sp.wait_ge(out_c, 2 * t + 2)
                sp.dma_start(out[0, t * PART:(t + 1) * PART, :], O_nat[:, t, :]).then_inc(out_d, 16)
            sp.wait_ge(out_d, 16 * QT)

        @block.gpsimd
        def _(pool):
            small = P0["small"]
            one = c_("one", 1).unsqueeze(2).to_broadcast([PART, KT, PC])
            pool.wait_ge(ld_const, 16)

            def cut(p, s):
                pool.wait_ge(raw_in[s], landed(p, s))
                if not (isinstance(p, int) and p < 2):
                    pool.wait_ge(lin_done, p * 2 - 2)
                nc.gpsimd.tensor_tensor(wh[:, s], raw[:, s], one, ALU.mult).then_inc(hi_done, 1)
                pool.wait_ge(hi_done, p + 1)
                nc.gpsimd.tensor_tensor(wl[:, s], raw[:, s], wh[:, s].bitcast(F32), ALU.subtract).then_inc(conv_done, 1)

            def landed(p, s):
                if isinstance(p, int):
                    return 16 * (p // 2 + 1 + (s == small % 2 and p >= small))
                return p * 8 + (16 + 16 * (s == small % 2) - 8 * s)

            first = small + 1
            first += first % 2
            for p in range(first):
                cut(p, p % 2)
            with pool.Fori(0, (PANELS - first) // 2) as i:
                for s in range(2):
                    cut(i * 2 + (first + s), s)
            if (PANELS - first) % 2:
                cut(PANELS - 1, (PANELS - 1) % 2)

        @block.tensor
        def _(pe):
            pe.sem_inc(at_s, UINIT)
            pe.sem_inc(at_t, UINIT)
            pe.sem_inc(at_o, UINIT)
            pe.sem_inc(fin_t, FINIT)
            pe.sem_inc(gl_i, 2)

            def product(o, w, x, first, last):
                nc.tensor.matmul(o, w[0], x[0], start=first, stop=False)
                nc.tensor.matmul(o, w[0], x[1], start=False, stop=False)
                return nc.tensor.matmul(o, w[1], x[0], start=False, stop=last)

            def begin(p, c):
                if not (isinstance(p, int) and p == 0):
                    pe.wait_ge(lin_freed[c], p)

            def panel_t(p, s, act, n=T, kt=KT, m=PART, each=None):
                pe.wait_ge(conv_done, p + 1)
                for c in range(2):
                    begin(p, c)
                    mc = m if isinstance(m, int) else m[c]
                    for k in range(kt):
                        if each and c == 0:
                            each(k)
                        cols = slice(c * PART, c * PART + mc)
                        mm = product(pl[c][0:mc, 0:n], (wh[:, s, k, cols], wl[:, s, k, cols]),
                                     (act[0][:, k, 0:n], act[1][:, k, 0:n]), k == 0, k == kt - 1)
                    mm.then_inc(lin_done, 1)

            def panel_n(p, s, act, cols=(0, PC), tiles_=((0, 1), (2, 3)), only=None):
                pe.wait_ge(conv_done, p + 1)
                for c in range(2) if only is None else (only,):
                    begin(p, c)
                    n = cols[1] - cols[0]
                    for j, t in enumerate(tiles_[c]):
                        for k in range(KT):
                            tok = slice(t * PART, (t + 1) * PART)
                            mm = product(pl[c][:, j * n:(j + 1) * n], (act[0][:, k, tok], act[1][:, k, tok]),
                                         (wh[:, s, k, cols[0]:cols[1]], wl[:, s, k, cols[0]:cols[1]]), k == 0, k == KT - 1)
                    mm.then_inc(lin_done, 1)

            X, Y = (xh, xl), (ah, al)

            def run_t(p0, n, act, kt=KT, each=None):
                if each or n <= 2:
                    for j in range(min(n, 2)):
                        panel_t(p0 + j, (p0 + j) % 2, act, kt=kt, each=each if j == 0 else None)
                    p0, n = p0 + 2, n - 2
                if n > 0:
                    with pe.Fori(0, n // 2) as i:
                        for j in range(2):
                            panel_t(i * 2 + (p0 + j), (p0 + j) % 2, act, kt=kt)

            def sums(call, n=T):
                for k in range(KT):
                    pe.wait_ge(nm_sq, 8 * call + k + 1)
                    nc.tensor.matmul(po[0][:, 0:n], ones, N_sq[:, k % 2, 0:n], start=(k == 0), stop=(k == KT - 1)).then_inc(nm_mm, 1)

            def units(U, Uh, us):
                n = len(us)
                for s in range(n + 3):
                    if s < n:
                        q, k, nk = us[s]["q"], us[s]["k"], us[s]["nk"]
                        pe.wait_ge(at_m, U + (s - 1))
                        for a in range(len(q)):
                            mm = nc.tensor.matmul(ps[s % 2][:, 0:nk], q[a], k[a], start=(a == 0), stop=(a == len(q) - 1))
                        mm.then_inc(at_s, 1)
                    if 2 <= s < n + 2:
                        j = s - 2
                        pe.wait_ge(at_p, U + (j + 1))
                        pe.wait_ge(at_pt[j % 2], Uh + j // 2)
                        for b, (lo, w) in enumerate(us[j]["blocks"]):
                            mm = nc.tensor.transpose(pt[j % 2][0:w, b * PART:(b + 1) * PART], PB[:, j % 2, lo:lo + w], ident)
                        mm.then_inc(at_t, 1)
                    if s >= 3:
                        j = s - 3
                        pe.wait_ge(at_pt[j % 2], Uh + (j // 2 + 1))
                        pe.wait_ge(at_of, U + (j - 1))
                        for b, (lo, w) in enumerate(us[j]["blocks"]):
                            mm = nc.tensor.matmul(po[j % 2][:, 0:us[j]["dv"]], PTs[0:w, j % 2, b * PART:(b + 1) * PART], us[j]["v"][b],
                                                  start=(b == 0), stop=(b == len(us[j]["blocks"]) - 1))
                        mm.then_inc(at_o, 1)

            def turn_back(F, f, src, width=PART):
                pe.wait_ge(fin_read, F)
                for t in range(QT):
                    mm = nc.tensor.transpose(pl[f][:, t * PART:(t + 1) * PART], src[:, t, f * PART:(f + 1) * PART], ident)
                mm.then_inc(fin_t, 1)

            pe.wait_ge(ld_const, 16)
            pe.wait_ge(ld_rows, 16 * N_ROW_LOADS)
            nc.tensor.transpose(pt[0][:, 0:NROWS], rows_in[0:NROWS, :], cst[0:NROWS, CAT["ident"]:CAT["ident"] + NROWS]).then_inc(st_t, 1)
            pe.wait_ge(ld_x, 16)
            for g in range(1, 17):
                if g == 9:
                    pe.wait_ge(ld_mem, 16)
                if g >= 2:
                    pe.wait_ge(st_c, g - 1)
                src = x_in if g < 9 else mem_in
                k = (g - 1) % KT
                for t in range(src.shape[1]):
                    mm = nc.tensor.transpose(pt[g % 2][:, t * PART:(t + 1) * PART], src[:, t, k * PART:(k + 1) * PART], ident)
                mm.then_inc(st_t, 1)
            pe.wait_ge(lam_s, 5)
            nc.tensor.matmul(ps[0][:, 0:1], cst[0:1, CAT["ones"]:CAT["ones"] + PART], lam[0:1, 2:3], start=True, stop=True).then_inc(lam_p, 1)

            sums(NORM["mix"])
            pe.wait_ge(nm_lo, 8 * NORM["mix"] + 8)
            pe.wait_ge(lam_d, 1)

            def head_sums(j, tile_sq, lhs):
                if j >= 2:
                    pe.wait_ge(hn_std, j - 1)
                for a, sq in enumerate(tile_sq):
                    mm = nc.tensor.matmul(po[j % 2][:, 0:sq.shape[-1]], lhs, sq, start=(a == 0), stop=(a == len(tile_sq) - 1))
                mm.then_inc(hn_mm, 1)

            def fox_sums(p):
                for c in range(2):
                    pe.wait_ge(lin_freed[c], p + 1)
                    head_sums(2 * p + c, [H_sq[:, c, :]], c_("block", PART))

            for p in range(P0["fv"]):
                panel_t(p, p % 2, X)
                if p:
                    fox_sums(p - 1)
            for p in range(P0["fv"], P0["fv"] + 2):
                panel_n(p, p % 2, X)
                if p == P0["fv"]:
                    fox_sums(p - 1)
            panel_t(P0["small"], P0["small"] % 2, X, m=(8, 16))

            def causal(heads, dv, v, mask_rows=None):
                us = []
                for q, k, hv in heads:
                    for t in range(QT):
                        nk = (t + 1) * PART
                        us.append(dict(q=[q[:, t * PART:(t + 1) * PART]], k=[k[:, 0:nk]], nk=nk, dv=dv,
                                       blocks=[(b * PART, PART) for b in range(t + 1)], v=[v(b, hv) for b in range(t + 1)]))
                return us

            with pe.Fori(0, 4) as i:
                pe.wait_ge(at_st, i + (A0["fox"] + 1))
                pe.wait_ge(at_ks, i + (A0["fox"] + 1))
                us = causal([(X_q[0:HALF + 8, a, :], X_k[0:HALF + 8, a, :], a) for a in range(2)], HALF,
                            lambda b, a: X_v[:, b, bass.ds(i * PART + a * HALF, HALF)])
                units(i * 8 + U0["fox"], i * 4 + U0["fox"] // 2, us)
                pe.wait_ge(at_of, i * 8 + (U0["fox"] + 8))
                turn_back(i + F0["fox"], 0, X_on)
            pe.wait_ge(fin_read, F0["gla"])

            p = P0["gqk"]
            pe.wait_ge(ld_late, 16 * 3)
            for a in range(2):
                nc.tensor.matmul(po[a][:, :], gate2[0:16, a * PART:(a + 1) * PART], G_glr[0:16, :], start=True, stop=True).then_inc(gl_g, 1)
            for j in range(2):
                panel_t(p + j, (p + j) % 2, X)
            for j in range(2):
                panel_n(P0["gv"] + j, (P0["gv"] + j) % 2, X)
            for j in range(2):
                panel_t(P0["gr"] + j, (P0["gr"] + j) % 2, X)

            with pe.Fori(0, QT) as i:
                pe.wait_ge(gl_st, i + 1)
                pe.sem_inc(go_pe, 1)
                for a in range(2):
                    mm = nc.tensor.transpose(pt[0][:, a * PART:(a + 1) * PART], G_es[:, a, :], ident)
                mm.then_inc(gl_kt, 1)
                for c in range(2):
                    for hd in range(4):
                        a, b = hd // 2, hd % 2
                        r = slice(b * HALF, (b + 1) * HALF)
                        tk = slice(c * HALF, (c + 1) * HALF)
                        mm = nc.tensor.matmul(ps[b][tk, a * HALF:(a + 1) * HALF], G_ks[r, a, tk], G_qs[r, a, tk], start=True, stop=True)
                mm.then_inc(gl_a, 1)
                pe.wait_ge(gl_kn, i + 1)
                pe.wait_ge(gl_at, i + 1)
                pe.wait_ge(gl_v, i + 1)
                pe.sem_inc(go_pe, 1)
                for c in range(2):
                    tk = slice(c * HALF, (c + 1) * HALF)
                    pe.wait_ge(gl_s, i * 2 + (c + 1))
                    pe.sem_inc(go_pe, 1)
                    for hd in range(4):
                        a, b = hd // 2, hd % 2
                        r = slice(b * HALF, (b + 1) * HALF)
                        nc.tensor.matmul(po[b][tk, a * PART:(a + 1) * PART], G_qs[r, a, tk], G_S[r, a, :], start=True, stop=True)
                    for hd in range(4):
                        a, b = hd // 2, hd % 2
                        nc.tensor.matmul(pt[c][tk, hd * PART:(hd + 1) * PART], G_at[tk, b, a, :], G_vs[tk, hd * PART:(hd + 1) * PART], start=True, stop=True)
                    for hd in range(4):
                        a, b = hd // 2, hd % 2
                        r = slice(b * HALF, (b + 1) * HALF)
                        mm = nc.tensor.matmul(ps[c][r, 256 + a * PART:256 + (a + 1) * PART], G_kn[tk, a, r], G_vs[tk, hd * PART:(hd + 1) * PART], start=True, stop=True)
                    mm.then_inc(gl_i, 1)
                pe.wait_ge(fin_rs, i + 1)
                pe.wait_ge(fin_read, i + F0["gla"])
                pe.sem_inc(go_pe, 1)
                for hd in range(4):
                    mm = nc.tensor.transpose(pl[0][:, hd * PART:(hd + 1) * PART], G_on[:, hd, :], ident)
                mm.then_inc(fin_t, 1)
            pe.wait_ge(fin_read, F0["gla"] + 4)

            run_t(P0["wout"], 4, Y)

            sums(NORM["mem"], M)
            sums(NORM["xattn"])
            pe.wait_ge(nm_lo, 8 * NORM["mem"] + 8)

            def pair_sums(p, j, n):
                for c in range(2):
                    pe.wait_ge(lin_freed[c], p + 1)
                head_sums(j, [C_sq[:, c, 0:n] for c in range(2)], ones)

            for j in range(4):
                p = P0["xk"] + j
                panel_t(p, p % 2, Y, n=M)
                if j:
                    pair_sums(p - 1, 8 + j - 1, M)
            for j in range(4):
                p = P0["xv"] + j
                panel_n(p, p % 2, Y, tiles_=((0,), (1,)))
                if j == 0:
                    pair_sums(p - 1, 8 + 3, M)
            pe.wait_ge(nm_lo, 8 * NORM["xattn"] + 8)
            for j in range(4):
                p = P0["xq"] + j
                panel_t(p, p % 2, X)
                if j:
                    pair_sums(p - 1, 12 + j - 1, T)
            pair_sums(P0["xq"] + 3, 12 + 3, T)
            with pe.Fori(0, 4) as i:
                pe.wait_ge(at_st, i + (A0["xa"] + 1))
                us = [dict(q=[C_q[:, a, t * PART:(t + 1) * PART] for a in range(2)],
                           k=[C_K[:, bass.ds(i * 2 + a, 1), :].rearrange("p a n -> p (a n)") for a in range(2)], nk=M, dv=M,
                           blocks=[(b * PART, PART) for b in range(2)],
                           v=[C_V[:, b, bass.ds(i * M, M)] for b in range(2)]) for t in range(QT)]
                units(i * 4 + U0["xa"], i * 2 + U0["xa"] // 2, us)
                pe.wait_ge(at_of, i * 4 + (U0["xa"] + 4))
                for f in range(2):
                    turn_back(i * 2 + (F0["xa"] + f), f, C_on)
            pe.wait_ge(fin_read, F0["da0"])
            run_t(P0["xo"], 4, Y)

            sums(NORM["mlp"])
            pe.wait_ge(nm_lo, 8 * NORM["mlp"] + 8)
            with pe.Fori(0, D_FF // D) as r:
                for j in range(4):
                    panel_t(r * 8 + (P0["mlp"] + j), (P0["mlp"] + j) % 2, X)
                for j in range(4):
                    panel_t(r * 8 + (P0["mlp"] + 4 + j), (P0["mlp"] + j) % 2, Y,
                            each=(lambda k: pe.wait_ge(ml_lo, r * 8 + (MLP0["mlp"] + k + 1))) if j == 0 else None)

            def ffn(name):
                sums(NORM[name])
                pe.wait_ge(nm_lo, 8 * NORM[name] + 8)
                p0, m0 = P0[name], MLP0[name]
                with pe.Fori(0, 2) as r:
                    for j in range(8):
                        panel_t(r * 12 + (p0 + j), (p0 + j) % 2, X)
                    for j in range(4):
                        panel_t(r * 12 + (p0 + 8 + j), (p0 + j) % 2, Y,
                                each=(lambda k: pe.wait_ge(ml_lo, r * 8 + (m0 + k + 1))) if j == 0 else None)
                for j in range(6):
                    panel_t(p0 + 24 + j, (p0 + j) % 2, X)
                for j in range(4):
                    panel_t(p0 + 30 + j, (p0 + j) % 2, Y, kt=6, each=(lambda k: pe.wait_ge(ml_lo, m0 + 16 + k + 1)) if j == 0 else None)

            ffn("ffn1")
            sums(NORM["mix2"])
            pe.wait_ge(nm_lo, 8 * NORM["mix2"] + 8)

            def rotate(R, o, src):
                nc.tensor.matmul(o[:, :], c_("rot", PART), src, start=True, stop=True).then_inc(rp_t, 1)

            for hf in range(2):
                st = f"da{hf}"
                for j in range(4):
                    panel_t(P0[st] + j, (P0[st] + j) % 2, X)
                for j in range(4, 6):
                    panel_n(P0[st] + j, (P0[st] + j) % 2, X)
                for c in range(2):
                    pe.wait_ge(lin_freed[c], P0[st] + 6)
                with pe.Fori(0, 4) as i:
                    pe.wait_ge(fin_read, i + F0[st])
                    for a, src in enumerate((D_Q, D_K)):
                        rotate(None, pl[a], src[:, bass.ds(i, 1), :].rearrange("p a n -> p (a n)"))
                    pe.wait_ge(at_st, i + (A0[st] + 1))
                    us = causal([(D_q[a * HALF:(a + 1) * HALF, :], D_k[a * HALF:(a + 1) * HALF, :], a) for a in range(2)], PART,
                                lambda b, a: D_V[:, b, bass.ds(i * PART, PART)])
                    units(i * 8 + U0[st], i * 4 + U0[st] // 2, us)
                    pe.wait_ge(fin_rs, i + (4 + 4 * hf + 1))
                    turn_back(i + F0[st], 0, D_on)
                pe.wait_ge(fin_read, F0[st] + 4)

            def alternate(p0):
                with pe.Fori(0, 4) as i:
                    panel_t(i * 2 + p0, p0 % 2, X)
                    panel_t(i * 2 + (p0 + 1), (p0 + 1) % 2, Y)

            alternate(P0["mda"])

            p = P0["kv"]
            panel_t(p, p % 2, X)
            for br in range(2):
                q = p + 1 + br
                pe.wait_ge(conv_done, q + 1)
                begin(q, 0)
                for k in range(KT):
                    mm = product(pl[0][:, :], (wh[:, q % 2, k, 0:PART], wl[:, q % 2, k, 0:PART]), (xh[:, k, :], xl[:, k, :]), k == 0, k == KT - 1)
                mm.then_inc(lin_done, 1)
                panel_n(q, q % 2, X, cols=(PART, 2 * PART), tiles_=(None, (0, 1, 2, 3)), only=1)
            panel_n(p + 3, (p + 3) % 2, X, cols=(0, 48))
            for br in range(2):
                pe.wait_ge(lin_freed[0], p + 2 + br)
                rotate(None, po[br], S_kraw[:, br, :])
            for a in range(2):
                for part in range(2):
                    q = P0["cmp"] + 2 * a + part
                    pe.wait_ge(conv_done, q + 1)
                    for c in range(2):
                        if part == 0:
                            begin(q, c)
                        if part == 0 and c == 0:
                            pe.wait_ge(cb_lo, 2 * a + 2)
                        for k in range(KT):
                            j = part * KT + k
                            cols = slice(c * PART, (c + 1) * PART)
                            mm = product(pl[c][:, 0:2 * NCMP], (wh[:, q % 2, k, cols], wl[:, q % 2, k, cols]),
                                         (B_h[:, j].rearrange("p g n -> p (g n)"), B_l[:, j].rearrange("p g n -> p (g n)")), j == 0, j == 15)
                        mm.then_inc(lin_done, 1)
            for c in range(2):
                pe.wait_ge(lin_freed[c], P0["cmp"] + 4)
            pe.wait_ge(ld_late, 16 * 6)
            pe.wait_ge(kd, 1)
            for c in range(2):
                mm = nc.tensor.matmul(po[0][:, 0:2 * NCMP], S_w2k[:, c, :], S_h1[:, 0, c, :], start=(c == 0), stop=(c == 1))
            mm.then_inc(cb_o, 1)
            for g in range(2):
                for c in range(2):
                    mm = nc.tensor.matmul(po[1][0:NCMP, g * HALF:(g + 1) * HALF], S_h1[:, 1, c, g * NCMP:(g + 1) * NCMP], S_w2v[:, c, :],
                                          start=(c == 0), stop=(c == 1))
            mm.then_inc(cb_o, 1)
            pe.wait_ge(cb_k, 2)

            for g in range(2):
                st = f"ns{g}"
                for j in range(2):
                    panel_t(P0[f"nq{g}"] + j, (P0[f"nq{g}"] + j) % 2, X)
                for c in range(2):
                    pe.wait_ge(lin_freed[c], P0[f"nq{g}"] + 2)
                with pe.Fori(0, 4) as i:
                    pe.wait_ge(fin_read, i + F0[st])
                    rotate(None, pl[1], S_Q[:, bass.ds(i, 1), :].rearrange("p a n -> p (a n)"))
                    pe.wait_ge(at_st, i + (A0[st] + 1))
                    us = []
                    for a in range(2):
                        r = slice(a * HALF, (a + 1) * HALF)
                        for t in range(QT):
                            us.append(dict(q=[S_qr[r, t * PART:(t + 1) * PART]], k=[S_kc[r, g * NCMP:(g + 1) * NCMP]], nk=NCMP, dv=HALF,
                                           blocks=[(0, NCMP)], v=[S_vc[0:NCMP, g, :]]))
                    for br in range(2):
                        us += causal([(S_q[a * HALF:(a + 1) * HALF, :], S_kd[a * HALF:(a + 1) * HALF, br, g, :], a) for a in range(2)], HALF,
                                     lambda b, a: S_v[:, br, b, g * HALF:(g + 1) * HALF])
                    units(i * 24 + U0[st], i * 12 + U0[st] // 2, us)
                    pe.wait_ge(at_of, i * 24 + (U0[st] + 24))
                    turn_back(i + F0[st], 0, S_on)
                pe.wait_ge(fin_read, F0[st] + 4)
            alternate(P0["mnsa"])
            pe.wait_ge(mg_lo, 8)
            run_t(P0["wout2"], 4, Y)
            ffn("ffn2")

            sums(NORM["final"])
            pe.wait_ge(nm_xn, 8 * NORM["final"] + 8)
            for g in range(2 * QT):
                t, f0 = g // 2, 4 * (g % 2)
                if g >= 2:
                    pe.wait_ge(out_c, g - 1)
                for f in range(4):
                    mm = nc.tensor.transpose(pt[g % 2][:, f * PART:(f + 1) * PART], F_out[:, f0 + f, t * PART:(t + 1) * PART], ident)
                mm.then_inc(out_t, 1)

        @block.scalar
        def _(act):
            act.sem_inc(at_p, UINIT)
            act.sem_inc(at_pt[1], UINIT // 2)
            act.sem_inc(fin_hi, FINIT)
            act.sem_inc(ml_hi, 2)

            def tile(p, c):
                act.wait_ge(lin_done, p * 2 + (c + 1))

            def dyn(buf, e):
                return buf[:, bass.ds(e, 1), :].rearrange("p a n -> p (a n)")

            def evac(p, c, dst, func=ACT.Copy, rows=PART, n=T, **kw):
                tile(p, c)
                nc.scalar.activation(dst, pl[c][0:rows, 0:n], func, **kw).then_inc(lin_freed[c], 1)

            def norm(call, src, ready, n=T, dst=None, after=None):
                for k in range(KT):
                    ready(k)
                    if call or k >= 2:
                        act.wait_ge(nm_mm, 8 * call + k - 1)
                    nc.scalar.activation(N_sq[:, k % 2, 0:n], src[:, k, 0:n], ACT.Square).then_inc(nm_sq, 1)
                act.wait_ge(nm_mm, 8 * call + 8)
                nc.scalar.activation(N_std[:, 0:n], po[0][:, 0:n], ACT.Sqrt, bias=eps, scale=1.0 / D).then_inc(nm_std, 1)
                if dst is None:
                    return
                if after:
                    act.wait_ge(lin_done, 2 * after)
                for k in range(KT):
                    act.wait_ge(nm_xn, 8 * call + k + 1)
                    nc.scalar.activation(dst[:, k, 0:n], N_xn[:, k % 2, 0:n], ACT.Copy).then_inc(nm_hi, 1)

            def units(U, Uh, us):
                n = len(us)
                for s in range(n + 2):
                    if s < n:
                        nk = us[s]["nk"]
                        act.wait_ge(at_m, U + (s + 1))
                        act.wait_ge(at_t, U + (s - 1))
                        act.sem_inc(go_act, 1)
                        nc.scalar.activation(PB[:, s % 2, 0:nk], SM[:, s % 2, 0:nk], ACT.Exp, bias=negm[:, s:s + 1], scale=-1.0,
                                             accum_out=rsum[:, s:s + 1]).then_inc(at_p, 1)
                    j = s - 2
                    if j >= 0 and j % 2 == 1:
                        w, nb = us[j]["w"], us[j]["nb"]
                        act.wait_ge(at_t, U + (j + 1))
                        act.wait_ge(at_o, U + (j - 1))
                        act.sem_inc(go_act, 1)
                        nc.scalar.activation(PTs[0:w, 1, 0:nb * PART], pt[1][0:w, 0:nb * PART], ACT.Copy).then_inc(at_pt[1], 1)

            def finish(F, f, dst):
                act.wait_ge(fin_t, F + 1)
                act.sem_inc(go_act, 1)
                nc.scalar.activation(dst, pl[f][:, :], ACT.Copy).then_inc(fin_hi, 1)

            def causal_units(n=2):
                return [dict(nk=(t + 1) * PART, w=PART, nb=t + 1) for _ in range(n) for t in range(QT)]

            act.wait_ge(st_t, 1)
            nc.scalar.activation(gT[:], pt[0][:, 0:NROWS], ACT.Copy).then_inc(st_c, 1)
            for g in range(1, 17):
                act.wait_ge(st_t, g + 1)
                dst, n = (h[:, g - 1, :], T) if g < 9 else (memT[:, g - 9, :], M)
                nc.scalar.activation(dst, pt[g % 2][:, 0:n], ACT.Copy).then_inc(st_c, 1)
            act.wait_ge(lam_s, 2)
            nc.scalar.activation(lam[0:1, 0:2], lam[0:1, 0:2], ACT.Exp).then_inc(lam_s, 1)
            norm(NORM["mix"], h, lambda k: act.wait_ge(st_c, 17), dst=xh)

            def root(j, std, n, width):
                act.wait_ge(hn_mm, j + 1)
                if j >= 2:
                    act.wait_ge(hn_rs, j - 1)
                nc.scalar.activation(std[:, j % 2, 0:n], po[j % 2][:, 0:n], ACT.Sqrt, bias=eps, scale=1.0 / width).then_inc(hn_std, 1)

            for p in range(P0["small"]):
                for c in range(2):
                    tile(p, c)
                    if p < P0["fv"]:
                        k = 2 * p + c
                        nc.scalar.activation(X_qk[:, k, :], pl[c][:, :], ACT.Copy)
                        if k >= 2:
                            act.wait_ge(hn_mm, k - 1)
                        nc.scalar.activation(H_sq[:, c, :], pl[c][:, :], ACT.Square).then_inc(lin_freed[c], 1)
                    else:
                        j = p - P0["fv"]
                        nc.scalar.activation(X_v[:, 2 * c:2 * c + 2, j * PC:(j + 1) * PC], pl[c][:, :].rearrange("p (a n) -> p a n", a=2),
                                             ACT.Copy).then_inc(lin_freed[c], 1)
                if 1 <= p <= P0["fv"]:
                    for c in range(2):
                        root(2 * (p - 1) + c, H_std, T, HALF)
            p = P0["small"]
            act.wait_ge(ld_late, 16 * 3)
            evac(p, 0, X_z[0:8, :], ACT.Identity, rows=8, bias=foxb[:, 0:1])
            evac(p, 1, G_glr[0:16, :], rows=16)
            act.wait_ge(lin_freed[0], p + 1)
            nc.scalar.activation(X_e[0:8, :], X_z[0:8, :], ACT.Abs).then_inc(ls_a, 1)
            act.wait_ge(ls_a, 1)
            nc.scalar.activation(X_e[0:8, :], X_e[0:8, :], ACT.Exp, scale=-1.0).then_inc(ls_a, 1)
            act.wait_ge(ls_a, 2)
            nc.scalar.activation(X_e[0:8, :], X_e[0:8, :], ACT.Ln, bias=c_("one", 1, 8)).then_inc(ls_a, 1)
            act.wait_ge(hn_out, 8)
            with act.Fori(0, 4) as i:
                act.wait_ge(at_s, i * 8 + U0["fox"])
                act.sem_inc(go_act, 1)
                for a in range(2):
                    src = X_qk[a * HALF:(a + 1) * HALF, bass.ds(i + 4, 1), :].rearrange("p a n -> p (a n)")
                    op = nc.scalar.activation(X_k[0:HALF, a, :], src, ACT.Copy)
                op.then_inc(at_ks, 1)
                units(i * 8 + U0["fox"], i * 4 + U0["fox"] // 2, causal_units())
                finish(i + F0["fox"], 0, dyn(ah, i))

            for a in range(2):
                act.wait_ge(gl_g, a + 1)
                nc.scalar.activation(G_z[:, a, :], po[a][:, :], ACT.Identity, bias=gcol("gla_b_gate", a)).then_inc(ls_a, 1)
            act.wait_ge(ls_a, 5)
            nc.scalar.activation(G_e, G_z, ACT.Abs).then_inc(ls_a, 1)
            act.wait_ge(ls_a, 6)
            nc.scalar.activation(G_e, G_e, ACT.Exp, scale=-1.0).then_inc(ls_a, 1)
            act.wait_ge(ls_a, 7)
            nc.scalar.activation(G_e, G_e, ACT.Ln, bias=c_("one", 1)).then_inc(ls_a, 1)
            last = G_b.rearrange("p a (n c) -> p (a n) c", c=HALF)[:, :, HALF - 1:HALF].rearrange("p n c -> p (n c)")
            act.wait_ge(ls_v, 7)
            nc.scalar.activation(G_e, G_b, ACT.Exp, scale=1.0 / 16).then_inc(ls_a, 1)
            nc.scalar.activation(G_dec.rearrange("p a n -> p (a n)"), last, ACT.Exp, scale=1.0 / 16).then_inc(ls_a, 1)
            act.wait_ge(ls_v, 8)
            nc.scalar.activation(G_ke, G_z, ACT.Exp, scale=1.0 / 16).then_inc(ls_a, 1)
            for j in range(2):
                for c in range(2):
                    evac(P0["gqk"] + j, c, G_qk[:, 2 * j + c, :])
            act.wait_ge(ls_v, 9)
            nc.scalar.activation(G_e, G_b, ACT.Exp, scale=-1.0 / 16).then_inc(ls_a, 1)
            for j in range(2):
                for c in range(2):
                    p = P0["gv"] + j
                    tile(p, c)
                    nc.scalar.activation(G_v[:, 2 * c:2 * c + 2, j * PC:(j + 1) * PC], pl[c][:, :].rearrange("p (a n) -> p a n", a=2),
                                         ACT.Copy).then_inc(lin_freed[c], 1)
            for j in range(2):
                for c in range(2):
                    evac(P0["gr"] + j, c, G_r[:, 2 * j + c, :], ACT.Silu)
            with act.Fori(0, QT) as i:
                act.wait_ge(gl_i, i * 2 + 2)
                act.sem_inc(go_act, 1)
                nc.scalar.activation(G_vs, dyn(G_v, i), ACT.Copy).then_inc(gl_v, 1)
                act.wait_ge(gl_i, i * 2 + 4)
                act.wait_ge(fin_t, i + F0["gla"])
                act.sem_inc(go_act, 1)
                for c in range(2):
                    r = slice(c * HALF, (c + 1) * HALF)
                    op = nc.scalar.activation(G_on[r].rearrange("p a n -> p (a n)"), pt[c][r, :], ACT.Copy)
                op.then_inc(gl_on, 1)
                act.wait_ge(gl_oi, i + 1)
                act.wait_ge(fin_read, i + F0["gla"])
                act.sem_inc(go_act, 1)
                for hd in range(4):
                    op = nc.scalar.activation(G_t[:, hd, :], G_on[:, hd, :], ACT.Square, accum_out=hss[:, hd:hd + 1])
                op.then_inc(fin_ss, 1)
                act.wait_ge(fin_ss, i + 1)
                nc.scalar.activation(hstd[:], hss[:], ACT.Sqrt, bias=eps, scale=1.0 / PART).then_inc(fin_std, 1)
                act.wait_ge(fin_g, i + 1)
                act.sem_inc(go_act, 1)
                nc.scalar.activation(ah[:, 4:8, bass.ds(i * PART, PART)], G_t, ACT.Copy).then_inc(fin_hi, 1)

            norm(NORM["mem"], memT, lambda k: act.wait_ge(lin_done, 2 * P0["xk"]) if k == 0 else None, n=M, dst=ah)
            norm(NORM["xattn"], h, lambda k: act.wait_ge(lin_freed[k % 2], P0["wout"] + k // 2 + 1), dst=xh)

            def evac_pair(p, j, dst, n):
                for c in range(2):
                    tile(p, c)
                    nc.scalar.activation(dst[:, 2 * (j % 4) + c, :], pl[c][:, 0:n], ACT.Copy)
                    if j > 8:
                        act.wait_ge(hn_mm, j)
                    nc.scalar.activation(C_sq[:, c, 0:n], pl[c][:, 0:n], ACT.Square).then_inc(lin_freed[c], 1)

            for j in range(4):
                evac_pair(P0["xk"] + j, 8 + j, C_K, M)
                if j:
                    root(8 + j - 1, C_std, M, M)
            for j in range(4):
                for c in range(2):
                    evac(P0["xv"] + j, c, C_V[:, c, j * PC:(j + 1) * PC], n=PC)
                if j == 0:
                    root(8 + 3, C_std, M, M)
            for j in range(4):
                evac_pair(P0["xq"] + j, 12 + j, C_Q, T)
                if j:
                    root(12 + j - 1, C_std, T, M)
            root(12 + 3, C_std, T, M)
            with act.Fori(0, 4) as i:
                units(i * 4 + U0["xa"], i * 2 + U0["xa"] // 2, [dict(nk=M, w=PART, nb=2) for _ in range(QT)])
                for f in range(2):
                    finish(i * 2 + (F0["xa"] + f), f, dyn(ah, i * 2 + f))

            norm(NORM["mlp"], h, lambda k: act.wait_ge(lin_freed[k % 2], P0["xo"] + k // 2 + 1), dst=xh)
            with act.Fori(0, D_FF // D) as r:
                for j in range(4):
                    for c in range(2):
                        k = 2 * j + c
                        m = r * 8 + (MLP0["mlp"] + k)
                        act.wait_ge(ml_u, m - 1)
                        tile(r * 8 + (P0["mlp"] + j), c)
                        act.sem_inc(go_act, 1)
                        nc.scalar.activation(E_t[:, c, :], pl[c][:, :], ACT.Relu).then_inc(lin_freed[c], 1)
                        act.wait_ge(ml_u, m + 1)
                        nc.scalar.activation(ah[:, k, :], E_u[:, c, :], ACT.Copy).then_inc(ml_hi, 1)

            def gated(p, m, j):
                for c in range(2):
                    act.wait_ge(lin_freed[c], p)
                    tile(p, c)
                    act.sem_inc(go_act, 1)
                    nc.scalar.activation(E_t[:, c, :], pl[c][:, :], ACT.Silu).then_inc(lin_freed[c], 1)
                for c in range(2):
                    act.wait_ge(lin_freed[c], p + 2)
                    act.sem_inc(go_act, 1)
                    nc.scalar.activation(ah[:, 2 * j + c, :], E_u[:, c, :], ACT.Copy).then_inc(ml_hi, 1)

            def ffn(name, before):
                norm(NORM[name], h, lambda k: act.wait_ge(lin_freed[k % 2], before + k // 2 + 1), dst=xh)
                p0, m0 = P0[name], MLP0[name]
                with act.Fori(0, 2) as r:
                    for j in range(4):
                        gated(r * 12 + (p0 + 2 * j), None, j)
                for j in range(3):
                    gated(p0 + 24 + 2 * j, None, j)

            ffn("ffn1", P0["mlp"] + 28)
            norm(NORM["mix2"], h, lambda k: act.wait_ge(lin_freed[k % 2], P0["ffn1"] + 30 + k // 2 + 1), dst=xh)
            for hf in range(2):
                st = f"da{hf}"
                for j in range(4):
                    for c in range(2):
                        evac(P0[st] + j, c, (D_Q, D_K)[j // 2][:, 2 * (j % 2) + c, :])
                for j in range(2):
                    for c in range(2):
                        p = P0[st] + 4 + j
                        tile(p, c)
                        nc.scalar.activation(D_V[:, 2 * c:2 * c + 2, j * PC:(j + 1) * PC], pl[c][:, :].rearrange("p (a n) -> p a n", a=2),
                                             ACT.Copy).then_inc(lin_freed[c], 1)
                with act.Fori(0, 4) as i:
                    units(i * 8 + U0[st], i * 4 + U0[st] // 2, causal_units())
                    act.wait_ge(at_of, i * 8 + (U0[st] + 8))
                    act.sem_inc(go_act, 1)
                    for t in range(QT):
                        op = nc.scalar.activation(D_t[:, 0, t * PART:(t + 1) * PART], D_on[:, t, :], ACT.Square, accum_out=hss[:, t:t + 1])
                    op.then_inc(fin_ss, 1)
                    act.wait_ge(fin_ss, i + (4 + 4 * hf + 1))
                    nc.scalar.activation(hstd[:], hss[:], ACT.Sqrt, bias=eps, scale=1.0 / PART).then_inc(fin_std, 1)
                    act.wait_ge(fin_g, i + (4 + 4 * hf + 1))
                    act.sem_inc(go_act, 1)
                    nc.scalar.activation(dyn(ah, i + 4 * hf), D_g, ACT.Copy).then_inc(fin_hi, 1)

            def gates(p0):
                with act.Fori(0, 4) as i:
                    for c in range(2):
                        act.wait_ge(lin_freed[c], i * 2 + p0)
                        tile(i * 2 + p0, c)
                        act.sem_inc(go_act, 1)
                        nc.scalar.activation(S_sg[:, c, :], pl[c][:, :], ACT.Sigmoid).then_inc(lin_freed[c], 1)

            gates(P0["mda"])
            p = P0["kv"]
            for a in range(2):
                tile(p, a)
                for g in range(2):
                    r = slice(g * HALF, (g + 1) * HALF)
                    nc.scalar.activation(S_x2[0:HALF, 2 * a + g, :], pl[a][r, :], ACT.Copy)
                    op = nc.scalar.activation(S_x2[HALF:PART, 2 * a + g, 0:T - 1], pl[a][r, 1:T], ACT.Copy)
                op.then_inc(lin_freed[a], 1)
            for br in range(2):
                evac(p + 1 + br, 0, S_kraw[:, br, :])
                tile(p + 1 + br, 1)
                nc.scalar.activation(S_v[:, br], pl[1][:, :].rearrange("p (a n) -> p a n", a=QT), ACT.Copy).then_inc(lin_freed[1], 1)
            for c in range(2):
                tile(p + 3, c)
                nc.scalar.activation(S_gate[:, 2 * c:2 * c + 2, :], pl[c][:, 0:96].rearrange("p (a n) -> p a n", a=2),
                                     ACT.Sigmoid).then_inc(lin_freed[c], 1)
            for a in range(2):
                for g in range(2):
                    j = 2 * a + g
                    act.wait_ge(cb_f, j + 1)
                    act.wait_ge(lin_done, 2 * (P0["cmp"] + 2 * a))
                    nc.scalar.activation(B_h[:, :, g, :], S_bf[:, g, 0:16 * NCMP].rearrange("p (j n) -> p j n", j=16), ACT.Copy).then_inc(cb_hi, 1)
                for c in range(2):
                    tile(P0["cmp"] + 2 * a + 1, c)
                    act.sem_inc(lin_freed[c], 1)
                    nc.scalar.activation(S_h1[:, a, c, :], pl[c][:, 0:2 * NCMP], ACT.Gelu_apprx_tanh).then_inc(lin_freed[c], 1)
            act.wait_ge(cb_o, 1)
            nc.scalar.activation(S_kc, po[0][:, 0:2 * NCMP], ACT.Copy).then_inc(cb_k, 1)
            act.wait_ge(cb_o, 2)
            nc.scalar.activation(S_vc[0:NCMP].rearrange("p g n -> p (g n)"), po[1][0:NCMP, 0:2 * HALF], ACT.Copy).then_inc(cb_k, 1)
            for g in range(2):
                st = f"ns{g}"
                for j in range(2):
                    for c in range(2):
                        if j == 0 and c == 0 and g:
                            act.wait_ge(fin_t, F0[st])
                        evac(P0[f"nq{g}"] + j, c, S_Q[:, 2 * j + c, :])
                with act.Fori(0, 4) as i:
                    units(i * 24 + U0[st], i * 12 + U0[st] // 2, [dict(nk=NCMP, w=NCMP, nb=1) for _ in range(2 * QT)] + causal_units(4))
                    finish(i + F0[st], 0, dyn(ah, i + 4 * g))
            gates(P0["mnsa"])
            act.wait_ge(lin_done, 2 * P0["wout2"])
            for k in range(KT):
                act.wait_ge(mg_t, 2 + k + 1)
                nc.scalar.activation(ah[:, k, :], S_mg[:, k, :], ACT.Copy).then_inc(mg_hi, 1)
            ffn("ffn2", P0["wout2"])
            norm(NORM["final"], h, lambda k: act.wait_ge(lin_freed[k % 2], P0["ffn2"] + 30 + k // 2 + 1))
            for g in range(2 * QT):
                act.wait_ge(out_t, g + 1)
                nc.scalar.activation(O_nat[:, g // 2, (g % 2) * 512:(g % 2 + 1) * 512], pt[g % 2][:, :], ACT.Copy).then_inc(out_c, 1)

        @block.vector
        def _(dve):
            dve.sem_inc(at_m, UINIT)
            dve.sem_inc(at_r, UINIT)
            dve.sem_inc(at_of, UINIT)
            dve.sem_inc(at_pt[0], UINIT // 2)
            dve.sem_inc(fin_read, FINIT)
            dve.sem_inc(ml_u, 2)
            dve.sem_inc(ml_lo, 2)
            dve.sem_inc(mg_t, 2)
            causal = c_("causal", T)

            def dyn(buf, e):
                return buf[:, bass.ds(e, 1), :].rearrange("p a n -> p (a n)")

            def tile(p, c):
                dve.wait_ge(lin_done, p * 2 + (c + 1))

            def low(dst, full, hi, done):
                nc.vector.tensor_tensor(dst, full, hi.bitcast(F32), ALU.subtract).then_inc(done, 1)

            def norm(call, name, src, n=T, dst=None):
                dve.wait_ge(nm_std, call + 1)
                nc.vector.reciprocal(N_rs[:, 0:n], N_std[:, 0:n]).then_inc(nm_rs, 1)
                dve.wait_ge(nm_rs, call + 1)
                for k in range(KT):
                    o = F_out[:, k, 0:n] if dst is None else N_xn[:, k % 2, 0:n]
                    if dst is not None and k >= 2:
                        dve.wait_ge(nm_lo, 8 * call + k - 1)
                    nc.vector.scalar_tensor_tensor(o, src[:, k, 0:n], gcol(name, k), N_rs[:, 0:n], ALU.mult, ALU.mult).then_inc(nm_xn, 1)
                    if dst is not None and k:
                        norm_low(call, k - 1, n, dst)
                if dst is not None:
                    norm_low(call, KT - 1, n, dst)

            def norm_low(call, k, n, dst):
                dve.wait_ge(nm_hi, 8 * call + k + 1)
                low(dst[1][:, k, 0:n], N_xn[:, k % 2, 0:n], dst[0][:, k, 0:n], nm_lo)

            def residual(p0, n, scale=1.0):
                with dve.Fori(0, n // 2) as i:
                    for j in range(2):
                        for c in range(2):
                            add(i * 2 + (p0 + j), c, dyn(h, i * 4 + (2 * j + c)), scale)

            def add(p, c, hk, scale):
                tile(p, c)
                if scale == 1.0:
                    nc.vector.tensor_tensor(hk, pl[c][:, :], hk, ALU.add).then_inc(lin_freed[c], 1)
                else:
                    nc.vector.scalar_tensor_tensor(hk, pl[c][:, :], scale, hk, ALU.mult, ALU.add).then_inc(lin_freed[c], 1)

            def units(U, Uh, us, out):
                n = len(us)
                for s in range(n + 3):
                    if s < n:
                        nk = us[s]["nk"]
                        dve.wait_ge(at_s, U + (s + 1))
                        dve.wait_ge(at_p, U + (s - 1))
                        dve.sem_inc(go_dve, 1)
                        nc.vector.tensor_tensor_reduce(out=SM[:, s % 2, 0:nk], in0=ps[s % 2][:, 0:nk], in1=us[s]["mask"], scale=us[s]["scale"],
                                                       scalar=BIG, op0=ALU.add, op1=ALU.min, accum_out=negm[:, s:s + 1]).then_inc(at_m, 1)
                    j = s - 2
                    if 0 <= j < n and j % 2 == 0:
                        w, nb = us[j]["w"], us[j]["nb"]
                        dve.wait_ge(at_t, U + (j + 1))
                        dve.wait_ge(at_o, U + (j - 1))
                        dve.sem_inc(go_dve, 1)
                        nc.vector.tensor_copy(PTs[0:w, 0, 0:nb * PART], pt[0][0:w, 0:nb * PART]).then_inc(at_pt[0], 1)
                    if s >= 3:
                        j = s - 3
                        dve.wait_ge(at_o, U + (j + 1))
                        dve.sem_inc(go_dve, 1)
                        nc.vector.reciprocal(rinv[:, j:j + 1], rsum[:, j:j + 1]).then_inc(at_r, 1)
                        dve.wait_ge(at_r, U + (j + 1))
                        out(j)

            def causal_units(n=2, scale=-float(HALF) ** -0.5):
                return [dict(nk=(t + 1) * PART, w=PART, nb=t + 1, mask=causal[:, T - (t + 1) * PART:], scale=scale) for _ in range(n) for t in range(QT)]

            def finish(F, f, dst_h, dst_l):
                dve.wait_ge(fin_hi, F + 1)
                low(dst_l, pl[f][:, :], dst_h, fin_read)

            dve.wait_ge(ld_late, 16 * 3)
            for a in range(2):
                nc.vector.tensor_tensor_reduce(out=lp_in[0:1, 2 * a, :], in0=lp_in[0:1, 2 * a, :], in1=lp_in[0:1, 2 * a + 1, :], scale=1.0,
                                               scalar=0.0, op0=ALU.mult, op1=ALU.add, accum_out=lam[0:1, a:a + 1]).then_inc(lam_s, 1)
            dve.wait_ge(lam_s, 3)
            nc.vector.tensor_tensor(lam[0:1, 2:3], lam[0:1, 0:1], lam[0:1, 1:2], ALU.subtract).then_inc(lam_s, 1)
            dve.wait_ge(lam_s, 4)
            nc.vector.tensor_scalar(lam[0:1, 2:3], lam[0:1, 2:3], -1.0, -LAM_INIT, ALU.mult, ALU.add).then_inc(lam_s, 1)
            dve.wait_ge(lam_p, 1)
            nc.vector.tensor_copy(lam[:, 3:4], ps[0][:, 0:1]).then_inc(lam_d, 1)
            norm(NORM["mix"], "norm_mix_g", h, dst=(xh, xl))

            for j in range(8):
                dve.wait_ge(hn_std, j + 1)
                if j >= 2:
                    dve.wait_ge(hn_out, j - 1)
                nc.vector.reciprocal(H_rs[:, j % 2, :], H_std[:, j % 2, :]).then_inc(hn_rs, 1)
                dve.wait_ge(hn_rs, j + 1)
                nc.vector.scalar_tensor_tensor(X_qk[:, j, :], X_qk[:, j, :], gcol("fox_q_norm_g" if j < 4 else "fox_k_norm_g", 0), H_rs[:, j % 2, :],
                                               ALU.mult, ALU.mult).then_inc(hn_out, 1)
            dve.wait_ge(ls_a, 3)
            nc.vector.scalar_tensor_tensor(X_z[0:8, :], X_z[0:8, :], 0.0, X_e[0:8, :], ALU.min, ALU.subtract).then_inc(ls_v, 1)
            dve.wait_ge(ls_v, 1)
            nc.vector.tensor_tensor_scan(X_c[0:8, :], c_("ones", T, 8), X_z[0:8, :], 0.0, ALU.mult, ALU.add).then_inc(ls_v, 1)
            dve.wait_ge(ls_v, 2)
            for a in range(2):
                nc.vector.tensor_copy(X_k[HALF:HALF + 8, a, :], X_c[0:8, :]).then_inc(ls_v, 1)
            dve.wait_ge(hn_out, 8)
            with dve.Fori(0, 4) as i:
                dve.wait_ge(at_s, i * 8 + U0["fox"])
                dve.sem_inc(go_dve, 1)
                for a in range(2):
                    src = X_qk[a * HALF:(a + 1) * HALF, bass.ds(i, 1), :].rearrange("p a n -> p (a n)")
                    nc.vector.tensor_copy(X_q[0:HALF, a, :], src)
                    r = slice(HALF, HALF + 8)
                    pick = cst[r, bass.ds(i * 2 + (CAT["sel"] + a), 1)]
                    op = nc.vector.tensor_scalar(X_q[r, a, :], cst[r, CAT["ones"]:CAT["ones"] + T], pick, None, ALU.mult)
                op.then_inc(at_st, 1)

                U = i * 8 + U0["fox"]

                def out_fox(j):
                    a, t = j // QT, j % QT
                    nc.vector.tensor_scalar(X_on[:, t, a * HALF:(a + 1) * HALF], po[j % 2][:, 0:HALF], rinv[:, j:j + 1], None, ALU.mult).then_inc(at_of, 1)

                units(U, i * 4 + U0["fox"] // 2, causal_units(), out_fox)
                finish(i + F0["fox"], 0, dyn(ah, i), dyn(al, i))

            nc.vector.memset(G_S, 0.0).then_inc(gl_s, 1)
            dve.wait_ge(ls_a, 8)
            nc.vector.scalar_tensor_tensor(G_z, G_z, 0.0, G_e, ALU.min, ALU.subtract).then_inc(ls_v, 1)
            dve.wait_ge(ls_v, 5)
            for a in range(2):
                nc.vector.tensor_tensor_scan(G_b[:, a, :], c_("chunk", T), G_z[:, a, :], 0.0, ALU.mult, ALU.add).then_inc(ls_v, 1)
            dve.wait_ge(ls_v, 7)
            chunks = G_b.rearrange("p a (n c) -> p (a n) c", c=HALF)
            nc.vector.tensor_tensor(G_z.rearrange("p a (n c) -> p (a n) c", c=HALF), chunks[:, :, HALF - 1:HALF].to_broadcast([PART, 2 * T // HALF, HALF]),
                                    chunks, ALU.subtract).then_inc(ls_v, 1)
            for c in range(2):
                dve.wait_ge(lin_freed[c], P0["gqk"] + 1)
            dve.wait_ge(ls_a, 9)
            nc.vector.scalar_tensor_tensor(G_qk[:, 0:2, :], G_qk[:, 0:2, :], float(HALF) ** -0.5, G_e, ALU.mult, ALU.mult).then_inc(ls_v, 1)
            for c in range(2):
                dve.wait_ge(lin_freed[c], P0["gqk"] + 2)
            dve.wait_ge(ls_a, 11)
            nc.vector.tensor_tensor(G_ke, G_ke, G_qk[:, 2:4, :], ALU.mult).then_inc(ls_v, 1)
            dve.wait_ge(ls_a, 12)
            dve.wait_ge(ls_v, 10)
            nc.vector.tensor_tensor(G_qk[:, 2:4, :], G_qk[:, 2:4, :], G_e, ALU.mult).then_inc(ls_v, 1)
            dve.wait_ge(ls_v, 11)
            for c in range(2):
                dve.wait_ge(lin_freed[c], P0["wout"])
            with dve.Fori(0, QT) as i:
                dve.wait_ge(gl_i, i * 2 + 2)
                dve.sem_inc(go_dve, 1)
                tok = bass.ds(i * PART, PART)
                nc.vector.tensor_copy(G_qs, G_qk[:, 0:2, tok])
                nc.vector.tensor_copy(G_ks, G_qk[:, 2:4, tok])
                nc.vector.tensor_copy(G_es, G_ke[:, :, tok]).then_inc(gl_st, 1)
                dve.wait_ge(gl_kt, i + 1)
                dve.sem_inc(go_dve, 1)
                nc.vector.tensor_copy(G_kn.rearrange("p a n -> p (a n)"), pt[0][:, 0:2 * PART]).then_inc(gl_kn, 1)
                dve.wait_ge(gl_a, i + 1)
                dve.sem_inc(go_dve, 1)
                for b in range(2):
                    op = nc.vector.tensor_tensor(G_at[:, b], ps[b][:, 0:2 * HALF].rearrange("p (a n) -> p a n", a=2),
                                                 c_("tril", HALF).unsqueeze(1).to_broadcast([PART, 2, HALF]), ALU.mult)
                op.then_inc(gl_at, 1)
                for c in range(2):
                    dve.wait_ge(gl_i, i * 2 + (3 + c))
                    dve.wait_ge(gl_s, i * 2 + (c + 1))
                    dve.sem_inc(go_dve, 1)
                    for a in range(2):
                        dec = G_dec[:, a, bass.ds(i * 2 + c, 1)]
                        op = nc.vector.scalar_tensor_tensor(G_S[:, a, :], G_S[:, a, :], dec, ps[c][:, 256 + a * PART:256 + (a + 1) * PART], ALU.mult, ALU.add)
                    op.then_inc(gl_s, 1)
                dve.wait_ge(gl_on, i + 1)
                dve.sem_inc(go_dve, 1)
                for b in range(2):
                    o = G_on.rearrange("p (a b) n -> p b a n", b=2)[:, b]
                    op = nc.vector.tensor_tensor(o, po[b][:, 0:2 * PART].rearrange("p (a n) -> p a n", a=2), o, ALU.add)
                op.then_inc(gl_oi, 1)
                dve.wait_ge(fin_std, i + 1)
                dve.sem_inc(go_dve, 1)
                nc.vector.reciprocal(hinv[:], hstd[:]).then_inc(fin_n, 1)
                dve.wait_ge(fin_n, i + 1)
                for hd in range(4):
                    op = nc.vector.tensor_scalar(G_on[:, hd, :], G_on[:, hd, :], hinv[:, hd:hd + 1], None, ALU.mult)
                op.then_inc(fin_rs, 1)
                dve.wait_ge(fin_t, i + (F0["gla"] + 1))
                dve.sem_inc(go_dve, 1)
                for hd in range(4):
                    op = nc.vector.scalar_tensor_tensor(G_t[:, hd, :], pl[0][:, hd * PART:(hd + 1) * PART], gcol("gla_out_norm_g", hd),
                                                        G_r[:, hd, tok], ALU.mult, ALU.mult)
                op.then_inc(fin_g, 1)
                dve.wait_ge(fin_hi, i + (F0["gla"] + 1))
                low(al[:, 4:8, tok], G_t, ah[:, 4:8, tok], fin_read)
            residual(P0["wout"], 4)

            norm(NORM["mem"], "norm_mem_g", memT, n=M, dst=(ah, al))
            norm(NORM["xattn"], "norm_xattn_g", h, dst=(xh, xl))
            for j in range(8, 16):
                n, buf, g = (M, C_K, "xattn_k_norm_g") if j < 12 else (T, C_Q, "xattn_q_norm_g")
                dve.wait_ge(hn_std, j + 1)
                dve.wait_ge(hn_out, j - 1)
                nc.vector.reciprocal(C_rs[:, j % 2, 0:n], C_std[:, j % 2, 0:n]).then_inc(hn_rs, 1)
                dve.wait_ge(hn_rs, j + 1)
                for c in range(2):
                    k = 2 * (j % 4) + c
                    op = nc.vector.scalar_tensor_tensor(buf[:, k, :], buf[:, k, :], gcol(g, c), C_rs[:, j % 2, 0:n], ALU.mult, ALU.mult)
                op.then_inc(hn_out, 1)
            dve.wait_ge(hn_out, 16)
            with dve.Fori(0, 4) as i:
                dve.wait_ge(at_s, i * 4 + U0["xa"])
                dve.sem_inc(go_dve, 1)
                nc.vector.tensor_copy(C_q, C_Q[:, bass.ds(i * 2, 2), :]).then_inc(at_st, 1)

                def out_xa(j):
                    nc.vector.tensor_scalar(C_on[:, j, :], po[j % 2][:, 0:M], rinv[:, j:j + 1], None, ALU.mult).then_inc(at_of, 1)

                units(i * 4 + U0["xa"], i * 2 + U0["xa"] // 2,
                      [dict(nk=M, w=PART, nb=2, mask=causal[:, 0:M], scale=-float(M) ** -0.5) for _ in range(QT)], out_xa)
                for f in range(2):
                    finish(i * 2 + (F0["xa"] + f), f, dyn(ah, i * 2 + f), dyn(al, i * 2 + f))
            residual(P0["xo"], 4)

            norm(NORM["mlp"], "norm_mlp_g", h, dst=(xh, xl))
            with dve.Fori(0, D_FF // D) as r:
                for j in range(4):
                    for c in range(2):
                        k = 2 * j + c
                        m = r * 8 + (MLP0["mlp"] + k)
                        dve.wait_ge(lin_freed[c], r * 8 + (P0["mlp"] + j + 1))
                        dve.wait_ge(ml_lo, m - 1)
                        dve.sem_inc(go_dve, 1)
                        nc.vector.tensor_tensor(E_u[:, c, :], E_t[:, c, :], E_t[:, c, :], ALU.mult).then_inc(ml_u, 1)
                        dve.wait_ge(ml_hi, m + 1)
                        low(al[:, k, :], E_u[:, c, :], ah[:, k, :], ml_lo)
                for j in range(4):
                    for c in range(2):
                        add(r * 8 + (P0["mlp"] + 4 + j), c, h[:, 2 * j + c, :], 1.0)

            def gated(p, m, j):
                for c in range(2):
                    dve.wait_ge(lin_freed[c], p + 1)
                    dve.wait_ge(ml_lo, m)
                    tile(p + 1, c)
                    dve.sem_inc(go_dve, 1)
                    nc.vector.tensor_tensor(E_u[:, c, :], pl[c][:, :], E_t[:, c, :], ALU.mult).then_inc(lin_freed[c], 1)
                for c in range(2):
                    dve.wait_ge(ml_hi, m + (c + 1))
                    low(al[:, 2 * j + c, :], E_u[:, c, :], ah[:, 2 * j + c, :], ml_lo)

            def ffn(name, gain):
                norm(NORM[name], gain, h, dst=(xh, xl))
                p0, m0 = P0[name], MLP0[name]
                with dve.Fori(0, 2) as r:
                    for j in range(4):
                        gated(r * 12 + (p0 + 2 * j), r * 8 + (m0 + 2 * j), j)
                    for j in range(4):
                        for c in range(2):
                            add(r * 12 + (p0 + 8 + j), c, h[:, 2 * j + c, :], 0.5)
                for j in range(3):
                    gated(p0 + 24 + 2 * j, m0 + 16 + 2 * j, j)
                for j in range(4):
                    for c in range(2):
                        add(p0 + 30 + j, c, h[:, 2 * j + c, :], 0.5)

            ffn("ffn1", "ffn1_norm_2")
            norm(NORM["mix2"], "mix_norm_2", h, dst=(xh, xl))
            cos, sin = c_("cos", T), c_("sin", T)
            for hf in range(2):
                st = f"da{hf}"
                for c in range(2):
                    dve.wait_ge(lin_freed[c], P0[st] + 4)
                with dve.Fori(0, 4) as i:
                    dve.wait_ge(at_s, i * 8 + U0[st])
                    dve.sem_inc(go_dve, 1)
                    for dst, src in ((D_q, D_Q), (D_k, D_K)):
                        nc.vector.tensor_tensor(dst, dyn(src, i), cos, ALU.mult)
                    dve.wait_ge(rp_t, i * 2 + (R0[st] + 2))
                    dve.sem_inc(go_dve, 1)
                    for a in range(2):
                        op = nc.vector.tensor_tensor(D_t[:, a, :], pl[a][:, :], sin, ALU.mult)
                    op.then_inc(rp_a, 1)
                    dve.wait_ge(rp_a, i + (RA0[st] + 1))
                    for a, dst in enumerate((D_q, D_k)):
                        op = nc.vector.tensor_tensor(dst, dst, D_t[:, a, :], ALU.add)
                    op.then_inc(at_st, 1)
                    U = i * 8 + U0[st]

                    def out_da(j):
                        a, t = j // QT, j % QT
                        if a == 0:
                            nc.vector.tensor_scalar(D_on[:, t, :], po[j % 2][:, 0:PART], rinv[:, j:j + 1], None, ALU.mult).then_inc(at_of, 1)
                            return
                        nc.vector.tensor_tensor(coef[:, j:j + 1], rinv[:, j:j + 1], lam[:, 3:4], ALU.mult).then_inc(at_cf, 1)
                        dve.wait_ge(at_cf, i * 4 + (CF0[st] + t + 1))
                        dve.sem_inc(go_dve, 1)
                        nc.vector.scalar_tensor_tensor(D_on[:, t, :], po[j % 2][:, 0:PART], coef[:, j:j + 1], D_on[:, t, :], ALU.mult, ALU.add).then_inc(at_of, 1)

                    units(U, i * 4 + U0[st] // 2, causal_units(), out_da)
                    dve.wait_ge(fin_std, i + (4 + 4 * hf + 1))
                    dve.sem_inc(go_dve, 1)
                    nc.vector.reciprocal(hinv[:], hstd[:]).then_inc(fin_n, 1)
                    dve.wait_ge(fin_n, i + (4 + 4 * hf + 1))
                    for t in range(QT):
                        op = nc.vector.tensor_scalar(D_on[:, t, :], D_on[:, t, :], hinv[:, t:t + 1], None, ALU.mult)
                    op.then_inc(fin_rs, 1)
                    dve.wait_ge(fin_t, i + (F0[st] + 1))
                    dve.sem_inc(go_dve, 1)
                    gain = gT[:, bass.ds(i + (ROWS["da_head_norm_2"] + 4 * hf), 1)]
                    nc.vector.tensor_scalar(D_g, pl[0][:, :], gain, 1.0 - LAM_INIT, ALU.mult, ALU.mult).then_inc(fin_g, 1)
                    dve.wait_ge(fin_hi, i + (F0[st] + 1))
                    low(dyn(al, i + 4 * hf), D_g, dyn(ah, i + 4 * hf), fin_read)

            def merge(p0, adds):
                with dve.Fori(0, 4) as i:
                    for c in range(2):
                        p = i * 2 + (p0 + 1)
                        dve.wait_ge(lin_freed[c], p)
                        tile(p, c)
                        mg = dyn(S_mg, i * 2 + c)
                        if adds:
                            dve.wait_ge(mg_t, i * 2 + (c + 1))
                        dve.sem_inc(go_dve, 1)
                        nc.vector.tensor_tensor(SM[:, c, :] if adds else mg, pl[c][:, :], S_sg[:, c, :], ALU.mult).then_inc(lin_freed[c], 1)
                        if adds:
                            dve.wait_ge(lin_freed[c], p + 1)
                            nc.vector.tensor_tensor(mg, mg, SM[:, c, :], ALU.add).then_inc(mg_t, 1)

            merge(P0["mda"], False)

            p = P0["kv"]
            parts = (S_t, S_q)
            for br in range(2):
                dve.wait_ge(lin_freed[0], p + 2 + br)
                nc.vector.tensor_tensor(S_kr[:, br, :], S_kraw[:, br, :], cos, ALU.mult)
                dve.wait_ge(rp_t, R0["kv"] + br + 1)
                op = nc.vector.tensor_tensor(parts[br], po[br][:, :], sin, ALU.mult)
            op.then_inc(rp_a, 1)
            dve.wait_ge(rp_a, RA0["kv"] + 1)
            for br in range(2):
                op = nc.vector.tensor_tensor(S_kr[:, br, :], S_kr[:, br, :], parts[br], ALU.add)
            op.then_inc(rp_b, 1)
            dve.wait_ge(rp_b, 1)
            for br in range(2):
                for g in range(2):
                    for a in range(2):
                        op = nc.vector.tensor_copy(S_kd[a * HALF:(a + 1) * HALF, br, g, :], S_kr[g * HALF:(g + 1) * HALF, br, :])
            op.then_inc(kd, 1)
            for c in range(2):
                dve.wait_ge(lin_freed[c], p + 4)
            nc.vector.tensor_scalar(S_gate[:, 0, 0:48:3], S_gate[:, 0, 0:48:3], c_("cmpany", 1), None, ALU.mult).then_inc(zero_s, 1)
            for a in range(2):
                for g in range(2):
                    j = 2 * a + g
                    if j >= 2:
                        dve.wait_ge(cb_lo, j - 1)
                    src = bass.AP(S_x2.tensor, S_x2.offset + j * T, [list(S_x2.ap[0]), [2, 16], [CMP_S, NCMP]])
                    pos = gT[:, ROWS["cmp_pos_2"] + a * 16:ROWS["cmp_pos_2"] + (a + 1) * 16].unsqueeze(2).to_broadcast([PART, 16, NCMP])
                    bf = S_bf[:, g, 0:16 * NCMP].rearrange("p (j n) -> p j n", j=16)
                    nc.vector.tensor_tensor(bf, src, pos, ALU.add).then_inc(cb_f, 1)
                    dve.wait_ge(cb_hi, j + 1)
                    low(B_l[:, :, g, :], bf, B_h[:, :, g, :], cb_lo)
            dve.wait_ge(zero_s, 1)
            for g in range(2):
                st = f"ns{g}"
                for c in range(2):
                    dve.wait_ge(lin_freed[c], P0[f"nq{g}"] + 2)
                with dve.Fori(0, 4) as i:
                    dve.wait_ge(at_s, i * 24 + U0[st])
                    dve.sem_inc(go_dve, 1)
                    nc.vector.tensor_copy(S_qr, dyn(S_Q, i))
                    nc.vector.tensor_tensor(S_q, dyn(S_Q, i), cos, ALU.mult)
                    dve.wait_ge(rp_t, i + (R0[st] + 1))
                    dve.sem_inc(go_dve, 1)
                    nc.vector.tensor_tensor(S_t, pl[1][:, :], sin, ALU.mult).then_inc(rp_a, 1)
                    dve.wait_ge(rp_a, i + (RA0[st] + 1))
                    nc.vector.tensor_tensor(S_q, S_q, S_t, ALU.add)
                    nc.vector.tensor_copy(S_gs, S_gate[:, :, bass.ds(i * 6 + 24 * g, 6)]).then_inc(at_st, 1)
                    dve.wait_ge(at_st, i + (A0[st] + 1))
                    dve.sem_inc(go_dve, 1)
                    U = i * 24 + U0[st]

                    def out_ns(j):
                        br, a, t = j // 8, j % 8 // QT, j % QT
                        o = S_on[:, t, a * HALF:(a + 1) * HALF]
                        gate = S_gs[:, t, 3 * a + br:3 * a + br + 1]
                        nc.vector.tensor_tensor(coef[:, j:j + 1], rinv[:, j:j + 1], gate, ALU.mult).then_inc(at_cf, 1)
                        dve.wait_ge(at_cf, i * 24 + (CF0[st] + j + 1))
                        dve.sem_inc(go_dve, 1)
                        if br == 0:
                            nc.vector.tensor_scalar(o, po[j % 2][:, 0:HALF], coef[:, j:j + 1], None, ALU.mult).then_inc(at_of, 1)
                        else:
                            nc.vector.scalar_tensor_tensor(o, po[j % 2][:, 0:HALF], coef[:, j:j + 1], o, ALU.mult, ALU.add).then_inc(at_of, 1)

                    cmpm = c_("cmpmask", QT * NCMP)
                    us = [dict(nk=NCMP, w=NCMP, nb=1, mask=cmpm[:, t * NCMP:(t + 1) * NCMP], scale=-float(HALF) ** -0.5) for _ in range(2) for t in range(QT)]
                    units(U, i * 12 + U0[st] // 2, us + causal_units(4), out_ns)
                    finish(i + F0[st], 0, dyn(ah, i + 4 * g), dyn(al, i + 4 * g))
            merge(P0["mnsa"], True)
            for k in range(KT):
                dve.wait_ge(mg_hi, k + 1)
                low(al[:, k, :], S_mg[:, k, :], ah[:, k, :], mg_lo)
            residual(P0["wout2"], 4)
            ffn("ffn2", "ffn2_norm_2")
            norm(NORM["final"], "final_norm_2", h)
    return nc


_INS = ["x", "mem", "norm_mix_g", "w_in", "fox_b_f", "fox_q_norm_g", "fox_k_norm_g", "gla_w_gate2", "gla_b_gate", "gla_out_norm_g", "w_out",
        "norm_xattn_g", "norm_mem_g", "xattn_wq", "xattn_wkv", "xattn_q_norm_g", "xattn_k_norm_g", "xattn_wo", "norm_mlp_g", "mlp_w1", "mlp_w2",
        "ffn1_norm_2", "ffn1_w1_2", "ffn1_w3_2", "ffn1_w2_2", "mix_norm_2", "w_in_2", "da_lambda_2", "da_head_norm_2", "cmp_pos_2", "cmp_w1_2",
        "cmp_w2_2", "w_proj_da_2", "w_proj_nsa_2", "w_out_2", "ffn2_norm_2", "ffn2_w1_2", "ffn2_w3_2", "ffn2_w2_2", "final_norm_2"]


def kernel(**inputs):
    import concourse.bacc as _bacc
    from concourse.bass_utils import run_bass_kernel_spmd as _run

    nc = _bacc.Bacc("TRN2", target_bir_lowering=False, num_devices=1)
    arrays, d = {}, {}
    for name in _INS + ["consts"]:
        a = CONSTS if name == "consts" else np.ascontiguousarray(inputs[name])
        arrays[f"in_{name}_dram"] = a
        d[name] = nc.dram_tensor(f"in_{name}_dram", a.shape, mybir.dt.from_np(a.dtype), kind="ExternalInput").ap()
    out = nc.dram_tensor("out_0_dram", (1, T, D), F32, kind="ExternalOutput").ap()
    build(nc, d, out)
    r = _run(nc, [arrays], core_ids=[0])
    return r.results[0]["out_0_dram"]
```

```python
from contextlib import ExitStack
import numpy as np
import concourse.bass as bass
from concourse import mybir

ALU = mybir.AluOpType
ACT = mybir.ActivationFunctionType
F32 = mybir.dt.float32
F32R = mybir.dt.float32r
AX = mybir.AxisListType

PART = 128
T, M, D = 512, 256, 1024
KT = D // PART
PC = 256
QT = T // PART
HALF = 64
D_FF, D_FF2 = 4096, 2816
CMP_L, CMP_S = 32, 16
NCMP = (T - CMP_L) // CMP_S + 1
EPS = 1e-6
NEG = -1e30
BIG = 3e38
LAM_INIT = 0.8 - 0.6
FOX, GLA_KW, GLA_VW = 512, 256, 512

W1_COL, at = {}, 0
for name_, width_ in (("fq", 512), ("fk", 512), ("fv", 512), ("ff", 8), ("gqk", 512), ("gv", 512), ("glr", 16), ("gr", 512)):
    W1_COL[name_] = at
    at += width_
W2_COL, at = {}, 0
for name_, width_ in (("q", 1024), ("k", 1024), ("v", 1024), ("nq", 1024), ("kv", 768), ("gate", 48), ("ga", 1024), ("gb", 1024)):
    W2_COL[name_] = at
    at += width_

P0, at = {}, 0
for name_, count_ in (("small", 1), ("fqk", 4), ("fv", 2), ("gqk", 2), ("gv", 2), ("gr", 2), ("wout", 4),
                      ("xk", 4), ("xq", 4), ("xv", 4), ("xo", 4), ("mlp", 32), ("ffn1", 34),
                      ("da", 12), ("mda", 8), ("kv", 4), ("cmp", 4), ("nq", 4),
                      ("mnsa", 8), ("wout2", 4), ("ffn2", 34)):
    P0[name_] = at
    at += count_
PANELS = at

ROWS, at = {}, 0
for name_, count_ in (("norm_mix_g", 8), ("norm_xattn_g", 8), ("norm_mem_g", 8), ("norm_mlp_g", 8),
                      ("ffn1_norm_2", 8), ("mix_norm_2", 8), ("ffn2_norm_2", 8), ("final_norm_2", 8),
                      ("gla_out_norm_g", 4), ("da_head_norm_2", 8), ("gla_b_gate", 2), ("xattn_q_norm_g", 2),
                      ("xattn_k_norm_g", 2), ("fox_q_norm_g", 1), ("fox_k_norm_g", 1), ("cmp_pos_2", 32)):
    ROWS[name_] = at
    at += count_
NROWS = at

CAUSAL_GROUPS = []
for pair_ in range(2):
    CAUSAL_GROUPS += [[(pair_, a_, 3, 0)] for a_ in range(2)]
    CAUSAL_GROUPS += [[(pair_, a_, 2, 0), (pair_, a_, 0, 3 * PART)] for a_ in range(2)]
CAUSAL_GROUPS += [[(0, a_, 1, 0), (1, a_, 1, 2 * PART)] for a_ in range(2)]
NG, NG_XA, NG_NS = len(CAUSAL_GROUPS), 4, 2 + 2 * len(CAUSAL_GROUPS)
CKEY = 32
UINIT = 8
U0 = {"fox": UINIT}
U0["xa"] = U0["fox"] + 2 * NG
U0["da"] = U0["xa"] + 2 * NG_XA
U0["ns"] = U0["da"] + 4 * NG
FINIT = 4
F0 = {"fox": FINIT, "gla": FINIT + 4, "xa": FINIT + 8, "da": FINIT + 16, "ns": FINIT + 24, "end": FINIT + 32}
A0 = {"fox": 0, "xa": 2, "da": 4, "ns": 8}
R0 = {"da": 0, "kv": 16, "ns": 18}
RA0 = {"da": 0, "kv": 16, "ns": 17}
CF0 = {"da": 0, "ns": 20}
MLP0 = {"mlp": 2, "ffn1": 2 + 32, "ffn2": 2 + 32 + 22}
NORM = {"mix": 0, "mem": 1, "xattn": 2, "mlp": 3, "ffn1": 4, "mix2": 5, "ffn2": 6, "final": 7}


def constants():
    p = np.arange(PART)
    parts, where, at = [], {}, 0

    def put(name, a):
        nonlocal at
        a = np.asarray(a, np.float32).reshape(PART, -1)
        where[name] = at
        at += a.shape[1]
        parts.append(a)

    put("ident", np.eye(PART))
    wide = np.zeros((PART, T))
    wide[:, T - PART:] = np.where(p[None, :] <= p[:, None], 0.0, NEG)
    put("causal", wide)
    t = np.arange(T).reshape(QT, PART)
    valid = (np.arange(NCMP) * CMP_S + CMP_L - 1)[None, None, :] <= t[:, :, None]
    cmask = np.full((PART, QT, 2, CKEY), NEG)
    cmask[..., :NCMP] = np.where(valid, 0.0, NEG).transpose(1, 0, 2)[:, :, None, :]
    put("cmpmask", cmask)
    put("cmpany", (valid.any(-1)).astype(np.float32).T)
    put("tril", (p[:, None] % HALF) <= np.arange(HALF)[None, :])
    put("chunk", np.tile(np.arange(T)[None, :] % HALF != 0, (PART, 1)))
    put("ones", np.ones((PART, T)))
    put("block", (p[:, None] // HALF) == (p[None, :] // HALF))
    rot = np.zeros((PART, PART))
    for o in range(PART):
        if o % HALF < HALF // 2:
            rot[o + HALF // 2, o] = -1.0
        else:
            rot[o - HALF // 2, o] = 1.0
    put("rot", rot)
    inv = (np.float32(1.0) / (np.float32(10000.0) ** (np.arange(0, HALF, 2, dtype=np.float32) / np.float32(HALF)))).astype(np.float32)
    ang = (np.arange(T, dtype=np.float32)[:, None] * inv[None, :]).astype(np.float32)
    put("cos", np.cos(ang).T[p % (HALF // 2)])
    put("sin", np.sin(ang).T[p % (HALF // 2)])
    sel = np.zeros((PART, 8))
    sel[HALF + np.arange(8), np.arange(8)] = -float(HALF) ** 0.5
    put("sel", sel)
    put("eps", np.full((PART, 1), EPS))
    put("one", np.ones((PART, 1)))
    return np.ascontiguousarray(np.concatenate(parts, axis=1)), where


CONSTS, CAT = constants()
N_ROW_LOADS = len(ROWS) + 2


def build(nc, d, out):
    ctx = ExitStack()
    with ctx:
        def sb(name, shape, dt=F32):
            return ctx.enter_context(nc.sbuf_tensor(name, shape, dt))

        def sem(name):
            return ctx.enter_context(nc.semaphore(name))

        h = sb("h", [PART, KT, T])
        xh = sb("xh", [PART, KT, T], F32R)
        xl = sb("xl", [PART, KT, T], F32R)
        ah = sb("ah", [PART, KT, T], F32R)
        al = sb("al", [PART, KT, T], F32R)
        raw = sb("raw", [PART, 2, KT, PC])
        wh = sb("wh", [PART, 2, KT, PC], F32R)
        wl = sb("wl", [PART, 2, KT, PC], F32R)
        cst = sb("cst", [PART, CONSTS.shape[1]])
        gT = sb("gT", [PART, NROWS])
        foxb = sb("foxb", [8, 1])
        lam = sb("lam", [PART, 4])
        gate2 = sb("gate2", [16, GLA_KW])
        negm = sb("negm", [PART, 48])
        rsum = sb("rsum", [PART, 48])
        rinv = sb("rinv", [PART, 48])
        coef = sb("coef", [PART, 48])
        hss = sb("hss", [PART, 16])
        hstd = sb("hstd", [PART, 16])
        hinv = sb("hinv", [PART, 16])
        AW = 16512
        arena = sb("arena", [PART, AW])

        class Arena:
            def __init__(self, at=0):
                self.at = at

            def __call__(self, *shape):
                n = int(np.prod(shape))
                assert self.at + n <= AW, (self.at, n)
                v = arena[:, self.at:self.at + n]
                self.at += n
                if len(shape) == 2:
                    v = v.rearrange("p (a b) -> p a b", a=shape[0])
                elif len(shape) == 3:
                    v = v.rearrange("p (a b c) -> p a b c", a=shape[0], b=shape[1])
                return v

        memT = arena[:, AW - KT * M:].rearrange("p (k t) -> p k t", k=KT)

        def bank(name):
            return ctx.enter_context(nc.psum_tensor(name, [PART, 512], F32))

        pl = [bank("lin0"), bank("lin1")]
        ps = [bank("score0"), bank("score1")]
        pt = [bank("turned0"), bank("turned1")]
        po = [bank("mix0"), bank("mix1")]

        def c_(name, n, rows=PART):
            return cst[0:rows, CAT[name]:CAT[name] + n]

        ident = c_("ident", PART)
        ones = c_("ones", PART)
        eps = c_("eps", 1)

        def gcol(name, k):
            return gT[:, ROWS[name] + k:ROWS[name] + k + 1]

        ld_const, ld_rows, ld_x, ld_mem, ld_late = sem("ld_const"), sem("ld_rows"), sem("ld_x"), sem("ld_mem"), sem("ld_late")
        raw_in = [sem("raw_in0"), sem("raw_in1")]
        hi_done, conv_done = sem("hi_done"), sem("conv_done")
        lin_done = sem("lin_done")
        lin_freed = [sem("lin_freed0"), sem("lin_freed1")]
        st_t, st_c = sem("st_t"), sem("st_c")
        nm_sq, nm_ac, nm_mm, nm_std, nm_rs, nm_xn, nm_hi, nm_lo = (sem("nm_" + n) for n in ("sq", "ac", "mm", "std", "rs", "xn", "hi", "lo"))
        hn_mm, hn_std, hn_rs, hn_out = (sem("hn_" + n) for n in ("mm", "std", "rs", "out"))
        ls_a, ls_v = sem("ls_a"), sem("ls_v")
        at_st, at_ks = sem("at_st"), sem("at_ks")
        at_s, at_m, at_p, at_t, at_pt, at_o, at_r, at_cf, at_of = (sem("at_" + n) for n in ("s", "m", "p", "t", "pt", "o", "r", "cf", "of"))
        cs_a, cs_m, cs_s = sem("cs_a"), sem("cs_m"), sem("cs_s")
        fin_n, fin_ss, fin_std, fin_rs = sem("fin_n"), sem("fin_ss"), sem("fin_std"), sem("fin_rs")
        fin_t, fin_g, fin_hi, fin_read = sem("fin_t"), sem("fin_g"), sem("fin_hi"), sem("fin_read")
        rp_t, rp_a, rp_b = sem("rp_t"), sem("rp_a"), sem("rp_b")
        gl_g, gl_st, gl_v, gl_kt, gl_kn, gl_a, gl_at, gl_i, gl_s, gl_oi, gl_on, gl_hi = (
            sem("gl_" + n) for n in ("g", "st", "v", "kt", "kn", "a", "at", "i", "s", "oi", "on", "hi"))
        ml_u, ml_hi, ml_lo = sem("ml_u"), sem("ml_hi"), sem("ml_lo")
        lam_s, lam_p, lam_d = sem("lam_s"), sem("lam_p"), sem("lam_d")
        mg_sg, mg_t, mg_hi, mg_lo = sem("mg_sg"), sem("mg_t"), sem("mg_hi"), sem("mg_lo")
        cb_f, cb_hi, cb_lo, cb_o, cb_k = (sem("cb_" + n) for n in ("f", "hi", "lo", "o", "k"))
        kd = sem("kd")
        vt_t, vt_c = sem("vt_t"), sem("vt_c")
        raw_zero = sem("raw_zero")
        go_sp, go_pe, go_act, go_dve = sem("go_sp"), sem("go_pe"), sem("go_act"), sem("go_dve")
        zero_s = sem("zero_s")
        out_t, out_c, out_d = sem("out_t"), sem("out_c"), sem("out_d")

        A = Arena()
        x_in, mem_in, rows_in, lp_in = A(QT, D), A(M // PART, D), A(PART), A(4, HALF)

        A = Arena()
        N_sq, N_xn, N_acc, N_rs = A(2, T), A(2, T), A(T), A(T)
        N_std = N_acc
        N_end = A.at
        F_out, O_nat = A(KT, T), A(QT, D)

        A = Arena()
        SM, PB, PTs = A(2, T), A(2, T), A(2, T)
        att_end = A.at

        A = Arena(att_end)
        X_on = A(2, QT, PART)
        X_q, X_k = A(4, T), A(4, T)
        X_qk, X_v = A(8, T), A(QT, FOX)
        X_z, X_e = (X_on[:, a].rearrange("p a b -> p (a b)") for a in range(2))
        X_c = X_q[:, 0, :]
        H_sq, H_std, H_rs = SM, PB, PTs
        assert A.at <= AW - KT * M

        A = Arena()
        G_z, G_e = A(2, T), A(2, T)
        G_b = A(2, T)
        G_dec = A(2, T // HALF)
        G_qk, G_ke, G_v, G_r = A(4, T), A(2, T), A(QT, GLA_VW), A(4, T)
        G_qs, G_ks, G_es, G_vs = A(2, PART), A(2, PART), A(2, PART), A(GLA_VW)
        G_kn, G_at, G_S = A(2, PART), A(2, 2, HALF), A(2, PART)
        G_O = arena[:, 0:QT * GLA_VW].rearrange("p (t n) -> p t n", t=QT)
        assert A.at <= AW - KT * M
        G_lr = [x[0:16, KT - 1, :] for x in (ah, al)]

        A = Arena(att_end)
        C_on, C_q = A(2, QT, M), A(4, T)
        C_Q, C_K = A(KT, T), A(KT, M)
        assert A.at <= AW - KT * M
        C_V = A(2, D)
        C_rs = PTs
        C_sq, C_std = C_on[:, 0].rearrange("p a b -> p (a b)").rearrange("p (a b) -> p a b", a=2), C_q

        A = Arena(N_end)
        E_t, E_u = A(2, T), A(2, T)

        A = Arena(att_end)
        D_on, D_q, D_k = A(2, QT, PART), A(4, T), A(2, T)
        D_raw, D_t = A(4, T), A(2, T)
        D_V, D_g = A(QT, PC), A(2, T)

        A = Arena(att_end)
        S_on, S_qr, S_q = A(2, QT, PART), A(2, T), A(4, T)
        S_mg = A(KT, T)
        S_kd = A(2, 2, T)
        S_v = A(2, QT, PART)
        S_gate = A(QT, 48)
        S_gs = A(QT, 12)
        S_kc, S_vc = A(2, 2 * CKEY), A(2, 4, HALF)
        S_w2k, S_w2v = A(2, PART), A(2, HALF)
        S_h1 = A(2, 2, 2 * NCMP)
        S_gT = A(T)
        S_hT = S_gT.rearrange("p (a n) -> p a n", a=2)
        S_vT = S_on.rearrange("p a t n -> p a (t n)")
        assert A.at <= AW, A.at
        S_sg = PB
        S_x2 = S_q
        S_bf = SM
        S_kr = PTs
        S_kraw = PB
        B_h, B_l = ([x[:, 2 * a:2 * a + 2, :].rearrange("p a b -> p (a b)")[:, 0:16 * 2 * NCMP].rearrange("p (j g n) -> p j g n", j=16, g=2)
                     for a in range(2)] for x in (ah, al))

        def tiles(w):
            return w.rearrange("(q p) n -> p q n", p=PART)

        w_in, w_in2 = tiles(d["w_in"]), tiles(d["w_in_2"][0])
        w_out, w_out2 = tiles(d["w_out"]), tiles(d["w_out_2"][0])
        xwq, xwkv, xwo = tiles(d["xattn_wq"]), tiles(d["xattn_wkv"]), tiles(d["xattn_wo"])
        mw1, mw2 = tiles(d["mlp_w1"]), tiles(d["mlp_w2"])
        ffw = {n: tuple(tiles(d[f"{n}_{w}_2"][0]) for w in ("w1", "w3", "w2")) for n in ("ffn1", "ffn2")}
        wda, wns = tiles(d["w_proj_da_2"][0]), tiles(d["w_proj_nsa_2"][0])
        cw1 = [tiles(d["cmp_w1_2"][0, a]) for a in range(2)]

        block = ctx.enter_context(nc.Block())

        @block.sync
        def _(sp):
            sp.dma_start(cst[:], d["consts"]).then_inc(ld_const, 16)
            sp.dma_start(x_in, d["x"][0].rearrange("(t p) n -> p t n", p=PART)).then_inc(ld_x, 16)
            n_rows = 0
            for name, r in ROWS.items():
                v = d[name]
                if name in ("fox_q_norm_g", "fox_k_norm_g"):
                    for a in range(2):
                        sp.dma_start(rows_in[r:r + 1, a * HALF:(a + 1) * HALF], v.rearrange("(a n) -> a n", a=1)).then_inc(ld_rows, 16)
                        n_rows += 1
                    continue
                if name == "cmp_pos_2":
                    v = v[0].rearrange("v (j b) e -> (v j) (b e)", b=2)
                elif name == "da_head_norm_2":
                    v = v[0]
                elif len(v.shape) == 2:
                    v = v[0].rearrange("(k p) -> k p", p=PART)
                else:
                    v = v.rearrange("(k p) -> k p", p=PART)
                sp.dma_start(rows_in[r:r + v.shape[0], :], v).then_inc(ld_rows, 16)
                n_rows += 1
            assert n_rows == N_ROW_LOADS
            sp.dma_start(mem_in, d["mem"][0].rearrange("(t p) n -> p t n", p=PART)).then_inc(ld_mem, 16)
            sp.dma_start(foxb[:], d["fox_b_f"].rearrange("(n a) -> n a", a=1)).then_inc(ld_late, 16)
            sp.dma_start(gate2[:], d["gla_w_gate2"]).then_inc(ld_late, 16)
            sp.dma_start(lp_in[0:1], d["da_lambda_2"]).then_inc(ld_late, 16)

            def load(p, s, src):
                if not (isinstance(p, int) and p < 2):
                    sp.wait_ge(conv_done, p - 1)
                    sp.sem_inc(go_sp, 1)
                sp.dma_start(raw[:, s, 0:src.shape[1], 0:src.shape[2]], src).then_inc(raw_in[s], 16)

            def run(p0, n, w, col, rows=KT):
                if n <= 2:
                    for j in range(n):
                        load(p0 + j, (p0 + j) % 2, w[:, 0:rows, col + j * PC:col + (j + 1) * PC])
                    return
                with sp.Fori(0, n // 2) as i:
                    for j in range(2):
                        load(i * 2 + (p0 + j), (p0 + j) % 2, w[:, 0:rows, bass.ds(i * (2 * PC) + (col + j * PC), PC)])

            p = P0["small"]
            sp.wait_ge(raw_zero, 1)
            sp.dma_start(raw[:, p % 2, :, 0:8], w_in[:, :, W1_COL["ff"]:W1_COL["ff"] + 8]).then_inc(raw_in[p % 2], 16)
            sp.wait_ge(raw_in[p % 2], 16 * (p // 2 + 1))
            sp.dma_start(raw[:, p % 2, :, PART:PART + 16], w_in[:, :, W1_COL["glr"]:W1_COL["glr"] + 16]).then_inc(raw_in[p % 2], 16)
            run(P0["fqk"], 2, w_in, W1_COL["fq"])
            run(P0["fqk"] + 2, 2, w_in, W1_COL["fk"])
            run(P0["fv"], 2, w_in, W1_COL["fv"])
            run(P0["gqk"], 2, w_in, W1_COL["gqk"])
            run(P0["gv"], 2, w_in, W1_COL["gv"])
            run(P0["gr"], 2, w_in, W1_COL["gr"])
            run(P0["wout"], 4, w_out, 0)
            run(P0["xk"], 4, xwkv, 0)
            run(P0["xq"], 4, xwq, 0)
            run(P0["xv"], 4, xwkv, D)
            run(P0["xo"], 4, xwo, 0)
            with sp.Fori(0, D_FF // D) as r:
                for j in range(4):
                    load(r * 8 + (P0["mlp"] + j), (P0["mlp"] + j) % 2, mw1[:, :, bass.ds(r * D + j * PC, PC)])
                for j in range(4):
                    load(r * 8 + (P0["mlp"] + 4 + j), (P0["mlp"] + j) % 2, mw2[:, bass.ds(r * KT, KT), j * PC:(j + 1) * PC])

            def ffn(name):
                w1, w3, w2 = ffw[name]
                p0 = P0[name]
                with sp.Fori(0, 2) as r:
                    for j in range(4):
                        for e, w in enumerate((w1, w3)):
                            load(r * 12 + (p0 + 2 * j + e), (p0 + e) % 2, w[:, :, bass.ds(r * D + j * PC, PC)])
                    for j in range(4):
                        load(r * 12 + (p0 + 8 + j), (p0 + j) % 2, w2[:, bass.ds(r * KT, KT), j * PC:(j + 1) * PC])
                for j in range(3):
                    for e, w in enumerate((w1, w3)):
                        load(p0 + 24 + 2 * j + e, (p0 + e) % 2, w[:, :, 2 * D + j * PC:2 * D + (j + 1) * PC])
                for j in range(4):
                    load(p0 + 30 + j, (p0 + j) % 2, w2[:, 2 * KT:, j * PC:(j + 1) * PC])

            ffn("ffn1")
            with sp.Fori(0, 2) as r:
                for e in range(2):
                    for n, name in enumerate("qkv"):
                        load(r * 6 + (P0["da"] + 3 * e + n), (P0["da"] + 3 * e + n) % 2, w_in2[:, :, bass.ds(r * 512 + (W2_COL[name] + e * PC), PC)])

            def alternate(p0, wa, ca, wb):
                with sp.Fori(0, 4) as i:
                    load(i * 2 + p0, p0 % 2, wa[:, :, bass.ds(i * PC + ca, PC)])
                    load(i * 2 + (p0 + 1), (p0 + 1) % 2, wb[:, :, bass.ds(i * PC, PC)])

            alternate(P0["mda"], w_in2, W2_COL["ga"], wda)
            for j in range(3):
                load(P0["kv"] + j, (P0["kv"] + j) % 2, w_in2[:, :, W2_COL["kv"] + j * PC:W2_COL["kv"] + (j + 1) * PC])
            load(P0["kv"] + 3, (P0["kv"] + 3) % 2, w_in2[:, :, W2_COL["gate"]:W2_COL["gate"] + 48])
            for a in range(2):
                for j in range(2):
                    load(P0["cmp"] + 2 * a + j, (P0["cmp"] + j) % 2, cw1[a][:, j * KT:(j + 1) * KT, :])
            sp.wait_ge(lin_freed[1], P0["kv"])
            w2 = d["cmp_w2_2"][0].rearrange("a (c p) e -> a p c e", p=PART)
            for a in range(2):
                sp.dma_start(S_w2k[:, :, a * HALF:(a + 1) * HALF], w2[0]).then_inc(ld_late, 16)
            sp.dma_start(S_w2v, w2[1]).then_inc(ld_late, 16)
            run(P0["nq"], 4, w_in2, W2_COL["nq"])
            alternate(P0["mnsa"], w_in2, W2_COL["gb"], wns)
            run(P0["wout2"], 4, w_out2, 0)
            ffn("ffn2")
            for t in range(QT):
                sp.wait_ge(out_c, 2 * t + 2)
                sp.dma_start(out[0, t * PART:(t + 1) * PART, :], O_nat[:, t, :]).then_inc(out_d, 16)
            sp.wait_ge(out_d, 16 * QT)

        @block.gpsimd
        def _(pool):
            small = P0["small"]
            one = c_("one", 1).unsqueeze(2).to_broadcast([PART, KT, PC])
            pool.wait_ge(ld_const, 16)

            def cut(p, s):
                pool.wait_ge(raw_in[s], landed(p, s))
                if not (isinstance(p, int) and p < 2):
                    pool.wait_ge(lin_done, p * 2 - 2)
                nc.gpsimd.tensor_tensor(wh[:, s], raw[:, s], one, ALU.mult).then_inc(hi_done, 1)
                pool.wait_ge(hi_done, p + 1)
                nc.gpsimd.tensor_tensor(wl[:, s], raw[:, s], wh[:, s].bitcast(F32), ALU.subtract).then_inc(conv_done, 1)

            def landed(p, s):
                if isinstance(p, int):
                    return 16 * (p // 2 + 1 + (s == small % 2 and p >= small))
                return p * 8 + (16 + 16 * (s == small % 2) - 8 * s)

            first = small + 1
            first += first % 2
            for p in range(first):
                cut(p, p % 2)
            with pool.Fori(0, (PANELS - first) // 2) as i:
                for s in range(2):
                    cut(i * 2 + (first + s), s)
            if (PANELS - first) % 2:
                cut(PANELS - 1, (PANELS - 1) % 2)

        @block.tensor
        def _(pe):
            pe.sem_inc(at_s, UINIT)
            pe.sem_inc(at_t, UINIT)
            pe.sem_inc(at_o, UINIT)
            pe.sem_inc(fin_t, FINIT)
            pe.sem_inc(gl_i, 2)

            def product(o, w, x, first, last):
                nc.tensor.matmul(o, w[0], x[0], start=first, stop=False)
                nc.tensor.matmul(o, w[0], x[1], start=False, stop=False)
                return nc.tensor.matmul(o, w[1], x[0], start=False, stop=last)

            def begin(p, c):
                if not (isinstance(p, int) and p == 0):
                    pe.wait_ge(lin_freed[c], p)

            def panel_t(p, s, act, n=T, kt=KT, m=PART, each=None, paired=False):
                pe.wait_ge(conv_done, p + 1)
                if paired:
                    begin(p, 0)
                    begin(p, 1)
                    for k in range(kt):
                        each(k)
                        for c in range(2):
                            cols = slice(c * PART, (c + 1) * PART)
                            mm = product(pl[c][:, 0:n], (wh[:, s, k, cols], wl[:, s, k, cols]), (act[0][:, k, 0:n], act[1][:, k, 0:n]), k == 0, k == kt - 1)
                            if k == kt - 1:
                                mm.then_inc(lin_done, 1)
                    return
                for c in range(2):
                    begin(p, c)
                    mc = m if isinstance(m, int) else m[c]
                    for k in range(kt):
                        if each and c == 0:
                            each(k)
                        cols = slice(c * PART, c * PART + mc)
                        mm = product(pl[c][0:mc, 0:n], (wh[:, s, k, cols], wl[:, s, k, cols]),
                                     (act[0][:, k, 0:n], act[1][:, k, 0:n]), k == 0, k == kt - 1)
                    mm.then_inc(lin_done, 1)

            def panel_n(p, s, act, tiles_=((0, 1), (2, 3)), between=None):
                pe.wait_ge(conv_done, p + 1)
                for c in range(2):
                    if c and between:
                        between()
                    begin(p, c)
                    for j, t in enumerate(tiles_[c]):
                        for k in range(KT):
                            tok = slice(t * PART, (t + 1) * PART)
                            mm = product(pl[c][:, j * PC:(j + 1) * PC], (act[0][:, k, tok], act[1][:, k, tok]),
                                         (wh[:, s, k, :], wl[:, s, k, :]), k == 0, k == KT - 1)
                    mm.then_inc(lin_done, 1)

            X, Y = (xh, xl), (ah, al)

            def normed(call):
                return lambda k: pe.wait_ge(nm_lo, 8 * NORM[call] + k + 1)

            def mean(call, n=T):
                pe.wait_ge(nm_ac, 7 * NORM[call] + 7)
                if NORM[call]:
                    pe.wait_ge(nm_std, NORM[call])
                nc.tensor.matmul(po[0][:, 0:n], ones, N_acc[:, 0:n], start=True, stop=True).then_inc(nm_mm, 1)

            def groups(U, gs):
                n = len(gs)
                for s in range(n + 3):
                    if s < n:
                        pe.wait_ge(at_m, U + (s - 1))
                        for u in gs[s]:
                            for a, (q, k) in enumerate(u["qk"]):
                                mm = nc.tensor.matmul(ps[s % 2][:, u["col"]:u["col"] + u["nk"]], q, k, start=(a == 0), stop=(a == len(u["qk"]) - 1))
                        mm.then_inc(at_s, 1)
                    j = s - 2
                    if 0 <= j < n:
                        pe.wait_ge(at_p, U + (j + 1))
                        pe.wait_ge(at_pt, U + (j - 1))
                        for lo in range(0, width(gs[j]), PART):
                            mm = nc.tensor.transpose(pt[j % 2][:, lo:lo + PART], PB[:, j % 2, lo:lo + PART], ident)
                        mm.then_inc(at_t, 1)
                    j = s - 3
                    if j >= 0:
                        pe.wait_ge(at_pt, U + (j + 1))
                        pe.wait_ge(at_of, U + (j - 1))
                        for u in gs[j]:
                            for o, dv, los, v in u["pv"]:
                                for b, lo in enumerate(los):
                                    mm = nc.tensor.matmul(po[j % 2][:, o:o + dv], PTs[:, j % 2, lo:lo + PART], v[b], start=(b == 0), stop=(b == len(los) - 1))
                        mm.then_inc(at_o, 1)

            def width(g):
                return sum(u["nk"] for u in g)

            def causal_groups(q, k, v, dv):
                gs = []
                for group in CAUSAL_GROUPS:
                    g = []
                    for n, (pr, a, t, col) in enumerate(group):
                        nk = (t + 1) * PART
                        g.append(dict(qk=[(q(pr, a, slice(t * PART, nk)), k(pr, a, nk))], col=col, nk=nk,
                                      pv=[(n * dv, dv, [col + b * PART for b in range(t + 1)], [v(pr, a, b) for b in range(t + 1)])]))
                    gs.append(g)
                return gs

            def turn_back(F, src, at=0):
                f = at % 2
                pe.wait_ge(fin_read, F - 1)
                for t in range(QT):
                    mm = nc.tensor.transpose(pt[f][:, t * PART:(t + 1) * PART], src[:, t, :], ident)
                mm.then_inc(fin_t, 1)

            pe.wait_ge(ld_const, 16)
            pe.wait_ge(ld_rows, 16 * N_ROW_LOADS)
            nc.tensor.transpose(pt[0][:, 0:NROWS], rows_in[0:NROWS, :], cst[0:NROWS, CAT["ident"]:CAT["ident"] + NROWS]).then_inc(st_t, 1)
            pe.wait_ge(ld_x, 16)
            for g in range(1, 17):
                if g == 9:
                    mean("mix")
                    pe.wait_ge(ld_mem, 16)
                if g >= 2:
                    pe.wait_ge(st_c, g - 1)
                src = x_in if g < 9 else mem_in
                k = (g - 1) % KT
                for t in range(src.shape[1]):
                    mm = nc.tensor.transpose(pt[g % 2][:, t * PART:(t + 1) * PART], src[:, t, k * PART:(k + 1) * PART], ident)
                mm.then_inc(st_t, 1)

            def head_sums(j, tile_sq, lhs):
                if j >= 2:
                    pe.wait_ge(hn_std, j - 1)
                for a, sq in enumerate(tile_sq):
                    mm = nc.tensor.matmul(po[j % 2][:, 0:sq.shape[-1]], lhs, sq, start=(a == 0), stop=(a == len(tile_sq) - 1))
                mm.then_inc(hn_mm, 1)

            def fox_sums(p):
                for c in range(2):
                    pe.wait_ge(lin_freed[c], p + 1)
                    head_sums(2 * (p - P0["fqk"]) + c, [H_sq[:, c, :]], c_("block", PART))

            p = P0["small"]
            panel_t(p, p % 2, X, m=(8, 16), each=normed("mix"))
            for p in range(P0["fqk"], P0["fv"]):
                panel_t(p, p % 2, X)
                if p > P0["fqk"]:
                    fox_sums(p - 1)
            for p in range(P0["fv"], P0["fv"] + 2):
                panel_n(p, p % 2, X)
                if p == P0["fv"]:
                    fox_sums(p - 1)
            pe.wait_ge(lam_s, 5)
            nc.tensor.matmul(ps[0][:, 0:1], cst[0:1, CAT["ones"]:CAT["ones"] + PART], lam[0:1, 2:3], start=True, stop=True).then_inc(lam_p, 1)
            pe.wait_ge(lam_d, 1)
            with pe.Fori(0, 2) as i:
                pe.wait_ge(at_st, i + (A0["fox"] + 1))
                pe.wait_ge(at_ks, i + (A0["fox"] + 1))
                pe.wait_ge(fin_read, i * 2 + F0["fox"])
                U = i * NG + U0["fox"]
                groups(U, causal_groups(lambda pr, a, tok: X_q[:, 2 * pr + a, tok], lambda pr, a, nk: X_k[:, 2 * pr + a, 0:nk],
                                        lambda pr, a, b: X_v[:, b, bass.ds(i * (2 * PART) + (pr * PART + a * HALF), HALF)], HALF))
                pe.wait_ge(at_of, U + NG)
                for pr in range(2):
                    turn_back(i * 2 + (F0["fox"] + pr), X_on[:, pr], pr)
            pe.wait_ge(fin_read, F0["gla"])

            p = P0["gqk"]
            pe.wait_ge(ld_late, 16 * 3)
            pe.wait_ge(lin_freed[1], p)
            for a in range(2):
                for n in range(2):
                    mm = nc.tensor.matmul(po[a][:, :], gate2[0:16, a * PART:(a + 1) * PART], G_lr[n].bitcast(F32), start=(n == 0), stop=(n == 1))
                mm.then_inc(gl_g, 1)
            for j in range(2):
                panel_t(p + j, (p + j) % 2, X)
            for j in range(2):
                panel_n(P0["gv"] + j, (P0["gv"] + j) % 2, X)
            for j in range(2):
                panel_t(P0["gr"] + j, (P0["gr"] + j) % 2, X)

            with pe.Fori(0, QT) as i:
                pe.wait_ge(gl_st, i + 1)
                pe.sem_inc(go_pe, 1)
                for a in range(2):
                    mm = nc.tensor.transpose(pt[0][:, a * PART:(a + 1) * PART], G_es[:, a, :], ident)
                mm.then_inc(gl_kt, 1)
                for c in range(2):
                    for hd in range(4):
                        a, b = hd // 2, hd % 2
                        r = slice(b * HALF, (b + 1) * HALF)
                        tk = slice(c * HALF, (c + 1) * HALF)
                        mm = nc.tensor.matmul(ps[b][tk, a * HALF:(a + 1) * HALF], G_ks[r, a, tk], G_qs[r, a, tk], start=True, stop=True)
                mm.then_inc(gl_a, 1)
                pe.wait_ge(gl_kn, i + 1)
                pe.wait_ge(gl_at, i + 1)
                pe.wait_ge(gl_v, i + 1)
                pe.sem_inc(go_pe, 1)
                for c in range(2):
                    tk = slice(c * HALF, (c + 1) * HALF)
                    pe.wait_ge(gl_s, i * 2 + (c + 1))
                    pe.sem_inc(go_pe, 1)
                    for hd in range(4):
                        a, b = hd // 2, hd % 2
                        r = slice(b * HALF, (b + 1) * HALF)
                        nc.tensor.matmul(po[b][tk, a * PART:(a + 1) * PART], G_qs[r, a, tk], G_S[r, a, :], start=True, stop=True)
                    for hd in range(4):
                        a, b = hd // 2, hd % 2
                        nc.tensor.matmul(pt[c][tk, hd * PART:(hd + 1) * PART], G_at[tk, b, a, :], G_vs[tk, hd * PART:(hd + 1) * PART], start=True, stop=True)
                    for hd in range(4):
                        a, b = hd // 2, hd % 2
                        r = slice(b * HALF, (b + 1) * HALF)
                        mm = nc.tensor.matmul(ps[c][r, 256 + a * PART:256 + (a + 1) * PART], G_kn[tk, a, r], G_vs[tk, hd * PART:(hd + 1) * PART], start=True, stop=True)
                    mm.then_inc(gl_i, 1)
            pe.wait_ge(fin_rs, 1)
            for hd in range(4):
                turn_back(F0["gla"] + hd, G_O[:, :, hd * PART:(hd + 1) * PART], hd)
            for j in range(4):
                panel_t(P0["wout"] + j, (P0["wout"] + j) % 2, Y, each=lambda k: pe.wait_ge(fin_read, F0["gla"] + max(k - 3, 0)), paired=j == 0)
                if j == 0:
                    mean("mem", M)

            def pair_sums(p, j, n):
                for c in range(2):
                    pe.wait_ge(lin_freed[c], p + 1)
                head_sums(j, [C_sq[:, c, 0:n] for c in range(2)], ones)

            for j in range(4):
                p = P0["xk"] + j
                panel_t(p, p % 2, Y, n=M, each=normed("mem"), paired=j == 0)
                if j == 0:
                    mean("xattn")
                if j == 1:
                    pe.wait_ge(nm_std, NORM["xattn"] + 1)
                if j:
                    pair_sums(p - 1, 8 + j - 1, M)
            for j in range(4):
                p = P0["xq"] + j
                panel_t(p, p % 2, X, each=normed("xattn"), paired=j == 0)
                if j == 0:
                    pair_sums(p - 1, 8 + 3, M)
                else:
                    pair_sums(p - 1, 12 + j - 1, T)
            for j in range(4):
                p = P0["xv"] + j
                panel_n(p, p % 2, Y, tiles_=((0,), (1,)))
                if j == 0:
                    pair_sums(p - 1, 12 + 3, T)
            with pe.Fori(0, 2) as i:
                pe.wait_ge(at_st, i + (A0["xa"] + 1))
                pe.wait_ge(fin_read, i * 4 + F0["xa"])
                U = i * NG_XA + U0["xa"]
                gs = []
                for hd in range(2):
                    for t0 in (0, 2):
                        gs.append([dict(qk=[(C_q[:, 2 * hd + a, (t0 + n) * PART:(t0 + n + 1) * PART],
                                             C_K[:, bass.ds(i * 4 + (2 * hd + a), 1), :].rearrange("p a n -> p (a n)")) for a in range(2)],
                                        col=n * M, nk=M, pv=[(n * M, M, [n * M, n * M + PART], [C_V[:, b, bass.ds(i * (2 * M) + hd * M, M)] for b in range(2)])])
                                   for n in range(2)])
                groups(U, gs)
                pe.wait_ge(at_of, U + NG_XA)
                for f in range(4):
                    turn_back(i * 4 + (F0["xa"] + f), C_on[:, f // 2, :, (f % 2) * PART:(f % 2 + 1) * PART], f)
            for j in range(4):
                panel_t(P0["xo"] + j, (P0["xo"] + j) % 2, Y, each=lambda k: pe.wait_ge(fin_read, F0["xa"] + k + 1), paired=j == 0)

            mean("mlp")
            with pe.Fori(0, D_FF // D) as r:
                for j in range(4):
                    panel_t(r * 8 + (P0["mlp"] + j), (P0["mlp"] + j) % 2, X, each=normed("mlp"), paired=j == 0)
                for j in range(4):
                    panel_t(r * 8 + (P0["mlp"] + 4 + j), (P0["mlp"] + j) % 2, Y,
                            each=(lambda k: pe.wait_ge(ml_lo, r * 8 + (MLP0["mlp"] + k + 1))) if j == 0 else None)

            def ffn(name):
                mean(name)
                p0, m0 = P0[name], MLP0[name]
                with pe.Fori(0, 2) as r:
                    for j in range(8):
                        panel_t(r * 12 + (p0 + j), (p0 + j) % 2, X, each=normed(name), paired=j == 0)
                    for j in range(4):
                        panel_t(r * 12 + (p0 + 8 + j), (p0 + j) % 2, Y,
                                each=(lambda k: pe.wait_ge(ml_lo, r * 8 + (m0 + k + 1))) if j == 0 else None)
                for j in range(6):
                    panel_t(p0 + 24 + j, (p0 + j) % 2, X)
                for j in range(4):
                    panel_t(p0 + 30 + j, (p0 + j) % 2, Y, kt=6, each=(lambda k: pe.wait_ge(ml_lo, m0 + 16 + k + 1)) if j == 0 else None)

            ffn("ffn1")
            mean("mix2")

            def rotate(o, src):
                nc.tensor.matmul(o[:, :], c_("rot", PART), src, start=True, stop=True).then_inc(rp_t, 1)

            with pe.Fori(0, 2) as r:
                for e in range(2):
                    p = r * 6 + (P0["da"] + 3 * e)
                    sl = (P0["da"] + 3 * e) % 2
                    it = r * 2 + e
                    U = it * NG + U0["da"]

                    panel_t(p, sl, X, each=normed("mix2"), paired=e == 0)
                    if e:
                        pe.wait_ge(fin_rs, it + 1)
                        for pr in range(2):
                            turn_back(it * 2 + (F0["da"] - 2 + pr), D_on[:, pr], pr)
                    panel_t(p + 1, 1 - sl, X)
                    for c in range(2):
                        pe.wait_ge(lin_freed[c], p + 1)
                        rotate(ps[c], D_raw[:, c, :])

                    def rotate_keys():
                        for c in range(2):
                            pe.wait_ge(lin_freed[c], p + 2)
                            rotate(po[c], D_raw[:, 2 + c, :])

                    panel_n(p + 2, sl, X, between=rotate_keys)
                    pe.wait_ge(at_st, it + (A0["da"] + 1))
                    for c in range(2):
                        pe.wait_ge(lin_freed[c], p + 3)
                    pe.wait_ge(fin_read, it * 2 + F0["da"])
                    groups(U, causal_groups(lambda pr, a, tok: D_q[:, 2 * pr + a, tok], lambda pr, a, nk: D_k[:, pr, 0:nk],
                                            lambda pr, a, b: D_V[:, b, pr * PART:(pr + 1) * PART], PART))
                pe.wait_ge(fin_rs, it + 2)
                for pr in range(2):
                    turn_back(it * 2 + (F0["da"] + pr), D_on[:, pr], pr)

            def alternate(p0, outputs):
                with pe.Fori(0, 4) as i:
                    panel_t(i * 2 + p0, p0 % 2, X)
                    pe.wait_ge(fin_read, outputs)
                    panel_t(i * 2 + (p0 + 1), (p0 + 1) % 2, Y)

            alternate(P0["mda"], F0["ns"])

            p = P0["kv"]
            panel_t(p, p % 2, X)
            for br in range(2):
                panel_t(p + 1 + br, (p + 1 + br) % 2, X)
            q = p + 3
            pe.wait_ge(conv_done, q + 1)
            begin(q, 0)
            for k in range(KT):
                mm = product(pl[0][0:48, :], (wh[:, q % 2, k, 0:48], wl[:, q % 2, k, 0:48]), (xh[:, k, :], xl[:, k, :]), k == 0, k == KT - 1)
            mm.then_inc(lin_done, 2)
            for br in range(2):
                pe.wait_ge(lin_freed[1], p + 2 + br)
                for t in range(QT):
                    mm = nc.tensor.transpose(pt[br][:, t * PART:(t + 1) * PART], S_vT[:, br, t * PART:(t + 1) * PART], ident)
                mm.then_inc(vt_t, 1)
            for br in range(2):
                pe.wait_ge(lin_freed[0], p + 2 + br)
                rotate(po[br], S_kraw[:, br, :])
            pe.wait_ge(lin_freed[0], p + 4)
            for t in range(QT):
                mm = nc.tensor.transpose(ps[0][:, t * 48:(t + 1) * 48], S_gT[0:48, t * PART:(t + 1) * PART], cst[0:48, CAT["ident"]:CAT["ident"] + 48])
            mm.then_inc(vt_t, 1)
            for a in range(2):
                for part in range(2):
                    q = P0["cmp"] + 2 * a + part
                    pe.wait_ge(conv_done, q + 1)
                    if part == 0:
                        begin(q, 0)
                        pe.wait_ge(cb_lo, 2 * a + 2)
                    for k in range(KT):
                        j = part * KT + k
                        mm = product(pl[0][0:2 * NCMP, 0:PC], tuple(x[a][:, j].rearrange("p g n -> p (g n)") for x in (B_h, B_l)),
                                     (wh[:, q % 2, k, :], wl[:, q % 2, k, :]), j == 0, j == 15)
                    mm.then_inc(lin_done, 2)
            for a in range(2):
                pe.wait_ge(lin_freed[0], P0["cmp"] + 2 * a + 2)
                for c in range(2):
                    mm = nc.tensor.transpose(ps[1][:, (2 * a + c) * 2 * NCMP:(2 * a + c + 1) * 2 * NCMP], S_hT[0:2 * NCMP, a, c * PART:(c + 1) * PART],
                                             cst[0:2 * NCMP, CAT["ident"]:CAT["ident"] + 2 * NCMP])
            mm.then_inc(vt_t, 1)
            pe.wait_ge(vt_c, 3 + 1)
            pe.wait_ge(ld_late, 16 * 6)
            pe.wait_ge(kd, 2)
            for c in range(2):
                mm = nc.tensor.matmul(po[0][:, 0:2 * NCMP], S_w2k[:, c, :], S_h1[:, 0, c, :], start=(c == 0), stop=(c == 1))
            mm.then_inc(cb_o, 1)
            for g in range(2):
                for c in range(2):
                    mm = nc.tensor.matmul(po[1][0:NCMP, g * HALF:(g + 1) * HALF], S_h1[:, 1, c, g * NCMP:(g + 1) * NCMP], S_w2v[:, c, :],
                                          start=(c == 0), stop=(c == 1))
            mm.then_inc(cb_o, 1)
            pe.wait_ge(cb_k, 2)

            with pe.Fori(0, 2) as g:
                kv = bass.ds(g, 1)
                for e in range(2):
                    it = g * 2 + e
                    p = it + P0["nq"]
                    U = it * NG_NS + U0["ns"]
                    panel_t(p, (P0["nq"] + e) % 2, X)
                    if e:
                        pe.wait_ge(at_of, U)
                        for pr in range(2):
                            turn_back(it * 2 + (F0["ns"] - 2 + pr), S_on[:, pr], pr)
                    for c in range(2):
                        pe.wait_ge(lin_freed[c], p + 1)
                        rotate(po[c], S_qr[:, c, :])
                    pe.wait_ge(fin_read, it * 2 + F0["ns"])
                    pe.wait_ge(at_st, it + (A0["ns"] + 1))
                    gs = []
                    for pr in range(2):
                        gs.append([dict(qk=[(S_qr[:, pr, t * PART:(t + 1) * PART], S_kc[:, kv, :].rearrange("p a n -> p (a n)"))], col=t * 2 * CKEY, nk=2 * CKEY,
                                        pv=[(t // 2 * PC, PC, [t // 2 * PART], [S_vc[:, kv].rearrange("p a n d -> p (a n d)")])] if t % 2 else [])
                                   for t in range(QT)])
                    for br in range(2):
                        gs += causal_groups(lambda pr, a, tok: S_q[:, 2 * pr + a, tok], lambda pr, a, nk: S_kd[:, br, kv, 0:nk].rearrange("p a n -> p (a n)"),
                                            lambda pr, a, b: S_v[:, br, b, bass.ds(g * HALF, HALF)], HALF)
                    groups(U, gs)
                pe.wait_ge(at_of, U + NG_NS)
                for pr in range(2):
                    turn_back(it * 2 + (F0["ns"] + pr), S_on[:, pr], pr)
            alternate(P0["mnsa"], F0["end"])
            for j in range(4):
                panel_t(P0["wout2"] + j, (P0["wout2"] + j) % 2, Y, each=lambda k: pe.wait_ge(mg_lo, k + 1), paired=j == 0)
            ffn("ffn2")

            mean("final")
            pe.wait_ge(nm_xn, 8 * NORM["final"] + 8)
            for g in range(2 * QT):
                t, f0 = g // 2, 4 * (g % 2)
                if g >= 2:
                    pe.wait_ge(out_c, g - 1)
                for f in range(4):
                    mm = nc.tensor.transpose(pt[g % 2][:, f * PART:(f + 1) * PART], F_out[:, f0 + f, t * PART:(t + 1) * PART], ident)
                mm.then_inc(out_t, 1)

        @block.scalar
        def _(act):
            act.sem_inc(at_p, UINIT)
            act.sem_inc(at_pt, UINIT)
            act.sem_inc(fin_hi, FINIT)
            act.sem_inc(ml_hi, 2)

            def tile(p, c):
                act.wait_ge(lin_done, p * 2 + (c + 1))

            def dyn(buf, e):
                return buf[:, bass.ds(e, 1), :].rearrange("p a n -> p (a n)")

            def evac(p, c, dst, func=ACT.Copy, rows=PART, n=T, **kw):
                tile(p, c)
                nc.scalar.activation(dst, pl[c][0:rows, 0:n], func, **kw).then_inc(lin_freed[c], 1)

            def squares(name, src, ready, n=T):
                call = NORM[name]
                for k in range(KT):
                    ready(k)
                    if k >= 2:
                        act.wait_ge(nm_ac, 7 * call + max(k - 2, 1))
                    elif call:
                        act.wait_ge(nm_ac, 7 * call)
                    nc.scalar.activation(N_sq[:, k % 2, 0:n], src[:, k, 0:n], ACT.Square).then_inc(nm_sq, 1)

            def mean(name, n=T):
                act.wait_ge(nm_mm, NORM[name] + 1)
                nc.scalar.activation(N_std[:, 0:n], po[0][:, 0:n], ACT.Sqrt, bias=eps, scale=1.0 / D).then_inc(nm_std, 1)

            def norm_high(name, dst, n=T, after=None, ks=range(KT)):
                if after:
                    act.wait_ge(lin_done, 2 * after)
                for k in ks:
                    act.wait_ge(nm_xn, 8 * NORM[name] + k + 1)
                    nc.scalar.activation(dst[:, k, 0:n], N_xn[:, k % 2, 0:n], ACT.Copy).then_inc(nm_hi, 1)

            def norm(name, ready, dst=xh):
                squares(name, h, ready)
                mean(name)
                if dst is not None:
                    norm_high(name, dst)

            def after(p0):
                return lambda k: act.wait_ge(lin_freed[k % 2], p0 + k // 2 + 1)

            def groups(U, gs):
                n = len(gs)
                for s in range(n + 2):
                    if s < n:
                        nks, scale, at = gs[s]
                        act.wait_ge(at_m, U + (s + 1))
                        act.wait_ge(at_t, U + (s - 1))
                        act.sem_inc(go_act, 1)
                        col = 0
                        for m, nk in enumerate(nks):
                            cols = slice(col, col + nk)
                            if at is None:
                                op = nc.scalar.activation(PB[:, s % 2, cols], SM[:, s % 2, cols], ACT.Exp, scale=scale)
                            else:
                                op = nc.scalar.activation(PB[:, s % 2, cols], SM[:, s % 2, cols], ACT.Exp, bias=negm[:, at + m:at + m + 1], scale=scale,
                                                          accum_out=rsum[:, at + m:at + m + 1])
                            col += nk
                        op.then_inc(at_p, 1)
                    j = s - 2
                    if j >= 0:
                        w = sum(gs[j][0])
                        act.wait_ge(at_t, U + (j + 1))
                        act.wait_ge(at_o, U + (j - 1))
                        act.sem_inc(go_act, 1)
                        nc.scalar.activation(PTs[:, j % 2, 0:w], pt[j % 2][:, 0:w], ACT.Copy).then_inc(at_pt, 1)

            def causal_groups(at=0):
                gs = []
                for g in CAUSAL_GROUPS:
                    gs.append(([(t + 1) * PART for _, _, t, _ in g], -1.0, at))
                    at += len(g)
                return gs

            def finish(F, dst, at=0):
                act.wait_ge(fin_t, F + 1)
                act.sem_inc(go_act, 1)
                nc.scalar.activation(dst, pt[at % 2][:, :], ACT.Copy).then_inc(fin_hi, 1)

            act.wait_ge(st_t, 1)
            nc.scalar.activation(gT[:], pt[0][:, 0:NROWS], ACT.Copy).then_inc(st_c, 1)
            for g in range(1, 17):
                if g == 9:
                    squares("mix", h, lambda k: act.wait_ge(st_c, k + 2))
                    mean("mix")
                act.wait_ge(st_t, g + 1)
                dst, n = (h[:, g - 1, :], T) if g < 9 else (memT[:, g - 9, :], M)
                nc.scalar.activation(dst, pt[g % 2][:, 0:n], ACT.Copy).then_inc(st_c, 1)
            norm_high("mix", xh)
            act.wait_ge(lam_s, 2)
            nc.scalar.activation(lam[0:1, 0:2], lam[0:1, 0:2], ACT.Exp).then_inc(lam_s, 1)

            def root(j, std, n, width):
                act.wait_ge(hn_mm, j + 1)
                if j >= 2:
                    act.wait_ge(hn_rs, j - 1)
                nc.scalar.activation(std[:, j % 2, 0:n], po[j % 2][:, 0:n], ACT.Sqrt, bias=eps, scale=1.0 / width).then_inc(hn_std, 1)

            p = P0["small"]
            act.wait_ge(ld_late, 16 * 3)
            evac(p, 0, X_z[0:8, :], ACT.Identity, rows=8, bias=foxb[:, 0:1])
            tile(p, 1)
            nc.scalar.activation(G_lr[0], pl[1][0:16, :], ACT.Copy).then_inc(gl_hi, 1)
            act.wait_ge(lin_freed[0], p + 1)
            nc.scalar.activation(X_e[0:8, :], X_z[0:8, :], ACT.Abs).then_inc(ls_a, 1)
            act.wait_ge(ls_a, 1)
            nc.scalar.activation(X_e[0:8, :], X_e[0:8, :], ACT.Exp, scale=-1.0).then_inc(ls_a, 1)
            act.wait_ge(ls_a, 2)
            nc.scalar.activation(X_e[0:8, :], X_e[0:8, :], ACT.Ln, bias=c_("one", 1, 8)).then_inc(ls_a, 1)
            for p in range(P0["fqk"], P0["fv"] + 2):
                for c in range(2):
                    tile(p, c)
                    if p < P0["fv"]:
                        k = 2 * (p - P0["fqk"]) + c
                        nc.scalar.activation(X_qk[:, k, :], pl[c][:, :], ACT.Copy)
                        if k >= 2:
                            act.wait_ge(hn_mm, k - 1)
                        nc.scalar.activation(H_sq[:, c, :], pl[c][:, :], ACT.Square).then_inc(lin_freed[c], 1)
                    else:
                        j = p - P0["fv"]
                        nc.scalar.activation(X_v[:, 2 * c:2 * c + 2, j * PC:(j + 1) * PC], pl[c][:, :].rearrange("p (a n) -> p a n", a=2),
                                             ACT.Copy).then_inc(lin_freed[c], 1)
                if P0["fqk"] < p <= P0["fv"]:
                    for c in range(2):
                        root(2 * (p - 1 - P0["fqk"]) + c, H_std, T, HALF)
            act.wait_ge(hn_out, 8)
            with act.Fori(0, 2) as i:
                act.wait_ge(at_s, i * NG + U0["fox"])
                act.sem_inc(go_act, 1)
                for pr in range(2):
                    for a in range(2):
                        src = X_qk[a * HALF:(a + 1) * HALF, bass.ds(i * 2 + (4 + pr), 1), :].rearrange("p a n -> p (a n)")
                        op = nc.scalar.activation(X_k[0:HALF, 2 * pr + a, :], src, ACT.Copy)
                op.then_inc(at_ks, 1)
                groups(i * NG + U0["fox"], causal_groups())
                for pr in range(2):
                    finish(i * 2 + (F0["fox"] + pr), dyn(ah, i * 2 + pr), pr)

            for a in range(2):
                act.wait_ge(gl_g, a + 1)
                nc.scalar.activation(G_z[:, a, :], po[a][:, :], ACT.Identity, bias=gcol("gla_b_gate", a)).then_inc(ls_a, 1)
            act.wait_ge(ls_a, 5)
            nc.scalar.activation(G_e, G_z, ACT.Abs).then_inc(ls_a, 1)
            act.wait_ge(ls_a, 6)
            nc.scalar.activation(G_e, G_e, ACT.Exp, scale=-1.0).then_inc(ls_a, 1)
            act.wait_ge(ls_a, 7)
            nc.scalar.activation(G_e, G_e, ACT.Ln, bias=c_("one", 1)).then_inc(ls_a, 1)
            last = G_b.rearrange("p a (n c) -> p (a n) c", c=HALF)[:, :, HALF - 1:HALF].rearrange("p n c -> p (n c)")
            act.wait_ge(ls_v, 7)
            nc.scalar.activation(G_e, G_b, ACT.Exp, scale=1.0 / 16).then_inc(ls_a, 1)
            nc.scalar.activation(G_dec.rearrange("p a n -> p (a n)"), last, ACT.Exp, scale=1.0 / 16).then_inc(ls_a, 1)
            act.wait_ge(ls_v, 8)
            nc.scalar.activation(G_ke, G_z, ACT.Exp, scale=1.0 / 16).then_inc(ls_a, 1)
            for j in range(2):
                for c in range(2):
                    evac(P0["gqk"] + j, c, G_qk[:, 2 * j + c, :])
            act.wait_ge(ls_v, 9)
            nc.scalar.activation(G_e, G_b, ACT.Exp, scale=-1.0 / 16).then_inc(ls_a, 1)
            for j in range(2):
                for c in range(2):
                    p = P0["gv"] + j
                    tile(p, c)
                    nc.scalar.activation(G_v[:, 2 * c:2 * c + 2, j * PC:(j + 1) * PC], pl[c][:, :].rearrange("p (a n) -> p a n", a=2),
                                         ACT.Copy).then_inc(lin_freed[c], 1)
            for j in range(2):
                for c in range(2):
                    evac(P0["gr"] + j, c, G_r[:, 2 * j + c, :], ACT.Silu)
            with act.Fori(0, QT) as i:
                act.wait_ge(gl_i, i * 2 + 2)
                act.sem_inc(go_act, 1)
                nc.scalar.activation(G_vs, dyn(G_v, i), ACT.Copy).then_inc(gl_v, 1)
                act.wait_ge(gl_i, i * 2 + 4)
                act.sem_inc(go_act, 1)
                for c in range(2):
                    rows = slice(c * HALF, (c + 1) * HALF)
                    op = nc.scalar.activation(dyn(G_O[rows], i), pt[c][rows, :], ACT.Copy)
                op.then_inc(gl_on, 1)
            act.wait_ge(gl_oi, QT)
            for n in range(4 * QT):
                op = nc.scalar.activation(G_qk[:, n // 4, n % 4 * PART:(n % 4 + 1) * PART], G_O[:, n // 4, n % 4 * PART:(n % 4 + 1) * PART], ACT.Square,
                                          accum_out=hss[:, n:n + 1])
            op.then_inc(fin_ss, 1)
            act.wait_ge(fin_ss, 1)
            nc.scalar.activation(hstd[:], hss[:], ACT.Sqrt, bias=eps, scale=1.0 / PART).then_inc(fin_std, 1)
            for hd in range(4):
                act.wait_ge(fin_g, hd + 1)
                nc.scalar.activation(ah[:, 4 + hd, :], G_r[:, hd, :], ACT.Copy).then_inc(fin_hi, 1)

            squares("mem", memT, lambda k: act.wait_ge(fin_read, F0["gla"] + 4), n=M)
            mean("mem", M)
            squares("xattn", h, after(P0["wout"]))
            norm_high("mem", ah, M, P0["xk"])
            mean("xattn")

            def evac_pair(p, j, dst, n):
                for c in range(2):
                    tile(p, c)
                    nc.scalar.activation(dst[:, 2 * (j % 4) + c, :], pl[c][:, 0:n], ACT.Copy)
                    if j > 8:
                        act.wait_ge(hn_mm, j)
                    nc.scalar.activation(C_sq[:, c, 0:n], pl[c][:, 0:n], ACT.Square).then_inc(lin_freed[c], 1)

            for j in range(4):
                evac_pair(P0["xk"] + j, 8 + j, C_K, M)
                if j:
                    root(8 + j - 1, C_std, M, M)
                if j < 2:
                    norm_high("xattn", xh, ks=range(4 * j, 4 * j + 4))
            for j in range(4):
                evac_pair(P0["xq"] + j, 12 + j, C_Q, T)
                if j == 0:
                    root(8 + 3, C_std, M, M)
                else:
                    root(12 + j - 1, C_std, T, M)
            for j in range(4):
                for c in range(2):
                    evac(P0["xv"] + j, c, C_V[:, c, j * PC:(j + 1) * PC], n=PC)
                if j == 0:
                    root(12 + 3, C_std, T, M)
            with act.Fori(0, 2) as i:
                groups(i * NG_XA + U0["xa"], [([M, M], -1.0, 2 * n) for n in range(NG_XA)])
                for f in range(4):
                    finish(i * 4 + (F0["xa"] + f), dyn(ah, i * 4 + f), f)

            norm("mlp", after(P0["xo"]))
            with act.Fori(0, D_FF // D) as r:
                for j in range(4):
                    for c in range(2):
                        k = 2 * j + c
                        m = r * 8 + (MLP0["mlp"] + k)
                        act.wait_ge(ml_u, m - 1)
                        tile(r * 8 + (P0["mlp"] + j), c)
                        act.sem_inc(go_act, 1)
                        nc.scalar.activation(E_t[:, c, :], pl[c][:, :], ACT.Relu).then_inc(lin_freed[c], 1)
                        act.wait_ge(ml_u, m + 1)
                        nc.scalar.activation(ah[:, k, :], E_u[:, c, :], ACT.Copy).then_inc(ml_hi, 1)

            def gated(p, m, j):
                for c in range(2):
                    act.wait_ge(lin_freed[c], p)
                    tile(p, c)
                    act.sem_inc(go_act, 1)
                    nc.scalar.activation(E_t[:, c, :], pl[c][:, :], ACT.Silu).then_inc(lin_freed[c], 1)
                for c in range(2):
                    act.wait_ge(lin_freed[c], p + 2)
                    act.sem_inc(go_act, 1)
                    nc.scalar.activation(ah[:, 2 * j + c, :], E_u[:, c, :], ACT.Copy).then_inc(ml_hi, 1)

            def ffn(name, before):
                norm(name, after(before))
                p0, m0 = P0[name], MLP0[name]
                with act.Fori(0, 2) as r:
                    for j in range(4):
                        gated(r * 12 + (p0 + 2 * j), None, j)
                for j in range(3):
                    gated(p0 + 24 + 2 * j, None, j)

            ffn("ffn1", P0["mlp"] + 28)
            norm("mix2", after(P0["ffn1"] + 30))
            def da_parts(it):
                for pr in range(2):
                    act.wait_ge(fin_g, it * 2 + (4 + pr + 1))
                    act.sem_inc(go_act, 1)
                    nc.scalar.activation(dyn(ah, it * 2 + pr), D_g[:, pr, :], ACT.Copy).then_inc(fin_hi, 1)

            with act.Fori(0, 2) as r:
                for e in range(2):
                    p = r * 6 + (P0["da"] + 3 * e)
                    it = r * 2 + e
                    for c in range(2):
                        act.wait_ge(at_st, it + A0["da"])
                        evac(p, c, D_raw[:, c, :])
                    if e:
                        da_parts(r * 2)
                    for c in range(2):
                        evac(p + 1, c, D_raw[:, 2 + c, :])
                    act.wait_ge(at_o, it * NG + U0["da"])
                    for c in range(2):
                        tile(p + 2, c)
                        act.sem_inc(go_act, 1)
                        nc.scalar.activation(D_V[:, 2 * c:2 * c + 2, :], pl[c][:, :].rearrange("p (a n) -> p a n", a=2), ACT.Copy).then_inc(lin_freed[c], 1)
                    groups(it * NG + U0["da"], causal_groups())
                    act.wait_ge(at_of, it * NG + (U0["da"] + NG))
                    act.sem_inc(go_act, 1)
                    for pr in range(2):
                        for t in range(QT):
                            op = nc.scalar.activation(D_g[:, pr, t * PART:(t + 1) * PART], D_on[:, pr, t, :], ACT.Square,
                                                      accum_out=hss[:, QT * pr + t:QT * pr + t + 1])
                    op.then_inc(fin_ss, 1)
                    act.wait_ge(fin_ss, it + (1 + 1))
                    nc.scalar.activation(hstd[:, 0:8], hss[:, 0:8], ACT.Sqrt, bias=eps, scale=1.0 / PART).then_inc(fin_std, 1)
                da_parts(r * 2 + 1)

            def gates(p0):
                with act.Fori(0, 4) as i:
                    for c in range(2):
                        act.wait_ge(lin_freed[c], i * 2 + p0)
                        tile(i * 2 + p0, c)
                        act.sem_inc(go_act, 1)
                        nc.scalar.activation(S_sg[:, c, :], pl[c][:, :], ACT.Sigmoid).then_inc(lin_freed[c], 1)

            gates(P0["mda"])
            p = P0["kv"]
            for a in range(2):
                tile(p, a)
                for g in range(2):
                    r = slice(g * HALF, (g + 1) * HALF)
                    nc.scalar.activation(S_x2[0:HALF, 2 * a + g, :], pl[a][r, :], ACT.Copy)
                    op = nc.scalar.activation(S_x2[HALF:PART, 2 * a + g, 0:T - 1], pl[a][r, 1:T], ACT.Copy)
                op.then_inc(lin_freed[a], 1)
            for j in range(4):
                act.wait_ge(cb_f, j + 1)
                nc.scalar.activation(B_h[j // 2][:, :, j % 2, :], S_bf[:, j % 2, 0:16 * NCMP].rearrange("p (j n) -> p j n", j=16), ACT.Copy).then_inc(cb_hi, 1)
            for br in range(2):
                evac(p + 1 + br, 0, S_kraw[:, br, :])
                evac(p + 1 + br, 1, S_vT[:, br, :])
            evac(p + 3, 0, S_gT[0:48, :], ACT.Sigmoid, rows=48)
            for br in range(2):
                act.wait_ge(vt_t, br + 1)
                nc.scalar.activation(S_v[:, br].rearrange("p a n -> p (a n)"), pt[br][:, :], ACT.Copy).then_inc(vt_c, 1)
            act.sem_inc(lin_freed[1], 1)
            act.wait_ge(vt_t, 3)
            nc.scalar.activation(S_gate.rearrange("p a n -> p (a n)"), ps[0][:, 0:QT * 48], ACT.Copy).then_inc(vt_c, 1)
            for a in range(2):
                act.wait_ge(lin_done, 2 * (P0["cmp"] + 2 * a + 2))
                nc.scalar.activation(S_hT[0:2 * NCMP, a, :], pl[0][0:2 * NCMP, 0:PC], ACT.Gelu_apprx_tanh).then_inc(lin_freed[0], 2)
                act.sem_inc(lin_freed[1], 2)
            act.wait_ge(vt_t, 3 + 1)
            nc.scalar.activation(S_h1.rearrange("p a c n -> p (a c n)"), ps[1][:, 0:8 * NCMP], ACT.Copy).then_inc(vt_c, 1)
            act.wait_ge(cb_o, 1)
            act.wait_ge(zero_s, 3)
            for a in range(2):
                half = slice(a * HALF, (a + 1) * HALF)
                op = nc.scalar.activation(S_kc[half, :, a * CKEY:a * CKEY + NCMP], po[0][half, 0:2 * NCMP].rearrange("p (g n) -> p g n", g=2), ACT.Copy)
            op.then_inc(cb_k, 1)
            act.wait_ge(cb_o, 2)
            for n in range(4):
                op = nc.scalar.activation(S_vc[n * CKEY:n * CKEY + NCMP, :, n, :], po[1][0:NCMP, 0:2 * HALF].rearrange("p (g n) -> p g n", g=2), ACT.Copy)
            op.then_inc(cb_k, 1)

            def ns_parts(it):
                for pr in range(2):
                    finish(it * 2 + (F0["ns"] + pr), dyn(ah, it * 2 + pr), pr)

            with act.Fori(0, 2) as g:
                for e in range(2):
                    it = g * 2 + e
                    act.wait_ge(at_s, it * NG_NS + U0["ns"])
                    act.wait_ge(at_st, it + A0["ns"])
                    for c in range(2):
                        evac(it + P0["nq"], c, S_qr[:, c, :])
                    if e:
                        ns_parts(g * 2)
                    groups(it * NG_NS + U0["ns"], [([QT * 2 * CKEY], float(HALF) ** -0.5, None)] * 2 + causal_groups(0) + causal_groups(16))
                ns_parts(g * 2 + 1)
            gates(P0["mnsa"])
            act.wait_ge(lin_done, 2 * P0["wout2"])
            for k in range(KT):
                act.wait_ge(mg_t, 2 + k + 1)
                nc.scalar.activation(ah[:, k, :], S_mg[:, k, :], ACT.Copy).then_inc(mg_hi, 1)
            ffn("ffn2", P0["wout2"])
            norm("final", after(P0["ffn2"] + 30), dst=None)
            for g in range(2 * QT):
                act.wait_ge(out_t, g + 1)
                nc.scalar.activation(O_nat[:, g // 2, (g % 2) * 512:(g % 2 + 1) * 512], pt[g % 2][:, :], ACT.Copy).then_inc(out_c, 1)

        @block.vector
        def _(dve):
            nc.vector.memset(raw[:, P0["small"] % 2], 0.0).then_inc(raw_zero, 1)
            dve.sem_inc(at_m, UINIT)
            dve.sem_inc(at_r, UINIT)
            dve.sem_inc(at_of, UINIT)
            dve.sem_inc(fin_read, FINIT)
            dve.sem_inc(ml_u, 2)
            dve.sem_inc(ml_lo, 2)
            dve.sem_inc(mg_t, 2)
            causal = c_("causal", T)

            def dyn(buf, e):
                return buf[:, bass.ds(e, 1), :].rearrange("p a n -> p (a n)")

            def tile(p, c):
                dve.wait_ge(lin_done, p * 2 + (c + 1))

            def low(dst, full, hi, done):
                nc.vector.tensor_tensor(dst, full, hi.bitcast(F32), ALU.subtract).then_inc(done, 1)

            def accumulate(name, k, n=T):
                call = NORM[name]
                dve.wait_ge(nm_sq, 8 * call + k + 1)
                if k == 1 and call:
                    dve.wait_ge(nm_rs, call)
                if k > 1:
                    dve.wait_ge(nm_ac, 7 * call + k - 1)
                nc.vector.tensor_tensor(N_acc[:, 0:n], N_sq[:, 0, 0:n] if k == 1 else N_acc[:, 0:n], N_sq[:, k % 2, 0:n], ALU.add).then_inc(nm_ac, 1)

            def norm(name, gain, src=h, n=T, dst=(xh, xl)):
                call = NORM[name]
                if name != "mem":
                    norm_root(name, n)
                dve.wait_ge(nm_rs, call + 1)
                for k in range(KT):
                    o = F_out[:, k, 0:n] if dst is None else N_xn[:, k % 2, 0:n]
                    if dst is not None and k >= 2:
                        dve.wait_ge(nm_lo, 8 * call + k - 1)
                    nc.vector.scalar_tensor_tensor(o, src[:, k, 0:n], gcol(gain, k), N_rs[:, 0:n], ALU.mult, ALU.mult).then_inc(nm_xn, 1)
                    if dst is not None and k:
                        norm_low(call, k - 1, n, dst)
                if dst is not None:
                    norm_low(call, KT - 1, n, dst)

            def norm_root(name, n):
                dve.wait_ge(nm_std, NORM[name] + 1)
                if NORM[name]:
                    dve.wait_ge(nm_lo, 8 * NORM[name])
                nc.vector.reciprocal(N_rs[:, 0:n], N_std[:, 0:n]).then_inc(nm_rs, 1)

            def norm_low(call, k, n, dst):
                dve.wait_ge(nm_hi, 8 * call + k + 1)
                low(dst[1][:, k, 0:n], N_xn[:, k % 2, 0:n], dst[0][:, k, 0:n], nm_lo)

            def residual(p0, name, scale=1.0):
                for k in range(KT):
                    add(p0 + k // 2, k % 2, h[:, k, :], scale)
                    if name and k >= 2:
                        accumulate(name, k - 1)
                if name:
                    accumulate(name, KT - 1)

            def add(p, c, hk, scale):
                tile(p, c)
                if scale == 1.0:
                    nc.vector.tensor_tensor(hk, pl[c][:, :], hk, ALU.add).then_inc(lin_freed[c], 1)
                else:
                    nc.vector.scalar_tensor_tensor(hk, pl[c][:, :], scale, hk, ALU.mult, ALU.add).then_inc(lin_freed[c], 1)

            def groups(U, gs, out, coefs=None):
                n = len(gs)
                for s in range(n + 3):
                    if s < n:
                        dve.wait_ge(at_s, U + (s + 1))
                    if s - 2 < n:
                        dve.wait_ge(at_p, U + (s - 1))
                        dve.sem_inc(go_dve, 1)
                    j = s - 2
                    if 0 <= j < n and "cmp" in gs[j]:
                        nc.vector.tensor_reduce(rsum[:, gs[j]["at"][0]:gs[j]["at"][1]], PB[:, j % 2, 0:gs[j]["w"]].rearrange("p (u k) -> p u k", k=CKEY),
                                                AX.X, ALU.add).then_inc(cs_s, 1)
                    if s < n:
                        gs[s]["scores"](s)
                    if s >= 3 and coefs:
                        dve.wait_ge(at_r, U + (s - 2))
                        dve.sem_inc(go_dve, 1)
                        coefs(s - 3)
                    if 0 <= j < n:
                        if "cmp" in gs[j]:
                            dve.wait_ge(cs_s, gs[j]["cmp"] + 1)
                            dve.sem_inc(go_dve, 1)
                        lo, hi = gs[j]["at"]
                        nc.vector.reciprocal(rinv[:, lo:hi], rsum[:, lo:hi]).then_inc(at_r, 1)
                    if s >= 3:
                        dve.wait_ge(at_o, U + (s - 2))
                        if not coefs:
                            dve.wait_ge(at_r, U + (s - 2))
                        dve.sem_inc(go_dve, 1)
                        out(s - 3)

            def score_tiles(tiles_):
                def run(s):
                    for col, nk, mask, scale, at in tiles_:
                        op = nc.vector.tensor_tensor_reduce(out=SM[:, s % 2, col:col + nk], in0=ps[s % 2][:, col:col + nk], in1=mask, scale=scale,
                                                            scalar=BIG, op0=ALU.add, op1=ALU.min, accum_out=negm[:, at:at + 1])
                    op.then_inc(at_m, 1)
                return run

            def causal_groups(at=0):
                gs = []
                for g in CAUSAL_GROUPS:
                    gs.append(dict(scores=score_tiles([(col, (t + 1) * PART, causal[:, T - (t + 1) * PART:], -float(HALF) ** -0.5, at + m)
                                                       for m, (_, _, t, col) in enumerate(g)]), at=(at, at + len(g))))
                    at += len(g)
                return gs

            def finish(F, dst_h, dst_l, at=0):
                dve.wait_ge(fin_hi, F + 1)
                low(dst_l, pt[at % 2][:, :], dst_h, fin_read)

            for k in range(1, KT):
                accumulate("mix", k)
            norm("mix", "norm_mix_g")

            dve.wait_ge(ld_late, 16 * 3)
            for a in range(2):
                nc.vector.tensor_tensor_reduce(out=lp_in[0:1, 2 * a, :], in0=lp_in[0:1, 2 * a, :], in1=lp_in[0:1, 2 * a + 1, :], scale=1.0,
                                               scalar=0.0, op0=ALU.mult, op1=ALU.add, accum_out=lam[0:1, a:a + 1]).then_inc(lam_s, 1)
            dve.wait_ge(lam_s, 3)
            nc.vector.tensor_tensor(lam[0:1, 2:3], lam[0:1, 0:1], lam[0:1, 1:2], ALU.subtract).then_inc(lam_s, 1)
            dve.wait_ge(lam_s, 4)
            nc.vector.tensor_scalar(lam[0:1, 2:3], lam[0:1, 2:3], -1.0, -LAM_INIT, ALU.mult, ALU.add).then_inc(lam_s, 1)
            for x in (X_q, X_k):
                op = nc.vector.memset(x[HALF:PART], 0.0)
            op.then_inc(kd, 1)
            dve.wait_ge(gl_hi, 1)
            low(G_lr[1], pl[1][0:16, :], G_lr[0], lin_freed[1])
            dve.wait_ge(ls_a, 3)
            nc.vector.scalar_tensor_tensor(X_z[0:8, :], X_z[0:8, :], 0.0, X_e[0:8, :], ALU.min, ALU.subtract).then_inc(ls_v, 1)
            dve.wait_ge(ls_v, 1)
            nc.vector.tensor_tensor_scan(X_c[0:8, :], c_("ones", T, 8), X_z[0:8, :], 0.0, ALU.mult, ALU.add).then_inc(ls_v, 1)
            dve.wait_ge(ls_v, 2)
            dve.wait_ge(kd, 1)
            for a in range(4):
                op = nc.vector.tensor_copy(X_k[HALF:HALF + 8, a, :], X_c[0:8, :])
            op.then_inc(ls_v, 2)
            dve.wait_ge(ls_v, 4)
            for j in range(8):
                dve.wait_ge(hn_std, j + 1)
                if j >= 2:
                    dve.wait_ge(hn_out, j - 1)
                nc.vector.reciprocal(H_rs[:, j % 2, :], H_std[:, j % 2, :]).then_inc(hn_rs, 1)
                dve.wait_ge(hn_rs, j + 1)
                nc.vector.scalar_tensor_tensor(X_qk[:, j, :], X_qk[:, j, :], gcol("fox_q_norm_g" if j < 4 else "fox_k_norm_g", 0), H_rs[:, j % 2, :],
                                               ALU.mult, ALU.mult).then_inc(hn_out, 1)
            dve.wait_ge(lam_p, 1)
            nc.vector.tensor_copy(lam[:, 3:4], ps[0][:, 0:1]).then_inc(lam_d, 1)
            dve.wait_ge(hn_out, 8)
            with dve.Fori(0, 2) as i:
                dve.wait_ge(at_s, i * NG + U0["fox"])
                dve.sem_inc(go_dve, 1)
                for n in range(4):
                    a = n % 2
                    src = X_qk[a * HALF:(a + 1) * HALF, bass.ds(i * 2 + n // 2, 1), :].rearrange("p a n -> p (a n)")
                    nc.vector.tensor_copy(X_q[0:HALF, n, :], src)
                    rows = slice(HALF, HALF + 8)
                    pick = cst[rows, bass.ds(i * 4 + (CAT["sel"] + n), 1)]
                    op = nc.vector.tensor_scalar(X_q[rows, n, :], cst[rows, CAT["ones"]:CAT["ones"] + T], pick, None, ALU.mult)
                op.then_inc(at_st, 1)
                gs = causal_groups()

                def out_fox(j):
                    for m, (pr, a, t, _) in enumerate(CAUSAL_GROUPS[j]):
                        at = gs[j]["at"][0] + m
                        op = nc.vector.tensor_scalar(X_on[:, pr, t, a * HALF:(a + 1) * HALF], po[j % 2][:, m * HALF:(m + 1) * HALF], rinv[:, at:at + 1], None, ALU.mult)
                    op.then_inc(at_of, 1)

                groups(i * NG + U0["fox"], gs, out_fox)
                for pr in range(2):
                    finish(i * 2 + (F0["fox"] + pr), dyn(ah, i * 2 + pr), dyn(al, i * 2 + pr), pr)

            nc.vector.memset(G_S, 0.0).then_inc(gl_s, 1)
            dve.wait_ge(ls_a, 8)
            nc.vector.scalar_tensor_tensor(G_z, G_z, 0.0, G_e, ALU.min, ALU.subtract).then_inc(ls_v, 1)
            dve.wait_ge(ls_v, 5)
            for a in range(2):
                nc.vector.tensor_tensor_scan(G_b[:, a, :], c_("chunk", T), G_z[:, a, :], 0.0, ALU.mult, ALU.add).then_inc(ls_v, 1)
            dve.wait_ge(ls_v, 7)
            chunks = G_b.rearrange("p a (n c) -> p (a n) c", c=HALF)
            nc.vector.tensor_tensor(G_z.rearrange("p a (n c) -> p (a n) c", c=HALF), chunks[:, :, HALF - 1:HALF].to_broadcast([PART, 2 * T // HALF, HALF]),
                                    chunks, ALU.subtract).then_inc(ls_v, 1)
            for c in range(2):
                dve.wait_ge(lin_freed[c], P0["gqk"] + 1)
            dve.wait_ge(ls_a, 9)
            nc.vector.scalar_tensor_tensor(G_qk[:, 0:2, :], G_qk[:, 0:2, :], float(HALF) ** -0.5, G_e, ALU.mult, ALU.mult).then_inc(ls_v, 1)
            for c in range(2):
                dve.wait_ge(lin_freed[c], P0["gqk"] + 2)
            dve.wait_ge(ls_a, 11)
            nc.vector.tensor_tensor(G_ke, G_ke, G_qk[:, 2:4, :], ALU.mult).then_inc(ls_v, 1)
            dve.wait_ge(ls_a, 12)
            dve.wait_ge(ls_v, 10)
            nc.vector.tensor_tensor(G_qk[:, 2:4, :], G_qk[:, 2:4, :], G_e, ALU.mult).then_inc(ls_v, 1)
            dve.wait_ge(ls_v, 11)
            for c in range(2):
                dve.wait_ge(lin_freed[c], P0["wout"])
            with dve.Fori(0, QT) as i:
                dve.wait_ge(gl_i, i * 2 + 2)
                dve.sem_inc(go_dve, 1)
                tok = bass.ds(i * PART, PART)
                nc.vector.tensor_copy(G_qs, G_qk[:, 0:2, tok])
                nc.vector.tensor_copy(G_ks, G_qk[:, 2:4, tok])
                nc.vector.tensor_copy(G_es, G_ke[:, :, tok]).then_inc(gl_st, 1)
                dve.wait_ge(gl_kt, i + 1)
                dve.sem_inc(go_dve, 1)
                nc.vector.tensor_copy(G_kn.rearrange("p a n -> p (a n)"), pt[0][:, 0:2 * PART]).then_inc(gl_kn, 1)
                dve.wait_ge(gl_a, i + 1)
                dve.sem_inc(go_dve, 1)
                for b in range(2):
                    op = nc.vector.tensor_tensor(G_at[:, b], ps[b][:, 0:2 * HALF].rearrange("p (a n) -> p a n", a=2),
                                                 c_("tril", HALF).unsqueeze(1).to_broadcast([PART, 2, HALF]), ALU.mult)
                op.then_inc(gl_at, 1)
                for c in range(2):
                    dve.wait_ge(gl_i, i * 2 + (3 + c))
                    dve.wait_ge(gl_s, i * 2 + (c + 1))
                    dve.sem_inc(go_dve, 1)
                    for a in range(2):
                        dec = G_dec[:, a, bass.ds(i * 2 + c, 1)]
                        op = nc.vector.scalar_tensor_tensor(G_S[:, a, :], G_S[:, a, :], dec, ps[c][:, 256 + a * PART:256 + (a + 1) * PART], ALU.mult, ALU.add)
                    op.then_inc(gl_s, 1)
                dve.wait_ge(gl_on, i + 1)
                dve.sem_inc(go_dve, 1)
                for b in range(2):
                    o = dyn(G_O, i).rearrange("p (a b n) -> p b a n", b=2, n=PART)[:, b]
                    op = nc.vector.tensor_tensor(o, po[b][:, 0:2 * PART].rearrange("p (a n) -> p a n", a=2), o, ALU.add)
                op.then_inc(gl_oi, 1)
            dve.wait_ge(fin_std, 1)
            nc.vector.reciprocal(hinv[:], hstd[:]).then_inc(fin_n, 1)
            dve.wait_ge(fin_n, 1)
            on = G_O.rearrange("p t (a n) -> p (t a) n", n=PART)
            nc.vector.tensor_tensor(on, on, hinv[:].unsqueeze(2).to_broadcast([PART, 4 * QT, PART]), ALU.mult).then_inc(fin_rs, 1)
            for hd in range(4):
                dve.wait_ge(fin_t, F0["gla"] + hd + 1)
                nc.vector.scalar_tensor_tensor(G_r[:, hd, :], pt[hd % 2][:, :], gcol("gla_out_norm_g", hd), G_r[:, hd, :], ALU.mult, ALU.mult).then_inc(fin_g, 1)
                dve.wait_ge(fin_hi, F0["gla"] + hd + 1)
                low(al[:, 4 + hd, :], G_r[:, hd, :], ah[:, 4 + hd, :], fin_read)

            for k in range(1, KT):
                accumulate("mem", k, M)
            norm_root("mem", M)
            residual(P0["wout"], "xattn")
            norm("mem", "norm_mem_g", memT, M, (ah, al))
            norm("xattn", "norm_xattn_g")
            for j in range(8, 16):
                n, buf, g = (M, C_K, "xattn_k_norm_g") if j < 12 else (T, C_Q, "xattn_q_norm_g")
                dve.wait_ge(hn_std, j + 1)
                dve.wait_ge(hn_out, j - 1)
                nc.vector.reciprocal(C_rs[:, j % 2, 0:n], C_std[:, j % 2, 0:n]).then_inc(hn_rs, 1)
                dve.wait_ge(hn_rs, j + 1)
                for c in range(2):
                    k = 2 * (j % 4) + c
                    op = nc.vector.scalar_tensor_tensor(buf[:, k, :], buf[:, k, :], gcol(g, c), C_rs[:, j % 2, 0:n], ALU.mult, ALU.mult)
                op.then_inc(hn_out, 1)
            dve.wait_ge(hn_out, 16)
            with dve.Fori(0, 2) as i:
                dve.wait_ge(at_s, i * NG_XA + U0["xa"])
                dve.sem_inc(go_dve, 1)
                nc.vector.tensor_copy(C_q, C_Q[:, bass.ds(i * 4, 4), :]).then_inc(at_st, 1)
                gs = [dict(scores=score_tiles([(m * M, M, causal[:, 0:M], -float(M) ** -0.5, 2 * n + m) for m in range(2)]), at=(2 * n, 2 * n + 2))
                      for n in range(NG_XA)]

                def out_xa(j):
                    for m in range(2):
                        op = nc.vector.tensor_scalar(C_on[:, j // 2, 2 * (j % 2) + m, :], po[j % 2][:, m * M:(m + 1) * M], rinv[:, 2 * j + m:2 * j + m + 1], None, ALU.mult)
                    op.then_inc(at_of, 1)

                groups(i * NG_XA + U0["xa"], gs, out_xa)
                for f in range(4):
                    finish(i * 4 + (F0["xa"] + f), dyn(ah, i * 4 + f), dyn(al, i * 4 + f), f)
            residual(P0["xo"], "mlp")

            norm("mlp", "norm_mlp_g")

            def mlp(r):
                for j in range(4):
                    for c in range(2):
                        k = 2 * j + c
                        m = r * 8 + (MLP0["mlp"] + k)
                        dve.wait_ge(lin_freed[c], r * 8 + (P0["mlp"] + j + 1))
                        dve.wait_ge(ml_lo, m - 1)
                        dve.sem_inc(go_dve, 1)
                        nc.vector.tensor_tensor(E_u[:, c, :], E_t[:, c, :], E_t[:, c, :], ALU.mult).then_inc(ml_u, 1)
                        dve.wait_ge(ml_hi, m + 1)
                        low(al[:, k, :], E_u[:, c, :], ah[:, k, :], ml_lo)

            with dve.Fori(0, D_FF // D - 1) as r:
                mlp(r)
                residual(r * 8 + (P0["mlp"] + 4), None)
            mlp(D_FF // D - 1)
            residual(P0["mlp"] + 8 * (D_FF // D - 1) + 4, "ffn1")

            def gated(p, m, j):
                for c in range(2):
                    dve.wait_ge(lin_freed[c], p + 1)
                    dve.wait_ge(ml_lo, m)
                    tile(p + 1, c)
                    dve.sem_inc(go_dve, 1)
                    nc.vector.tensor_tensor(E_u[:, c, :], pl[c][:, :], E_t[:, c, :], ALU.mult).then_inc(lin_freed[c], 1)
                for c in range(2):
                    dve.wait_ge(ml_hi, m + (c + 1))
                    low(al[:, 2 * j + c, :], E_u[:, c, :], ah[:, 2 * j + c, :], ml_lo)

            def ffn(name, gain, after):
                norm(name, gain)
                p0, m0 = P0[name], MLP0[name]
                with dve.Fori(0, 2) as r:
                    for j in range(4):
                        gated(r * 12 + (p0 + 2 * j), r * 8 + (m0 + 2 * j), j)
                    residual(r * 12 + (p0 + 8), None, 0.5)
                for j in range(3):
                    gated(p0 + 24 + 2 * j, m0 + 16 + 2 * j, j)
                residual(p0 + 30, after, 0.5)

            ffn("ffn1", "ffn1_norm_2", "mix2")
            norm("mix2", "mix_norm_2")
            cos, sin = c_("cos", T), c_("sin", T)
            nc.vector.memset(D_q, 0.0).then_inc(zero_s, 1)

            def da_parts(it):
                for pr in range(2):
                    dve.wait_ge(fin_t, it * 2 + (F0["da"] + pr + 1))
                    dve.sem_inc(go_dve, 1)
                    gain = gT[:, bass.ds(it * 2 + (ROWS["da_head_norm_2"] + pr), 1)]
                    nc.vector.tensor_scalar(D_g[:, pr, :], pt[pr][:, :], gain, 1.0 - LAM_INIT, ALU.mult, ALU.mult).then_inc(fin_g, 1)
                for pr in range(2):
                    dve.wait_ge(fin_hi, it * 2 + (F0["da"] + pr + 1))
                    low(dyn(al, it * 2 + pr), D_g[:, pr, :], dyn(ah, it * 2 + pr), fin_read)

            def da_rope(it, which, src, rot, add):
                for c in range(2):
                    dve.wait_ge(rp_t, it * 4 + (R0["da"] + 2 * which + c + 1))
                    dve.sem_inc(go_dve, 1)
                    nc.vector.tensor_tensor(src[:, c, :], src[:, c, :], cos, ALU.mult)
                    nc.vector.tensor_tensor(D_t[:, c, :], rot[c][:, :], sin, ALU.mult).then_inc(rp_a, 1)
                for c in range(2):
                    dve.wait_ge(rp_a, it * 4 + (RA0["da"] + 2 * which + c + 1))
                    dve.sem_inc(go_dve, 1)
                    op = add(c)
                return op

            dve.wait_ge(zero_s, 1)
            with dve.Fori(0, 2) as r:
                for e in range(2):
                    it = r * 2 + e
                    if e:
                        da_parts(r * 2)

                    def add_q(c):
                        for a in range(2):
                            half = slice(a * HALF, (a + 1) * HALF)
                            op = nc.vector.tensor_tensor(D_q[half, 2 * c + a, :], D_raw[half, c, :], D_t[half, c, :], ALU.add)
                        return op

                    da_rope(it, 0, D_raw[:, 0:2], ps, add_q).then_inc(rp_b, 1)
                    dve.wait_ge(rp_b, it + 1)
                    da_rope(it, 1, D_raw[:, 2:4], po,
                            lambda c: nc.vector.tensor_tensor(D_k[:, c, :], D_raw[:, 2 + c, :], D_t[:, c, :], ALU.add)).then_inc(at_st, 1)
                    U = it * NG + U0["da"]
                    gs = causal_groups()

                    def coef_da(j):
                        if CAUSAL_GROUPS[j][0][1]:
                            lo, hi = gs[j]["at"]
                            nc.vector.tensor_scalar(coef[:, lo:hi], rinv[:, lo:hi], lam[:, 3:4], None, ALU.mult).then_inc(at_cf, 1)

                    def out_da(j):
                        a = CAUSAL_GROUPS[j][0][1]
                        if a:
                            dve.wait_ge(at_of, U + j)
                            dve.wait_ge(at_cf, it * (NG // 2) + (CF0["da"] + j // 2 + 1))
                            dve.sem_inc(go_dve, 1)
                        for m, (pr, _, t, _) in enumerate(CAUSAL_GROUPS[j]):
                            at = gs[j]["at"][0] + m
                            o, v = D_on[:, pr, t, :], po[j % 2][:, m * PART:(m + 1) * PART]
                            if a == 0:
                                op = nc.vector.tensor_scalar(o, v, rinv[:, at:at + 1], None, ALU.mult)
                            else:
                                op = nc.vector.scalar_tensor_tensor(o, v, coef[:, at:at + 1], o, ALU.mult, ALU.add)
                        op.then_inc(at_of, 1)

                    groups(U, gs, out_da, coef_da)
                    dve.wait_ge(fin_std, it + (1 + 1))
                    dve.sem_inc(go_dve, 1)
                    nc.vector.reciprocal(hinv[:, 0:8], hstd[:, 0:8]).then_inc(fin_n, 1)
                    dve.wait_ge(fin_n, it + (1 + 1))
                    on = D_on.rearrange("p a t n -> p (a t) n")
                    nc.vector.tensor_tensor(on, on, hinv[:, 0:8].unsqueeze(2).to_broadcast([PART, 2 * QT, PART]), ALU.mult).then_inc(fin_rs, 1)
                da_parts(r * 2 + 1)

            def merge(p0, adds):
                with dve.Fori(0, 4) as i:
                    for c in range(2):
                        p = i * 2 + (p0 + 1)
                        dve.wait_ge(lin_freed[c], p)
                        tile(p, c)
                        mg = dyn(S_mg, i * 2 + c)
                        if adds:
                            dve.wait_ge(mg_t, i * 2 + (c + 1))
                        dve.sem_inc(go_dve, 1)
                        nc.vector.tensor_tensor(SM[:, c, :] if adds else mg, pl[c][:, :], S_sg[:, c, :], ALU.mult).then_inc(lin_freed[c], 1)
                        if adds:
                            dve.wait_ge(lin_freed[c], p + 1)
                            nc.vector.tensor_tensor(mg, mg, SM[:, c, :], ALU.add).then_inc(mg_t, 1)

            merge(P0["mda"], False)

            for a in range(2):
                dve.wait_ge(lin_freed[a], P0["kv"] + 1)
                for g in range(2):
                    j = 2 * a + g
                    if j >= 2:
                        dve.wait_ge(cb_lo, j - 1)
                    src = bass.AP(S_x2.tensor, S_x2.offset + j * T, [list(S_x2.ap[0]), [2, 16], [CMP_S, NCMP]])
                    pos = gT[:, ROWS["cmp_pos_2"] + a * 16:ROWS["cmp_pos_2"] + (a + 1) * 16].unsqueeze(2).to_broadcast([PART, 16, NCMP])
                    bf = S_bf[:, g, 0:16 * NCMP].rearrange("p (j n) -> p j n", j=16)
                    nc.vector.tensor_tensor(bf, src, pos, ALU.add).then_inc(cb_f, 1)
                    dve.wait_ge(cb_hi, j + 1)
                    low(B_l[a][:, :, g, :], bf, B_h[a][:, :, g, :], cb_lo)
            p = P0["kv"]
            parts = (S_qr[:, 0, :], S_qr[:, 1, :])
            for br in range(2):
                dve.wait_ge(lin_freed[0], p + 2 + br)
                nc.vector.tensor_tensor(S_kr[:, br, :], S_kraw[:, br, :], cos, ALU.mult)
                dve.wait_ge(rp_t, R0["kv"] + br + 1)
                op = nc.vector.tensor_tensor(parts[br], po[br][:, :], sin, ALU.mult)
            op.then_inc(rp_a, 1)
            dve.wait_ge(rp_a, RA0["kv"] + 1)
            for br in range(2):
                op = nc.vector.tensor_tensor(S_kr[:, br, :], S_kr[:, br, :], parts[br], ALU.add)
            op.then_inc(rp_b, 1)
            dve.wait_ge(rp_b, 4 + 1)
            for br in range(2):
                for g in range(2):
                    for a in range(2):
                        op = nc.vector.tensor_copy(S_kd[a * HALF:(a + 1) * HALF, br, g, :], S_kr[g * HALF:(g + 1) * HALF, br, :])
            op.then_inc(kd, 1)
            dve.wait_ge(vt_c, 3)
            nc.vector.tensor_scalar(S_gate[:, 0, 0:48:3], S_gate[:, 0, 0:48:3], c_("cmpany", 1), None, ALU.mult)
            nc.vector.memset(S_kc, 0.0)
            nc.vector.memset(S_vc, 0.0).then_inc(zero_s, 2)
            dve.wait_ge(zero_s, 3)
            dve.wait_ge(cb_lo, 4)
            nc.vector.memset(S_q, 0.0).then_inc(zero_s, 1)
            dve.wait_ge(zero_s, 4)
            dve.wait_ge(cb_k, 2)
            cmpm = c_("cmpmask", QT * 2 * CKEY)

            def ns_parts(it):
                for pr in range(2):
                    finish(it * 2 + (F0["ns"] + pr), dyn(ah, it * 2 + pr), dyn(al, it * 2 + pr), pr)

            with dve.Fori(0, 2) as g:
                for e in range(2):
                    it = g * 2 + e
                    if e:
                        ns_parts(g * 2)
                    U = it * NG_NS + U0["ns"]
                    for c in range(2):
                        dve.wait_ge(rp_t, it * 2 + (R0["ns"] + c + 1))
                        dve.sem_inc(go_dve, 1)
                        nc.vector.tensor_tensor(PTs[:, c, :], S_qr[:, c, :], cos, ALU.mult)
                        nc.vector.tensor_tensor(SM[:, c, :], po[c][:, :], sin, ALU.mult).then_inc(rp_a, 1)
                    for c in range(2):
                        dve.wait_ge(rp_a, it * 2 + (RA0["ns"] + c + 1))
                        dve.sem_inc(go_dve, 1)
                        for a in range(2):
                            half = slice(a * HALF, (a + 1) * HALF)
                            nc.vector.tensor_tensor(S_q[half, 2 * c + a, :], PTs[half, c, :], SM[half, c, :], ALU.add)
                    nc.vector.tensor_copy(S_gs, S_gate[:, :, bass.ds(g * 24 + 12 * e, 12)]).then_inc(at_st, 1)
                    dve.wait_ge(at_st, it + (A0["ns"] + 1))
                    dve.sem_inc(go_dve, 1)

                    def cmp_scores(s):
                        w, n = QT * 2 * CKEY, it * 2 + s
                        sm = SM[:, s % 2, 0:w]
                        tiles_ = sm.rearrange("p (u k) -> p u k", k=CKEY)
                        top = negm[:, 32 + 8 * s:40 + 8 * s]
                        nc.vector.tensor_tensor(sm, ps[s % 2][:, 0:w], cmpm, ALU.add).then_inc(cs_a, 1)
                        dve.wait_ge(cs_a, n + 1)
                        dve.sem_inc(go_dve, 1)
                        nc.vector.tensor_reduce(top, tiles_, AX.X, ALU.max).then_inc(cs_m, 1)
                        dve.wait_ge(cs_m, n + 1)
                        dve.sem_inc(go_dve, 1)
                        nc.vector.tensor_tensor(tiles_, tiles_, top.unsqueeze(2).to_broadcast([PART, 2 * QT, CKEY]), ALU.subtract).then_inc(at_m, 1)

                    gs = [dict(scores=cmp_scores, cmp=it * 2 + pr, at=(32 + 8 * pr, 40 + 8 * pr), w=QT * 2 * CKEY) for pr in range(2)]
                    gs += causal_groups(0) + causal_groups(16)

                    def coef_ns(j):
                        lo, hi = gs[j]["at"]
                        if j < 2:
                            gate = S_gs[:, :, 6 * j:6 * j + 6:3]
                            op = nc.vector.tensor_tensor(coef[:, lo:hi].rearrange("p (t a) -> p t a", a=2), rinv[:, lo:hi].rearrange("p (t a) -> p t a", a=2), gate, ALU.mult)
                        else:
                            br = 1 + (j - 2) // NG
                            for m, (pr, a, t, _) in enumerate(CAUSAL_GROUPS[(j - 2) % NG]):
                                col = 6 * pr + 3 * a + br
                                op = nc.vector.tensor_tensor(coef[:, lo + m:lo + m + 1], rinv[:, lo + m:lo + m + 1], S_gs[:, t, col:col + 1], ALU.mult)
                        op.then_inc(at_cf, 1)

                    def out_ns(j):
                        lo, hi = gs[j]["at"]
                        dve.wait_ge(at_cf, it * NG_NS + (CF0["ns"] + j + 1))
                        if j < 2:
                            dve.sem_inc(go_dve, 1)
                            op = nc.vector.tensor_tensor(S_on[:, j].rearrange("p t (a d) -> p (t a) d", d=HALF), po[j % 2][:, :].rearrange("p (u d) -> p u d", d=HALF),
                                                         coef[:, lo:hi].unsqueeze(2).to_broadcast([PART, 2 * QT, HALF]), ALU.mult)
                        else:
                            dve.wait_ge(at_of, U + j)
                            dve.sem_inc(go_dve, 1)
                            for m, (pr, a, t, _) in enumerate(CAUSAL_GROUPS[(j - 2) % NG]):
                                o = S_on[:, pr, t, a * HALF:(a + 1) * HALF]
                                op = nc.vector.scalar_tensor_tensor(o, po[j % 2][:, m * HALF:(m + 1) * HALF], coef[:, lo + m:lo + m + 1], o, ALU.mult, ALU.add)
                        op.then_inc(at_of, 1)

                    groups(U, gs, out_ns, coef_ns)
                ns_parts(g * 2 + 1)
            merge(P0["mnsa"], True)
            for k in range(KT):
                dve.wait_ge(mg_hi, k + 1)
                low(al[:, k, :], S_mg[:, k, :], ah[:, k, :], mg_lo)
            residual(P0["wout2"], "ffn2")
            ffn("ffn2", "ffn2_norm_2", "final")
            norm("final", "final_norm_2", dst=None)
    return nc


_INS = ["x", "mem", "norm_mix_g", "w_in", "fox_b_f", "fox_q_norm_g", "fox_k_norm_g", "gla_w_gate2", "gla_b_gate", "gla_out_norm_g", "w_out",
        "norm_xattn_g", "norm_mem_g", "xattn_wq", "xattn_wkv", "xattn_q_norm_g", "xattn_k_norm_g", "xattn_wo", "norm_mlp_g", "mlp_w1", "mlp_w2",
        "ffn1_norm_2", "ffn1_w1_2", "ffn1_w3_2", "ffn1_w2_2", "mix_norm_2", "w_in_2", "da_lambda_2", "da_head_norm_2", "cmp_pos_2", "cmp_w1_2",
        "cmp_w2_2", "w_proj_da_2", "w_proj_nsa_2", "w_out_2", "ffn2_norm_2", "ffn2_w1_2", "ffn2_w3_2", "ffn2_w2_2", "final_norm_2"]


def kernel(**inputs):
    import concourse.bacc as _bacc
    from concourse.bass_utils import run_bass_kernel_spmd as _run

    nc = _bacc.Bacc("TRN2", target_bir_lowering=False, num_devices=1)
    arrays, d = {}, {}
    for name in _INS + ["consts"]:
        a = CONSTS if name == "consts" else np.ascontiguousarray(inputs[name])
        arrays[f"in_{name}_dram"] = a
        d[name] = nc.dram_tensor(f"in_{name}_dram", a.shape, mybir.dt.from_np(a.dtype), kind="ExternalInput").ap()
    out = nc.dram_tensor("out_0_dram", (1, T, D), F32, kind="ExternalOutput").ap()
    build(nc, d, out)
    r = _run(nc, [arrays], core_ids=[0])
    return r.results[0]["out_0_dram"]
```
